# Optimizing a Trainium2 kernel written in Bass

```python
import jax, jax.numpy as jnp
from jax import lax
import numpy as np
import math

D_MODEL = 1024
BATCH = 1
SEQ = 256
DEPTH = 2

N_META = 16
BLOCK = 128
N_PAD = BLOCK - N_META
FOX_HEADS = 8
FOX_HEAD_DIM = D_MODEL // 16
FOX_WIDTH = FOX_HEADS * FOX_HEAD_DIM
GLA_HEADS = 4
GLA_WIDTH = D_MODEL // 2
GLA_DV = GLA_WIDTH // GLA_HEADS
GLA_DK = GLA_DV // 2
GLA_KWIDTH = GLA_HEADS * GLA_DK
GLA_GATE_RANK = 16
GLA_GATE_TEMP = 16.0
D_FF = ((8 * D_MODEL // 3 + 127) // 128) * 128
RMS_EPS = 1e-6
SPLIT_SIZES = (FOX_WIDTH, FOX_WIDTH, FOX_WIDTH, FOX_HEADS, GLA_KWIDTH, GLA_KWIDTH, GLA_WIDTH, GLA_GATE_RANK, GLA_WIDTH, D_MODEL, D_MODEL)
N_IN = 3 * FOX_WIDTH + FOX_HEADS + 2 * GLA_KWIDTH + 2 * GLA_WIDTH + GLA_GATE_RANK + 2 * D_MODEL


def rmsnorm(x, gain):
    xf = x.astype(jnp.float32)
    y = xf * lax.rsqrt(jnp.mean(xf * xf, axis=-1, keepdims=True) + RMS_EPS)
    return (y * gain.astype(jnp.float32)).astype(x.dtype)

def swiglu(h, w_gu, w_down):
    gate, up = jnp.split(h @ w_gu, 2, axis=-1)
    return (jax.nn.silu(gate) * up) @ w_down

def to_heads(t, n_heads):
    b, l, _ = t.shape
    return t.reshape(b, l, n_heads, -1).transpose(0, 2, 1, 3)

def from_heads(t):
    b, h, l, d = t.shape
    return t.transpose(0, 2, 1, 3).reshape(b, l, h * d)

def fox_attention(q, k, v, log_f, key_valid):
    lp = q.shape[2]
    cum = jnp.cumsum(log_f, axis=-1)
    scale = FOX_HEAD_DIM ** -0.5
    outs = []
    for start in range(0, lp, BLOCK):
        end = start + BLOCK
        s = jnp.einsum('bhqd,bhkd->bhqk', q[:, :, start:end], k[:, :, :end]).astype(jnp.float32) * scale
        s = s + cum[:, :, start:end, None] - cum[:, :, None, :end]
        qpos = jnp.arange(start, end)[:, None]
        kpos = jnp.arange(end)[None, :]
        allowed = (kpos <= qpos) & (key_valid[None, :end] | (kpos == qpos))
        p = jax.nn.softmax(jnp.where(allowed, s, -jnp.inf), axis=-1)
        outs.append(jnp.einsum('bhqk,bhkd->bhqd', p.astype(v.dtype), v[:, :, :end]))
    return jnp.concatenate(outs, axis=2)

def gla_chunked(q, k, v, log_a):
    b, h, lp, dk = q.shape
    dv = v.shape[-1]
    n = lp // BLOCK

    def to_chunks(t):
        return jnp.moveaxis(t.reshape(b, h, n, BLOCK, t.shape[-1]), 2, 0)

    causal = jnp.tril(jnp.ones((BLOCK, BLOCK), dtype=bool))[:, :, None]

    def step(state, inp):
        qi, ki, vi, ai = inp
        cb = jnp.cumsum(ai, axis=2)
        qf, kf, vf = qi.astype(jnp.float32), ki.astype(jnp.float32), vi.astype(jnp.float32)
        inter = jnp.einsum('bhtk,bhkv->bhtv', qf * jnp.exp(cb), state)
        diff = cb[:, :, :, None, :] - cb[:, :, None, :, :]
        decay = jnp.exp(jnp.where(causal, diff, -jnp.inf))
        att = jnp.einsum('bhtk,bhsk,bhtsk->bhts', qf, kf, decay)
        intra = jnp.einsum('bhts,bhsv->bhtv', att, vf)
        last = cb[:, :, -1:, :]
        new_state = jnp.exp(last[:, :, 0, :, None]) * state + jnp.einsum('bhsk,bhsv->bhkv', kf * jnp.exp(last - cb), vf)
        return new_state, (inter + intra).astype(vi.dtype)

    s0 = jnp.zeros((b, h, dk, dv), jnp.float32)
    _, o = lax.scan(step, s0, (to_chunks(q), to_chunks(k), to_chunks(v), to_chunks(log_a)))
    return jnp.moveaxis(o, 0, 2).reshape(b, h, lp, dv)

def token_mixer(h, key_valid, w_in, w_alpha_up, b_alpha, b_f, g_gla_out, w_fox_o, w_gla_o, w_out):
    valid = key_valid.astype(jnp.float32)[None, :, None]
    points = np.cumsum(SPLIT_SIZES)[:-1].tolist()
    fq, fk, fv, ff, gq, gk, gv, ga, gr, g_merge_a, g_merge_b = jnp.split(h @ w_in, points, axis=-1)
    log_f = jax.nn.log_sigmoid(ff.astype(jnp.float32) + b_f.astype(jnp.float32)) * valid
    o_fox = fox_attention(to_heads(fq, FOX_HEADS), to_heads(fk, FOX_HEADS), to_heads(fv, FOX_HEADS),
                          log_f.transpose(0, 2, 1), key_valid)
    log_a = jax.nn.log_sigmoid((ga @ w_alpha_up).astype(jnp.float32) + b_alpha.astype(jnp.float32)) * (valid / GLA_GATE_TEMP)
    gk = gk * valid.astype(gk.dtype)
    o_gla = gla_chunked(to_heads(gq * (GLA_DK ** -0.5), GLA_HEADS), to_heads(gk, GLA_HEADS),
                        to_heads(gv, GLA_HEADS), to_heads(log_a, GLA_HEADS))
    o_gla = rmsnorm(o_gla, g_gla_out.reshape(GLA_HEADS, 1, GLA_DV))
    o_gla = from_heads(o_gla) * jax.nn.silu(gr)
    y = jax.nn.sigmoid(g_merge_a) * (from_heads(o_fox) @ w_fox_o) + jax.nn.sigmoid(g_merge_b) * (o_gla @ w_gla_o)
    return y @ w_out

def first_inputs(seed: int = 0) -> dict:
    key = jax.random.key(seed)
    ks = jax.random.split(key, 21)

    def nrm(k, shape, scale):
        return jax.random.normal(k, shape, jnp.float32) * scale

    def gain(k):
        return 1.0 + nrm(k, (DEPTH, D_MODEL), 0.02)

    return {
        "x": nrm(ks[0], (BATCH, SEQ, D_MODEL), 1.0),
        "meta_tokens": nrm(ks[1], (N_META, D_MODEL), 1.0),
        "w_in": nrm(ks[2], (DEPTH, D_MODEL, N_IN), D_MODEL ** -0.5),
        "w_alpha_up": nrm(ks[3], (DEPTH, GLA_GATE_RANK, GLA_KWIDTH), GLA_GATE_RANK ** -0.5),
        "b_alpha": nrm(ks[4], (DEPTH, GLA_KWIDTH), 0.1),
        "b_f": 2.0 + nrm(ks[5], (DEPTH, FOX_HEADS), 0.1),
        "g_gla_out": 1.0 + nrm(ks[6], (DEPTH, GLA_WIDTH), 0.02),
        "w_fox_o": nrm(ks[7], (DEPTH, FOX_WIDTH, D_MODEL), FOX_WIDTH ** -0.5),
        "w_gla_o": nrm(ks[8], (DEPTH, GLA_WIDTH, D_MODEL), GLA_WIDTH ** -0.5),
        "w_out": nrm(ks[9], (DEPTH, D_MODEL, D_MODEL), D_MODEL ** -0.5),
        "w_ffn1_gu": nrm(ks[10], (DEPTH, D_MODEL, 2 * D_FF), D_MODEL ** -0.5),
        "w_ffn1_down": nrm(ks[11], (DEPTH, D_FF, D_MODEL), D_FF ** -0.5),
        "w_ffn2_gu": nrm(ks[12], (DEPTH, D_MODEL, 2 * D_FF), D_MODEL ** -0.5),
        "w_ffn2_down": nrm(ks[13], (DEPTH, D_FF, D_MODEL), D_FF ** -0.5),
        "g_pre_ffn1": gain(ks[14]),
        "g_post_ffn1": gain(ks[15]),
        "g_pre_mix": gain(ks[16]),
        "g_post_mix": gain(ks[17]),
        "g_pre_ffn2": gain(ks[18]),
        "g_post_ffn2": gain(ks[19]),
    }

def first_block(x, meta_tokens, w_in, w_alpha_up, b_alpha, b_f, g_gla_out, w_fox_o, w_gla_o, w_out,
              w_ffn1_gu, w_ffn1_down, w_ffn2_gu, w_ffn2_down,
              g_pre_ffn1, g_post_ffn1, g_pre_mix, g_post_mix, g_pre_ffn2, g_post_ffn2):
    b = x.shape[0]
    pad = jnp.zeros((b, N_PAD, D_MODEL), x.dtype)
    meta = jnp.broadcast_to(meta_tokens.astype(x.dtype)[None], (b, N_META, D_MODEL))
    h = jnp.concatenate([pad, meta, x], axis=1)
    key_valid = jnp.arange(h.shape[1]) >= N_PAD
    for l in range(DEPTH):
        h = h + 0.5 * rmsnorm(swiglu(rmsnorm(h, g_pre_ffn1[l]), w_ffn1_gu[l], w_ffn1_down[l]), g_post_ffn1[l])
        mix = token_mixer(rmsnorm(h, g_pre_mix[l]), key_valid, w_in[l], w_alpha_up[l], b_alpha[l], b_f[l],
                          g_gla_out[l], w_fox_o[l], w_gla_o[l], w_out[l])
        h = h + rmsnorm(mix, g_post_mix[l])
        h = h + 0.5 * rmsnorm(swiglu(rmsnorm(h, g_pre_ffn2[l]), w_ffn2_gu[l], w_ffn2_down[l]), g_post_ffn2[l])
    return h[:, BLOCK:]


N_A_LAYERS = DEPTH // 2
N_B_LAYERS = DEPTH - N_A_LAYERS
MEM_TOKENS = 256
D_FF_2 = 2816
HEAD_DIM = 64
MEM_HEADS = 4
MEM_WIDTH = MEM_HEADS * HEAD_DIM
MLSTM_HEADS = 4
MLSTM_HEAD_DIM = 192
MLSTM_WIDTH = MLSTM_HEADS * MLSTM_HEAD_DIM
MLSTM_CHUNK = 128
CONV_WIDTH = 4
DILATED_GROUPS = ((128, 1), (512, 4), (2048, 16))
HEADS_PER_GROUP = 4
N_DIL_HEADS = HEADS_PER_GROUP * len(DILATED_GROUPS)
DIL_WIDTH = N_DIL_HEADS * HEAD_DIM
A_IN_WIDTH = 4 * MLSTM_WIDTH + 2 * MLSTM_HEADS + MEM_WIDTH
B_IN_WIDTH = DIL_WIDTH + MEM_WIDTH
NUM_BUCKETS = 32
MAX_DISTANCE = 2048
NEG_INF = -1e30
ATTN_SCALE = HEAD_DIM ** -0.5


def rms_norm(x, gain):
    xf = x.astype(jnp.float32)
    y = xf * lax.rsqrt(jnp.mean(xf * xf, axis=-1, keepdims=True) + RMS_EPS)
    return (y * gain.astype(jnp.float32)).astype(x.dtype)

def swiglu_2(h, w_gate, w_up, w_down):
    return (jax.nn.silu(h @ w_gate) * (h @ w_up)) @ w_down

def causal_conv(x, w):
    C = x.shape[-1]
    return lax.conv_general_dilated(x, w[:, None, :].astype(x.dtype), window_strides=(1,),
                                    padding=[(w.shape[0] - 1, 0)],
                                    dimension_numbers=('NWC', 'WIO', 'NWC'),
                                    feature_group_count=C)

def t5_causal_bucket(dist):
    max_exact = NUM_BUCKETS // 2
    d_f = jnp.maximum(dist, 1).astype(jnp.float32)
    large = max_exact + (jnp.log(d_f / max_exact) / math.log(MAX_DISTANCE / max_exact)
                         * (NUM_BUCKETS - max_exact)).astype(jnp.int32)
    large = jnp.minimum(large, NUM_BUCKETS - 1)
    return jnp.where(dist < max_exact, dist, large)

def mlstm_chunkwise(q, k, v, i_pre, f_pre):
    B, S, H, DK = q.shape
    DV = v.shape[-1]
    L = MLSTM_CHUNK
    NC = S // L
    f32 = jnp.float32

    def chunks(t):
        t = t.astype(f32).reshape(B, NC, L, H, *t.shape[3:])
        return jnp.moveaxis(t, 3, 2)

    qc = chunks(q)
    kc = chunks(k) * (DK ** -0.5)
    vc = chunks(v)
    ic = chunks(i_pre)
    logf = jax.nn.log_sigmoid(chunks(f_pre))
    b = jnp.cumsum(logf, axis=-1)
    b_last = b[..., -1]
    a = b_last[..., None] - b + ic

    def step(carry, xs):
        C, n, m = carry
        k_j, v_j, a_j, bl_j = xs
        m_new = jnp.maximum(bl_j + m, jnp.max(a_j, axis=-1))
        w = jnp.exp(a_j - m_new[..., None])
        decay = jnp.exp(bl_j + m - m_new)
        C_new = decay[..., None, None] * C + jnp.einsum('bhl,bhlk,bhlv->bhkv', w, k_j, v_j)
        n_new = decay[..., None] * n + jnp.einsum('bhl,bhlk->bhk', w, k_j)
        return (C_new, n_new, m_new), (C, n, m)

    init = (jnp.zeros((B, H, DK, DV), f32), jnp.zeros((B, H, DK), f32), jnp.zeros((B, H), f32))
    xs = (jnp.moveaxis(kc, 1, 0), jnp.moveaxis(vc, 1, 0), jnp.moveaxis(a, 1, 0), jnp.moveaxis(b_last, 1, 0))
    _, (C0, n0, m0) = lax.scan(step, init, xs)
    C0 = jnp.moveaxis(C0, 0, 1)
    n0 = jnp.moveaxis(n0, 0, 1)
    m0 = jnp.moveaxis(m0, 0, 1)

    causal = jnp.tril(jnp.ones((L, L), dtype=bool))
    Dlog = jnp.where(causal, b[..., :, None] - b[..., None, :] + ic[..., None, :], NEG_INF)
    g = b + m0[..., None]
    m_t = jnp.maximum(g, jnp.max(Dlog, axis=-1))
    W = jnp.exp(Dlog - m_t[..., None]) * jnp.einsum('bchtk,bchsk->bchts', qc, kc)
    inter = jnp.exp(g - m_t)
    num = jnp.einsum('bchts,bchsv->bchtv', W, vc) + inter[..., None] * jnp.einsum('bchtk,bchkv->bchtv', qc, C0)
    den = jnp.sum(W, axis=-1) + inter * jnp.einsum('bchtk,bchk->bcht', qc, n0)
    h = num / jnp.maximum(jnp.abs(den), jnp.exp(-m_t))[..., None]
    return jnp.moveaxis(h, 2, 3).reshape(B, S, H, DV)

def dilated_group_attention(q, k, v, bias_table, window, dilation):
    B, S, H, E = q.shape
    blk = window // dilation
    span = window
    Lp = -(-S // span) * span
    nb = Lp // span
    pad = ((0, 0), (0, Lp - S), (0, 0), (0, 0))

    def to_blocks(t):
        t = jnp.pad(t.astype(jnp.float32), pad).reshape(B, Lp // dilation, dilation, H, E)
        return jnp.transpose(t, (0, 2, 1, 3, 4)).reshape(B, dilation, nb, blk, H, E)

    qb = to_blocks(q)
    kb = to_blocks(k)
    vb = to_blocks(v)
    prev = lambda t: jnp.pad(t, ((0, 0), (0, 0), (1, 0), (0, 0), (0, 0), (0, 0)))[:, :, :-1]
    kk = jnp.concatenate([prev(kb), kb], axis=3)
    vv = jnp.concatenate([prev(vb), vb], axis=3)

    qi = jnp.arange(blk)[:, None]
    kj = jnp.arange(2 * blk)[None, :]
    m_off = qi + blk - kj
    band = (m_off >= 0) & (m_off <= blk)
    bucket = t5_causal_bucket(jnp.clip(m_off, 0, blk) * dilation)
    bias = jnp.transpose(bias_table.astype(jnp.float32)[bucket], (2, 0, 1))
    n_idx = jnp.arange(nb)[:, None, None]
    allowed = band[None] & ~((n_idx == 0) & (kj[None] < blk))

    s = jnp.einsum('brnqhe,brnkhe->brnhqk', qb, kk) * ATTN_SCALE + bias
    s = jnp.where(allowed[:, None], s, NEG_INF)
    mx = jnp.max(s, axis=-1, keepdims=True)
    p = jnp.exp(s - mx)
    den = jnp.sum(p, axis=-1)
    out = jnp.einsum('brnhqk,brnkhe->brnqhe', p, vv) / jnp.moveaxis(den, 3, 4)[..., None]
    lse = mx[..., 0] + jnp.log(den)

    out = jnp.transpose(out.reshape(B, dilation, Lp // dilation, H, E), (0, 2, 1, 3, 4)).reshape(B, Lp, H, E)[:, :S]
    lse = jnp.moveaxis(lse, 3, 4).reshape(B, dilation, Lp // dilation, H)
    lse = jnp.transpose(lse, (0, 2, 1, 3)).reshape(B, Lp, H)[:, :S]
    return out, lse

def memory_cross_attention(q_mem, mem_n, w_mem_kv, q_gain, k_gain):
    B, S, _ = q_mem.shape
    M = mem_n.shape[1]
    q = rms_norm(q_mem.reshape(B, S, MEM_HEADS, HEAD_DIM), q_gain)
    kv = mem_n @ w_mem_kv
    k = rms_norm(kv[..., :MEM_WIDTH].reshape(B, M, MEM_HEADS, HEAD_DIM), k_gain)
    v = kv[..., MEM_WIDTH:].reshape(B, M, MEM_HEADS, HEAD_DIM)
    s = jnp.einsum('bshe,bmhe->bhsm', q.astype(jnp.float32), k.astype(jnp.float32)) * ATTN_SCALE
    p = jax.nn.softmax(s, axis=-1)
    out = jnp.einsum('bhsm,bmhe->bshe', p, v.astype(jnp.float32))
    return out.reshape(B, S, MEM_WIDTH).astype(q_mem.dtype)

def mlstm_mixer(h, mem_n, w_in, conv_w, gate_bias, h_gain, w_out, w_mem_kv, mq_gain, mk_gain):
    B, S, _ = h.shape
    W = MLSTM_WIDTH
    p = h @ w_in
    qk = jax.nn.silu(causal_conv(p[..., :2 * W], conv_w))
    v = p[..., 2 * W:3 * W]
    o = p[..., 3 * W:4 * W]
    gates = p[..., 4 * W:4 * W + 2 * MLSTM_HEADS].astype(jnp.float32) + gate_bias.astype(jnp.float32)
    q_mem = p[..., 4 * W + 2 * MLSTM_HEADS:]
    heads = lambda t: t.reshape(B, S, MLSTM_HEADS, MLSTM_HEAD_DIM)
    cell = mlstm_chunkwise(heads(qk[..., :W]), heads(qk[..., W:]), heads(v),
                           gates[..., :MLSTM_HEADS], gates[..., MLSTM_HEADS:])
    cell = rms_norm(cell, h_gain).reshape(B, S, W)
    h_a = (jax.nn.sigmoid(o.astype(jnp.float32)) * cell).astype(h.dtype)
    h_m = memory_cross_attention(q_mem, mem_n, w_mem_kv, mq_gain, mk_gain)
    return jnp.concatenate([h_a, h_m], axis=-1) @ w_out

def dilated_mixer(h, mem_n, k_sh, v_sh, w_q, q_gain, w_out, rel_bias, w_mem_kv, mq_gain, mk_gain):
    B, S, _ = h.shape
    p = h @ w_q
    q_d = rms_norm(p[..., :DIL_WIDTH].reshape(B, S, len(DILATED_GROUPS), HEADS_PER_GROUP, HEAD_DIM), q_gain)
    outs, lses = [], []
    for g, (window, dilation) in enumerate(DILATED_GROUPS):
        table = rel_bias[:, g * HEADS_PER_GROUP:(g + 1) * HEADS_PER_GROUP]
        o_g, l_g = dilated_group_attention(q_d[:, :, g], k_sh[:, :, g], v_sh[:, :, g], table, window, dilation)
        outs.append(o_g)
        lses.append(l_g)
    outs = jnp.stack(outs, axis=2)
    alpha = jax.nn.softmax(jnp.stack(lses, axis=2), axis=2)
    h_d = (outs * alpha[..., None]).reshape(B, S, DIL_WIDTH).astype(h.dtype)
    h_m = memory_cross_attention(p[..., DIL_WIDTH:], mem_n, w_mem_kv, mq_gain, mk_gain)
    return jnp.concatenate([h_d, h_m], axis=-1) @ w_out

def second_inputs(seed: int = 0) -> dict:
    key = jax.random.key(seed)
    ks = iter(jax.random.split(key, 40))
    nrm = lambda shape, scale: jax.random.normal(next(ks), shape, jnp.float32) * scale
    gain = lambda shape: 1.0 + nrm(shape, 0.02)
    D, F = D_MODEL, D_FF_2
    return {
        'x': nrm((BATCH, SEQ, D), 1.0),
        'mem': nrm((BATCH, MEM_TOKENS, D), 1.0),
        'ffn1_norm': gain((DEPTH, D)),
        'ffn1_w_gate': nrm((DEPTH, D, F), D ** -0.5),
        'ffn1_w_up': nrm((DEPTH, D, F), D ** -0.5),
        'ffn1_w_down': nrm((DEPTH, F, D), F ** -0.5),
        'ffn2_norm': gain((DEPTH, D)),
        'ffn2_w_gate': nrm((DEPTH, D, F), D ** -0.5),
        'ffn2_w_up': nrm((DEPTH, D, F), D ** -0.5),
        'ffn2_w_down': nrm((DEPTH, F, D), F ** -0.5),
        'mix_norm': gain((DEPTH, D)),
        'mem_norm': gain((DEPTH, D)),
        'w_mem_kv': nrm((DEPTH, D, 2 * MEM_WIDTH), D ** -0.5),
        'mem_q_norm': gain((DEPTH, HEAD_DIM)),
        'mem_k_norm': gain((DEPTH, HEAD_DIM)),
        'a_w_in': nrm((N_A_LAYERS, D, A_IN_WIDTH), D ** -0.5),
        'a_conv': nrm((N_A_LAYERS, CONV_WIDTH, 2 * MLSTM_WIDTH), CONV_WIDTH ** -0.5),
        'a_gate_bias': jnp.concatenate([nrm((N_A_LAYERS, MLSTM_HEADS), 0.1),
                                        3.0 + nrm((N_A_LAYERS, MLSTM_HEADS), 0.5)], axis=-1),
        'a_h_norm': gain((N_A_LAYERS, MLSTM_HEADS, MLSTM_HEAD_DIM)),
        'a_w_out': nrm((N_A_LAYERS, MLSTM_WIDTH + MEM_WIDTH, D), (MLSTM_WIDTH + MEM_WIDTH) ** -0.5),
        'b_w_q': nrm((N_B_LAYERS, D, B_IN_WIDTH), D ** -0.5),
        'b_q_norm': gain((N_B_LAYERS, HEAD_DIM)),
        'b_w_out': nrm((N_B_LAYERS, DIL_WIDTH + MEM_WIDTH, D), (DIL_WIDTH + MEM_WIDTH) ** -0.5),
        'kv_norm': gain((D,)),
        'w_kv': nrm((D, 2 * DIL_WIDTH), D ** -0.5),
        'kv_k_norm': gain((HEAD_DIM,)),
        'rel_bias': nrm((NUM_BUCKETS, N_DIL_HEADS), 0.3),
    }

def second_block(x, mem, ffn1_norm, ffn1_w_gate, ffn1_w_up, ffn1_w_down,
              ffn2_norm, ffn2_w_gate, ffn2_w_up, ffn2_w_down,
              mix_norm, mem_norm, w_mem_kv, mem_q_norm, mem_k_norm,
              a_w_in, a_conv, a_gate_bias, a_h_norm, a_w_out,
              b_w_q, b_q_norm, b_w_out, kv_norm, w_kv, kv_k_norm, rel_bias):
    B, S, _ = x.shape
    n_groups = len(DILATED_GROUPS)
    k_sh = None
    v_sh = None
    for layer in range(DEPTH):
        x = x + 0.5 * swiglu_2(rms_norm(x, ffn1_norm[layer]), ffn1_w_gate[layer], ffn1_w_up[layer], ffn1_w_down[layer])
        h = rms_norm(x, mix_norm[layer])
        mem_n = rms_norm(mem, mem_norm[layer])
        if layer < N_A_LAYERS:
            ia = layer
            mix = mlstm_mixer(h, mem_n, a_w_in[ia], a_conv[ia], a_gate_bias[ia], a_h_norm[ia], a_w_out[ia],
                              w_mem_kv[layer], mem_q_norm[layer], mem_k_norm[layer])
        else:
            ib = layer - N_A_LAYERS
            mix = dilated_mixer(h, mem_n, k_sh, v_sh, b_w_q[ib], b_q_norm[ib], b_w_out[ib], rel_bias,
                                w_mem_kv[layer], mem_q_norm[layer], mem_k_norm[layer])
        x = x + mix
        x = x + 0.5 * swiglu_2(rms_norm(x, ffn2_norm[layer]), ffn2_w_gate[layer], ffn2_w_up[layer], ffn2_w_down[layer])
        if layer == N_A_LAYERS - 1:
            kv = rms_norm(x, kv_norm) @ w_kv
            k_sh = rms_norm(kv[..., :DIL_WIDTH].reshape(B, S, N_DIL_HEADS, HEAD_DIM), kv_k_norm)
            k_sh = k_sh.reshape(B, S, n_groups, HEADS_PER_GROUP, HEAD_DIM)
            v_sh = kv[..., DIL_WIDTH:].reshape(B, S, n_groups, HEADS_PER_GROUP, HEAD_DIM)
    return x


def setup_inputs(seed=0):
    out = dict(first_inputs(seed))
    for name, value in second_inputs(seed + 1).items():
        if name != "x":
            out[name + "_2"] = value
    return out


def reference(
    x, meta_tokens, w_in, w_alpha_up, b_alpha, b_f, g_gla_out, w_fox_o, w_gla_o, w_out,
    w_ffn1_gu, w_ffn1_down, w_ffn2_gu, w_ffn2_down, g_pre_ffn1, g_post_ffn1, g_pre_mix,
    g_post_mix, g_pre_ffn2, g_post_ffn2, mem_2, ffn1_norm_2, ffn1_w_gate_2, ffn1_w_up_2,
    ffn1_w_down_2, ffn2_norm_2, ffn2_w_gate_2, ffn2_w_up_2, ffn2_w_down_2, mix_norm_2,
    mem_norm_2, w_mem_kv_2, mem_q_norm_2, mem_k_norm_2, a_w_in_2, a_conv_2, a_gate_bias_2,
    a_h_norm_2, a_w_out_2, b_w_q_2, b_q_norm_2, b_w_out_2, kv_norm_2, w_kv_2, kv_k_norm_2,
    rel_bias_2,
):
    x = first_block(
        x, meta_tokens, w_in, w_alpha_up, b_alpha, b_f, g_gla_out, w_fox_o, w_gla_o, w_out,
        w_ffn1_gu, w_ffn1_down, w_ffn2_gu, w_ffn2_down, g_pre_ffn1, g_post_ffn1, g_pre_mix,
        g_post_mix, g_pre_ffn2, g_post_ffn2,
    )
    return second_block(
        x, mem_2, ffn1_norm_2, ffn1_w_gate_2, ffn1_w_up_2, ffn1_w_down_2, ffn2_norm_2,
        ffn2_w_gate_2, ffn2_w_up_2, ffn2_w_down_2, mix_norm_2, mem_norm_2, w_mem_kv_2,
        mem_q_norm_2, mem_k_norm_2, a_w_in_2, a_conv_2, a_gate_bias_2, a_h_norm_2, a_w_out_2,
        b_w_q_2, b_q_norm_2, b_w_out_2, kv_norm_2, w_kv_2, kv_k_norm_2, rel_bias_2,
    )


_drawn_inputs = setup_inputs


def setup_inputs(seed=0):
    import zlib

    import numpy as np

    out = dict(_drawn_inputs(seed))
    spreads = {}
    factors = {'g_gla_out': 2.799,
     'g_pre_ffn2': 3.656,
     'g_post_ffn2': 5.236,
     'ffn1_norm_2': 8.0,
     'ffn2_norm_2': 8.0,
     'mix_norm_2': 7.617,
     'mem_norm_2': 8.0,
     'mem_q_norm_2': 8.0,
     'mem_k_norm_2': 8.0,
     'a_h_norm_2': 41.966,
     'b_q_norm_2': 42.457,
     'kv_norm_2': 33.094,
     'kv_k_norm_2': 37.492,
     'rel_bias_2': 50.829}
    for name, (base, spread) in spreads.items():
        noise = np.random.default_rng([zlib.crc32(name.encode()), seed]).standard_normal(out[name].shape)
        drawn = base * np.exp(spread * noise) if base else spread * noise
        out[name] = __import__('jax').numpy.asarray(drawn.astype(out[name].dtype))
    for name, factor in factors.items():
        out[name] = (out[name] * factor).astype(out[name].dtype)
    return out
```

```python
import math
from contextlib import ExitStack

import numpy as np

import concourse.bass as bass
from concourse import mybir

F32 = mybir.dt.float32
ALU = mybir.AluOpType
ACT = mybir.ActivationFunctionType
AX_X = mybir.AxisListType.X

P = 128
D = 1024
KD = D // P
SEQ = 256
N_META = 16
T1 = N_META + SEQ
DEPTH = 2
D_FF = 2816
NF = D_FF // P
EPS = 1e-6
NEG = -1e30
RING = 11
SLOT = 2048
HALF = NF // 2
assert HALF == RING

FOX_HEADS, HD = 8, 64
FOX_W = FOX_HEADS * HD
GLA_HEADS, GLA_DK, GLA_DV = 4, 64, 128
GLA_KW, GLA_W, GATE_RANK = GLA_HEADS * GLA_DK, GLA_HEADS * GLA_DV, 16
SUB = 16
N_SUB = T1 // SUB
SPLIT = (FOX_W, FOX_W, FOX_W, FOX_HEADS, GLA_KW, GLA_KW, GLA_W, GATE_RANK, GLA_W, D, D)
SPLIT_AT = [sum(SPLIT[:i]) for i in range(len(SPLIT))]

ML_HEADS, ML_DK = 4, 192
ML_W = ML_HEADS * ML_DK
MH = ML_DK // 2
MEM_W = 256
DIL_GROUPS = ((128, 1), (512, 4), (2048, 16))
DIL_HEADS = 4
DIL_W = 3 * DIL_HEADS * HD
BUCKETS, MAX_DIST = 32, 2048

TOK_TILES1 = [(0, 128), (128, 128), (256, 16)]
TOK_TILES2 = [(0, 128), (128, 128)]


CONST_W = [("ident", 128), ("mean1024", 128), ("mean128", 128), ("mean64", 128), ("mean192", 128), ("ones", T1),
           ("causal", 384), ("causalT", 256), ("pickd", 2 * 80), ("spread", GLA_HEADS * 240), ("dmask", T1),
           ("sel", 4 * 128)]
CONST_AT = {}
_at = 0
for _n, _w in CONST_W:
    CONST_AT[_n] = (_at, _w)
    _at += _w
CONST_N = _at


def constants():
    c = {n: np.zeros((P, w), np.float32) for n, w in CONST_W}
    p = np.arange(P)
    c["ident"][p, p] = 1.0
    c["mean1024"][:] = 1.0 / D
    c["mean128"][:] = 1.0 / GLA_DV
    c["mean64"][:] = (p[:, None] // HD == p[None, :] // HD) / HD
    c["mean192"][:] = 1.0 / ML_DK
    c["ones"][:] = 1.0
    c["causal"][:] = np.where(np.arange(384)[None, :] <= p[:, None] + 256, 0.0, NEG)
    c["causalT"][:] = np.where(np.arange(256)[None, :] >= p[:, None], 0.0, NEG)
    for ct in range(2):
        for half in range(2):
            c["pickd"][half * 64:half * 64 + 64, ct * 80 + 15 + 16 * (2 * ct + half)] = 1.0
    for h in range(GLA_HEADS):
        for j in range(SUB):
            c["spread"][16 * h + j, 240 * h + 112 + j] = 1.0
    for r in range(64):
        c["dmask"][r, :] = (np.arange(T1) % SUB) >= r % SUB
    for h in range(4):
        c["sel"][h, 128 * h:128 * h + 128] = 1.0
    return np.ascontiguousarray(np.concatenate([c[n] for n, _ in CONST_W], axis=1))


def bucket_rows():
    oh = np.zeros((BUCKETS + 1, 3 * 512), np.float32)
    for g, (window, dil) in enumerate(DIL_GROUPS):
        for u in range(512):
            d = 255 - u
            if d < 0 or d % dil or d > window:
                b = BUCKETS
            elif d < BUCKETS // 2:
                b = d
            else:
                e = BUCKETS // 2
                b = min(e + int(math.log(d / e) / math.log(MAX_DIST / e) * (BUCKETS - e)), BUCKETS - 1)
            oh[b, 512 * g + u] = 1.0
    return oh


class Lane:

    def __init__(self, name, eng, sem, spare):
        self.name, self.eng, self.sem = name, eng, sem
        self.n = 0
        self.open = False
        self.spare = spare
        self.loop = 0
        self.seen = {}

    def at(self, n):
        return (self.sem, self.loop, n)

    def now(self):
        return self.at(self.n)

    def wait(self, *toks):
        for tok in toks:
            if tok is None:
                continue
            sem, loop, n = tok
            if isinstance(loop, int) and loop + n <= 0:
                continue
            key = sem.name
            if self.seen.get(key, -10 ** 9) >= n:
                continue
            self.seen[key] = n
            self.eng.wait_ge(sem, loop + n)
            self.open = not isinstance(loop, int)

    def settle(self):
        if self.open:
            self.eng.sem_inc(self.spare, 1)
            self.open = False

    def tick(self, ins):
        ins.then_inc(self.sem, 1)
        self.n += 1
        return self.now()


class Ring:

    def __init__(self, nc, sync, buf, full, free, spare):
        self.spare = spare
        self.nc, self.sync, self.buf, self.full, self.free = nc, sync, buf, full, free
        self.n = 0
        self.loop = 0
        self.freed = 0

    def load(self, src, rows=P):
        slot, n = self.n % RING, self.n
        a, b = src.shape[1], src.shape[2]
        dst = self.buf[0:rows, slot, 0:a * b].rearrange("p (a b) -> p a b", a=a)
        self.sync.wait_ge(self.free, self.loop + n + 1)
        if not isinstance(self.loop, int):
            self.sync.sem_inc(self.spare, 1)
        self.sync.dma_start(dst, src).then_inc(self.full[slot], 16)
        per = 0 if isinstance(self.loop, int) else self.loop16
        self.n += 1
        return dst, (self.full[slot], per, 16 * (n // RING + 1))

    def release(self, ins):
        ins.then_inc(self.free, 1)
        self.freed += 1
        return (self.free, self.loop, RING + self.freed)


def program(nc, IN, out):
    ctx = ExitStack()
    with ctx:
        def sb(name, shape):
            return ctx.enter_context(nc.sbuf_tensor(name, shape, F32))

        def sem(name):
            return ctx.enter_context(nc.semaphore(name))

        bank = [ctx.enter_context(nc.psum_tensor(f"bank{i}", [P, 512], F32)) for i in range(8)]
        wring = sb("wring", [P, RING, SLOT])
        hT = sb("hT", [P, KD, T1])
        xn = sb("xn", [P, KD, T1])
        act = sb("act", [P, NF, T1])
        sg = sb("sg", [P, 3, T1])
        rst = sb("rst", [P, T1])
        cst = sb("cst", [P, CONST_N])
        gain1 = sb("gain1", [P, 108])
        gain2 = sb("gain2", [P, 80])
        gain3 = sb("gain3", [MH, 72])
        gcur = sb("gcur", [P, 56])
        small = sb("small", [P, 64])
        wau = sb("wau", [GATE_RANK, GLA_KW])
        rst2 = sb("rst2", [P, T1])
        rz = sb("rz", [P, T1])
        ry = sb("ry", [P, T1])
        arena = sb("arena", [P, 14300])

        def C(name):
            a, w = CONST_AT[name]
            return cst[:, a:a + w]

        full = [sem(f"full{i}") for i in range(RING)]
        free = sem("free")
        par = sem("par")
        s_in = sem("s_in")
        s_bias = sem("s_bias")
        s_out = sem("s_out")
        spare = sem("spare")
        PE = Lane("pe", nc.tensor, sem("pe_done"), spare)
        AC = Lane("act", nc.scalar, sem("act_done"), spare)
        VE = Lane("dve", nc.vector, sem("dve_done"), spare)
        PO = Lane("pool", nc.gpsimd, sem("pool_done"), spare)
        lanes = [PE, AC, VE, PO]
        nc.sync.sem_inc(free, RING)
        ring = Ring(nc, nc.sync, wring, full, free, spare)
        par_n = [0, 0]

        def ve(fn, toks, *a, **k):
            VE.wait(*toks)
            return VE.tick(getop(nc.vector, fn)(*a, **k))

        def po(fn, toks, *a, **k):
            PO.wait(*toks)
            PO.settle()
            return PO.tick(getop(nc.gpsimd, fn)(*a, **k))

        def getop(eng, fn):
            return {"tt": eng.tensor_tensor, "ts": eng.tensor_scalar, "copy": eng.tensor_copy, "memset": eng.memset,
                    "stt": nc.vector.scalar_tensor_tensor, "ttr": nc.vector.tensor_tensor_reduce,
                    "scan": nc.vector.tensor_tensor_scan, "rmax": nc.vector.reduce_max,
                    "recip": nc.vector.reciprocal}[fn]

        def ac(toks, out_, in_, func, **k):
            AC.wait(*toks)
            return AC.tick(nc.scalar.activation(out_, in_, func, **k))

        def mm(out_, lhsT, rhs, start, stop):
            return nc.tensor.matmul(out_, lhsT, rhs, start=start, stop=stop, skip_group_check=True)

        def rsqrt(dst, src, toks):
            z = rz[0:src.shape[0], 0:src.shape[1]]
            rd = ve("ts", toks, z, src, EPS, None, ALU.add)
            t = ac([rd], dst, z, ACT.Ln)
            t = ac([t], dst, dst, ACT.Exp, scale=-0.5)
            u = ry[0:src.shape[0], 0:src.shape[1]]
            t = ve("stt", [t], u, dst, -0.5, dst, ALU.mult, ALU.mult)
            t = ve("tt", [t], u, u, z, ALU.mult)
            return ve("stt", [t], dst, u, 1.5, dst, ALU.add, ALU.mult)

        def par_load(dst, src, toks=(), slow=False):
            PO.wait(*toks)
            PO.settle()
            if slow:
                with nc.allow_non_contiguous_dma(reason="a few small columns"):
                    nc.gpsimd.dma_start(dst, src).then_inc(par, 16)
            else:
                nc.gpsimd.dma_start(dst, src).then_inc(par, 16)
            par_n[0] += 16

        def par_all():
            return (par, par_n[1], par_n[0])

        def forget():
            for ln in lanes:
                ln.seen = {}

        def join():
            toks = [ln.now() for ln in lanes]
            for ln in lanes:
                ln.wait(*[t for t in toks if t[0] is not ln.sem])

        class Layout:

            def __init__(self, base, at=0, top=None):
                self.base, self.at, self.top = base, at, top if top is not None else base.shape[1]

            def take(self, *shape):
                n = 1
                for s in shape:
                    n *= s
                assert self.at + n <= self.top, (self.at, n, self.top)
                v = self.base[:, self.at:self.at + n]
                self.at += n
                if len(shape) == 2:
                    v = v.rearrange("p (a b) -> p a b", a=shape[0])
                elif len(shape) == 3:
                    v = v.rearrange("p (a b c) -> p a b c", a=shape[0], b=shape[1])
                return v

        h_tok = [None] * KD

        start = Layout(arena)
        g1 = start.take(P)
        g2 = start.take(P)
        g3 = start.take(P)
        xs = start.take(3, D)
        nc.scalar.dma_start(cst[:, :], IN["consts"]).then_inc(s_in, 16)
        nc.scalar.dma_start(xs[0:N_META, 2, :], IN["meta_tokens"]).then_inc(s_in, 16)
        nc.scalar.dma_start(xs[:, 0:2, :], IN["x"][0].rearrange("(t p) d -> p t d", p=P)).then_inc(s_in, 16)
        for i, name in enumerate(("g_pre_ffn1", "g_post_ffn1", "g_pre_mix", "g_post_mix", "g_pre_ffn2", "g_post_ffn2")):
            par_load(g1[16 * i:16 * i + 16, :], IN[name].rearrange("l (k p) -> (l k) p", p=P))
        par_load(g1[96:100, :], IN["b_alpha"].rearrange("l (k p) -> (l k) p", p=P))
        par_load(g1[100:108, :], IN["g_gla_out"].rearrange("l (k p) -> (l k) p", p=P))
        for i, name in enumerate(("ffn1_norm_2", "ffn2_norm_2", "mix_norm_2", "mem_norm_2")):
            par_load(g2[16 * i:16 * i + 16, :], IN[name].rearrange("l (k p) -> (l k) p", p=P))
        par_load(g2[64:72, :], IN["kv_norm_2"].rearrange("(k p) -> k p", p=P))
        for c in (0, HD):
            par_load(g2[72:74, c:c + HD], IN["mem_q_norm_2"])
            par_load(g2[74:76, c:c + HD], IN["mem_k_norm_2"])
            par_load(g2[76:77, c:c + HD], IN["b_q_norm_2"])
            par_load(g2[77:78, c:c + HD], IN["kv_k_norm_2"].rearrange("(a p) -> a p", a=1))
        par_load(g3[0:8, 0:MH], IN["a_h_norm_2"].rearrange("l h (j p) -> (l h j) p", p=MH))
        par_load(g3[8:72, 0:MH], IN["a_conv_2"].rearrange("l j (c p) -> (l j c) p", p=MH))
        PE.wait(par_all(), (s_in, 0, 48))
        VE.wait((s_in, 0, 48))
        AC.wait((s_in, 0, 48))
        ident = C("ident")
        for b, (src, rows, w, dst) in enumerate(((g1, 108, P, gain1), (g2, 78, P, gain2), (g3, 72, MH, gain3))):
            t = PE.tick(nc.tensor.transpose(bank[b][0:w, 0:rows], src[0:rows, 0:w], ident[0:rows, 0:rows]))
            ve("copy", [t], dst[:, 0:rows], bank[b][0:w, 0:rows])
        ve("ts", [VE.now()], gain2[:, 72:74], gain2[:, 72:74], HD ** -0.5, None, ALU.mult)
        ve("ts", [VE.now()], gain2[:, 76:77], gain2[:, 76:77], HD ** -0.5, None, ALU.mult)
        taken = [None] * 8

        def turn_rows(src, rows, t, dst, c0):
            for k in range(KD):
                b = 4 + k % 4
                PE.wait(taken[b])
                tk = PE.tick(nc.tensor.transpose(bank[b][:, 0:rows], src[0:rows, t, k * P:k * P + P], ident[0:rows, 0:rows]))
                taken[b] = ve("copy", [tk], dst[:, k, c0:c0 + rows], bank[b][:, 0:rows])
                h_tok[k] = taken[b]

        turn_rows(xs, N_META, 2, hT, 0)
        turn_rows(xs, P, 0, hT, N_META)
        turn_rows(xs, P, 1, hT, N_META + P)

        def rms_of(src, toks, mean, b, cols, n_tiles=KD, rows=P, dst=None):
            c0, c1 = cols
            for k in range(n_tiles):
                t = ac([toks[k]], act[:, k, c0:c1], src[:, k, c0:c1], ACT.Square)
                PE.wait(t)
                m = mm(bank[b][:, 0:c1 - c0], mean, act[:, k, c0:c1], k == 0, k == n_tiles - 1)
            t = PE.tick(m)
            return rsqrt((rst if dst is None else dst)[:, c0:c1], bank[b][:, 0:c1 - c0], [t])

        def prenorm(gain, cols):
            c0, c1 = cols
            PE.wait(VE.now())
            t = rms_of(hT, h_tok, C("mean1024"), 0, cols)
            return [ve("stt", [t, h_tok[k]], xn[:, k, c0:c1], hT[:, k, c0:c1], gain(k), rst[:, c0:c1], ALU.mult, ALU.mult)
                    for k in range(KD)]

        def ffn(gu_src, down_src, gain, cols, post):
            c0, c1 = cols
            T = c1 - c0
            xt = prenorm(gain, cols)
            PE.wait(*xt)
            forget()
            entry = {ln: (ln.n, ln.loop) for ln in lanes}
            ring_entry = (ring.n, ring.loop, ring.loop16 if not isinstance(ring.loop, int) else 0)
            for ln in lanes:
                ln.settle()
            with nc.Fori(0, 2) as half:
                for ln, per in ((PE, HALF), (AC, HALF), (VE, HALF)):
                    ln.loop = ln.loop + half * per
                ring.loop = ring.loop + half * HALF
                ring.loop16 = ring_entry[2] + half * 16
                v0 = VE.n
                for j in range(HALF):
                    gu, up_src = gu_src(half, j)
                    slot = ring.n % RING
                    w = wring[:, slot, :].rearrange("p (g k c) -> p g k c", g=2, k=KD)
                    ring.sync.wait_ge(ring.free, ring.loop + ring.n + 1)
                    ring.sync.sem_inc(spare, 1)
                    ring.sync.dma_start(w[:, 0], gu).then_inc(full[slot], 16)
                    ring.sync.dma_start(w[:, 1], up_src).then_inc(full2[slot], 16)
                    landed = (full[slot], ring.loop16, 16 * (ring.n // RING + 1))
                    landed2 = (full2[slot], *gu_count(half))
                    ring.n += 1
                    g, u = 2 * (j % 3), 2 * (j % 3) + 1
                    PE.wait(landed, VE.at(v0 + j - 1))
                    for k in range(KD):
                        m = mm(bank[g][:, 0:T], w[:, 0, k, :], xn[:, k, c0:c1], k == 0, k == KD - 1)
                    tg = PE.tick(m)
                    PE.wait(landed2)
                    for k in range(KD):
                        m = mm(bank[u][:, 0:T], w[:, 1, k, :], xn[:, k, c0:c1], k == 0, k == KD - 1)
                    tu = ring.release(m)
                    ts = ac([tg, VE.at(v0 + j - 1)], sg[:, j % 3, 0:T], bank[g][:, 0:T], ACT.Silu)
                    ve("tt", [ts, tu], act[:, half * HALF + j, c0:c1], sg[:, j % 3, 0:T], bank[u][:, 0:T], ALU.mult)
            for ln in (PE, AC, VE):
                assert ln.n == entry[ln][0] + HALF
                ln.n, ln.loop = ln.n + HALF, entry[ln][1]
            ring.n, ring.freed, ring.loop, ring.loop16 = ring.n + HALF, ring.freed + HALF, ring_entry[1], ring_entry[2]
            gu_total[0] += 2
            forget()
            PE.wait(VE.now())
            done = []
            for m2 in range(NF // 2):
                w, landed = ring.load(down_src(m2))
                PE.wait(landed)
                for r in range(2):
                    f = 2 * m2 + r
                    for d in range(KD):
                        m = mm(bank[d][:, 0:T], w[:, r, d * P:d * P + P], act[:, f, c0:c1], f == 0, f == NF - 1)
                        if f == NF - 1:
                            done.append(PE.tick(m) if d < KD - 1 else ring.release(m))
                        elif r == 1 and d == KD - 1:
                            ring.release(m)
            if post is None:
                for d in range(KD):
                    h_tok[d] = ve("stt", [done[d]], hT[:, d, c0:c1], bank[d][:, 0:T], 0.5, hT[:, d, c0:c1], ALU.mult, ALU.add)
            else:
                postnorm(done, post, 0.5, cols)

        def postnorm(done, gain, factor, cols):
            c0, c1 = cols
            T = c1 - c0
            tv, ts = [], []
            for d in range(KD):
                tv.append(ve("copy", [done[d]], act[:, KD + d, c0:c1], bank[d][:, 0:T]))
                ts.append(ac([tv[d]], act[:, d, c0:c1], act[:, KD + d, c0:c1], ACT.Square))
            PE.wait(tv[0])
            for d in range(KD):
                PE.wait(ts[d])
                m = mm(bank[0][:, 0:T], C("mean1024"), act[:, d, c0:c1], d == 0, d == KD - 1)
            t = rsqrt(rst[:, c0:c1], bank[0][:, 0:T], [PE.tick(m)])
            if factor != 1.0:
                t = ve("ts", [t], rst[:, c0:c1], rst[:, c0:c1], factor, None, ALU.mult)
            for d in range(KD):
                y = act[:, KD + d, c0:c1]
                ty = ve("stt", [t, tv[d]], y, y, gain(d), rst[:, c0:c1], ALU.mult, ALU.mult)
                h_tok[d] = po("tt", [ty], hT[:, d, c0:c1], hT[:, d, c0:c1], y, ALU.add)

        def free_all(count, t):
            PE.wait(t)
            nc.tensor.sem_inc(free, count)
            ring.freed += count

        def columns(wd, a, w):
            return wd.rearrange("(k p) n -> p k n", p=P)[:, :, a:a + w]

        proj_bank = [0]

        def next_bank():
            b = proj_bank[0]
            proj_bank[0] = 1 - b
            PE.wait(taken[b])
            return b

        def project(w, src, cols, c, M, last, n_k=KD):
            c0, c1 = cols
            b = next_bank()
            for k in range(n_k):
                m = mm(bank[b][0:M, 0:c1 - c0], w[:, k, c:c + M], src[:, k, c0:c1], k == 0, k == n_k - 1)
            return b, ring.release(m) if last else PE.tick(m)

        def project_rows(w, src, c0, n, N, last):
            b = next_bank()
            for k in range(KD):
                m = mm(bank[b][0:n, 0:N], src[:, k, c0:c0 + n], w[:, k, 0:N], k == 0, k == KD - 1)
            return b, ring.release(m) if last else PE.tick(m)

        def attention(units, bufs, s_banks, t_banks):
            SS, PP, PT, st = bufs
            s_free = [None, None]
            p_free = [None, None]
            t_free = [None, None]
            pt_free = [None, None]
            state = {}
            for i in range(len(units) + 2):
                if i < len(units):
                    u = units[i]
                    z = i % 2
                    n, W = u["n"], u["W"]
                    sb_ = s_banks[z]
                    PE.wait(s_free[z], *u["need"])
                    for (q, k, w, c) in u["qk"]:
                        m = mm(sb_[0:n, c:c + w], q, k, True, True)
                    t = PE.tick(m)
                    mx, nm, den, rd = (st[0:n, 4 * z + x:4 * z + x + 1] for x in range(4))
                    if u["mask"] is not None:
                        t = ve("tt", [t, p_free[z]], SS[z][0:n, 0:W], sb_[0:n, 0:W], u["mask"], ALU.add)
                        s_free[z] = t
                        src = SS[z][0:n, 0:W]
                    else:
                        src = sb_[0:n, 0:W]
                    t = ve("rmax", [t], mx, src, AX_X)
                    t = ve("ts", [t], nm, mx, -1.0, None, ALU.mult)
                    t = ac([t, p_free[z]], PP[z][0:n, 0:W], src, ACT.Exp, bias=nm, accum_out=den)
                    if u["mask"] is None:
                        s_free[z] = t
                    t = ve("recip", [t], rd, den)
                    t = ve("ts", [t], PP[z][0:n, 0:W], PP[z][0:n, 0:W], rd, None, ALU.mult)
                    state[i] = t
                if 0 <= i - 1 < len(units):
                    u = units[i - 1]
                    z = (i - 1) % 2
                    n = u["n"]
                    PE.wait(state[i - 1], t_free[z])
                    PE.settle()
                    for (c, ns, slot) in u["turn"]:
                        m = nc.tensor.transpose(t_banks[z][0:ns, slot * P:slot * P + n], PP[z][0:n, c:c + ns], ident[0:n, 0:n])
                    t = PE.tick(m)
                    p_free[z] = t
                    fulls = [s for s in u["turn"] if s[1] == P]
                    rest = [s for s in u["turn"] if s[1] != P]
                    nf = len(fulls)
                    if nf:
                        a = t_banks[z][:, 0:nf * P].rearrange("p (s c) -> p s c", c=P)[:, :, 0:n]
                        o = PT[z][:, 0:nf * P].rearrange("p (s c) -> p s c", c=P)[:, :, 0:n]
                        tc = ac([t, pt_free[z]], o, a, ACT.Copy)
                    for (c, ns, slot) in rest:
                        tc = ac([t, pt_free[z]], PT[z][0:ns, slot * P:slot * P + n], t_banks[z][0:ns, slot * P:slot * P + n], ACT.Copy)
                    t_free[z] = tc
                    state[i - 1] = tc
                if 0 <= i - 2 < len(units):
                    u = units[i - 2]
                    z = (i - 2) % 2
                    n = u["n"]
                    PE.wait(state[i - 2])
                    u["open"]()
                    for (o, terms) in u["pv"]:
                        for x, (slot, ns, v) in enumerate(terms):
                            m = mm(o, v, PT[z][0:ns, slot * P:slot * P + n], x == 0, x == len(terms) - 1)
                    t = PE.tick(m)
                    pt_free[z] = t
                    u["close"](t)
                yield

        def drive(main, sides):
            sides = list(sides)
            for _ in main:
                while sides:
                    try:
                        next(sides[0])
                        break
                    except StopIteration:
                        sides.pop(0)
            for s in sides:
                for _ in s:
                    pass

        def log_sigmoid(dst, z, scr, toks):
            t = ve("stt", toks, scr, z, -1.0, z, ALU.mult, ALU.max)
            t = ac([t], scr, scr, ACT.Exp, scale=-1.0)
            t = ac([t], scr, scr, ACT.Ln, bias=1.0)
            return ve("stt", [t], dst, z, 0.0, scr, ALU.min, ALU.subtract)

        cols1 = (0, T1)
        PER_LAYER = 4096
        LOADS = 99
        full2 = [sem(f"full2_{i}") for i in range(RING)]
        gu_total = [0]
        gu_layer = [0]

        def gu_count(half):
            return (half * 16 + gu_layer[0], 16 * (gu_total[0] + 1))

        w_in_at = dict(zip(("fq", "fk", "fv", "ff", "gq", "gk", "gv", "ga", "gr", "ma", "mb"), SPLIT_AT))

        def mixer1(L):
            lay = Layout(arena)
            qa = lay.take(FOX_HEADS, T1)
            ka = lay.take(FOX_HEADS, T1)
            fv = lay.take(3, FOX_W)
            gq = lay.take(2, T1)
            gk = lay.take(2, T1)
            gv = lay.take(3, GLA_W)
            cb = lay.take(2, T1)
            qz = lay.take(GLA_HEADS, T1)
            kz = lay.take(2, T1)
            gr = lay.take(4, T1)
            of = lay.take(4, T1)
            AT = lay.take(2, 432)
            dg = lay.take(T1)
            lay_x = rst2
            lay2 = Layout(act[:, :, :].rearrange("p a b -> p (a b)"), at=16 * T1)
            X = [sg[:, 0:2, :]]
            SS = [lay2.take(T1), lay2.take(T1)]
            PP = [sg[:, 0, :], sg[:, 1, :]]
            PT = [lay2.take(384), lay2.take(384)]
            og = gr
            sma, smb = act[:, 0:8, :], act[:, 8:16, :]
            w_in = IN["w_in"][L]
            gain = lambda g: (lambda k: gcur[:, 8 * g + k:8 * g + k + 1])

            xt = prenorm(gain(2), cols1)
            PE.wait(*xt)
            tz = [po("memset", [], qa, 0.0), po("memset", [], ka, 0.0), po("memset", [], qz, 0.0),
                  po("memset", [], kz, 0.0), po("memset", [], dg, 0.0)]
            tzx = po("memset", [], X[0], 0.0)
            zeroed = PO.now()
            tk = {}
            sc = small

            def load(name, a, w):
                return ring.load(columns(w_in, w_in_at[name] + a, w))

            def main_a():
                w, lt = load("ga", 0, GATE_RANK)
                PE.wait(lt)
                b, t = project(w, xn, cols1, 0, GATE_RANK, True)
                tga = taken[b] = ve("copy", [t], lay_x[0:GATE_RANK, :], bank[b][0:GATE_RANK, 0:T1])
                for c in range(2):
                    w, lt = load("gq", c * P, P)
                    PE.wait(lt)
                    b, t = project(w, xn, cols1, 0, P, True)
                    tk["gq", c] = taken[b] = ac([t], gq[:, c, :], bank[b][:, 0:T1], ACT.Copy, scale=GLA_DK ** -0.5)
                PE.wait(tga)
                for c in range(2):
                    b = next_bank()
                    t = PE.tick(mm(bank[b][:, 0:T1], wau[:, c * P:c * P + P], lay_x[0:GATE_RANK, :], True, True))
                    t = taken[b] = ve("ts", [t], cb[:, c, :], bank[b][:, 0:T1], gcur[:, 48 + c:49 + c], None, ALU.add)
                    t = log_sigmoid(cb[:, c, :], cb[:, c, :], rst[:, :], [t])
                    t = ve("ts", [t], cb[:, c, :], cb[:, c, :], 1.0 / 16.0, None, ALU.mult)
                    tk["cb", c] = ve("scan", [t], cb[:, c, :], C("ones"), cb[:, c, :], 0.0, ALU.mult, ALU.add)
                w, lt = load("gk", 0, 256)
                PE.wait(lt)
                for c in range(2):
                    b, t = project(w, xn, cols1, c * P, P, c == 1)
                    tk["gk", c] = taken[b] = ac([t], gk[:, c, :], bank[b][:, 0:T1], ACT.Copy)
                    yield
                w, lt = load("ff", 0, FOX_HEADS)
                PE.wait(lt)
                b, t = project(w, xn, cols1, 0, FOX_HEADS, True)
                H8 = slice(0, FOX_HEADS)
                cum, ncum = of[H8, 0, :], of[H8, 1, :]
                t = taken[b] = ve("ts", [t], cum, bank[b][H8, 0:T1], sc[H8, 0:1], None, ALU.add)
                t = log_sigmoid(cum, cum, ncum, [t])
                t = ve("scan", [t], cum, C("ones")[H8, :], cum, 0.0, ALU.mult, ALU.add)
                tk["cum"] = ve("ts", [t], ncum, cum, -1.0, None, ALU.mult)
                yield
                for name, dst, scale in (("fq", qa, HD ** -0.5), ("fk", ka, 1.0)):
                    for s in range(4 if name == "fq" else 2):
                        wd = 128 if name == "fq" else 256
                        w, lt = load(name, s * wd, wd)
                        PE.wait(lt)
                        for c in range(wd // P):
                            b, t = project(w, xn, cols1, c * P, P, c == wd // P - 1)
                            h = 2 * (s * wd // P + c)
                            ta = ac([t, zeroed], dst[0:64, h, :], bank[b][0:64, 0:T1], ACT.Copy, scale=scale)
                            taken[b] = ta = ac([t], dst[64:128, h + 1, :], bank[b][64:128, 0:T1], ACT.Copy, scale=scale)
                            tk[name, h] = ta
                            yield
                one = C("ones")[0:1, :]
                for h in range(FOX_HEADS):
                    r = 64 if h % 2 == 0 else 0
                    for dst, row, src in ((qa, r, of[h:h + 1, 0, :]), (qa, r + 1, one), (ka, r, one), (ka, r + 1, of[h:h + 1, 1, :])):
                        par_load(dst[row:row + 1, h, :], src, [tk["cum"], zeroed])
                tk["aug"] = par_all()
                for name, dst in (("fv", fv), ("gv", gv)):
                    pieces = [load(name, s * 256, 256) for s in range(2)]
                    for i, (c0, n) in enumerate(TOK_TILES1):
                        b = next_bank()
                        for s, (w, lt) in enumerate(pieces):
                            PE.wait(lt)
                            for k in range(KD):
                                m = mm(bank[b][0:n, s * 256:s * 256 + 256], xn[:, k, c0:c0 + n], w[:, k, :], k == 0, k == KD - 1)
                            if i == 2:
                                t = ring.release(m)
                        if i < 2:
                            t = PE.tick(m)
                        tk[name, i] = taken[b] = ac([t], dst[0:n, i, :], bank[b][0:n, :], ACT.Copy)
                        yield

            def main_b():
                for s in range(2):
                    w, lt = load("gr", s * 256, 256)
                    PE.wait(lt)
                    for c in range(2):
                        i = 2 * s + c
                        b, t = project(w, xn, cols1, c * P, P, c == 1)
                        t1 = ac([t], rst2[:, 0:T1], bank[b][:, 0:T1], ACT.Exp, scale=-1.0)
                        t1 = ve("ts", [t1], rst2[:, 0:T1], rst2[:, 0:T1], 1.0, None, ALU.add)
                        t1 = ve("recip", [t1], rst2[:, 0:T1], rst2[:, 0:T1])
                        tk["gr", i] = taken[b] = ve("tt", [t1], gr[:, i, :], bank[b][:, 0:T1], rst2[:, 0:T1], ALU.mult)
                        AC.wait(taken[b])
                        yield
                for name, dst in (("ma", sma), ("mb", smb)):
                    widths = [256] * 4
                    for s, wd in enumerate(widths):
                        w, lt = load(name, s * 256, wd)
                        PE.wait(lt)
                        for c in range(wd // P):
                            i = (s * 256) // P + c
                            b, t = project(w, xn, cols1, c * P, P, c == wd // P - 1)
                            t = taken[b] = ac([t], dst[:, i, :], bank[b][:, 0:T1], ACT.Exp, scale=-1.0)
                            t = ve("ts", [t], dst[:, i, :], dst[:, i, :], 1.0, None, ALU.add)
                            tk[name, i] = ve("recip", [t], dst[:, i, :], dst[:, i, :])
                            yield

            def gla_diag():
                sub = lambda a: a.rearrange("p c (i j) -> p c i j", j=SUB)
                x = X[0]
                ready = [tk["gq", 0], tk["gq", 1], tk["gk", 0], tk["gk", 1], tk["cb", 0], tk["cb", 1], tzx]
                read = None
                for j in reversed(range(SUB)):
                    n = SUB - j
                    for c in range(2):
                        s3 = lambda a: a[:, c, :].rearrange("p (i j) -> p i j", j=SUB)
                        xs_ = s3(x)[:, :, j:SUB]
                        at_s = lambda a: s3(a)[:, :, j:j + 1].broadcast_to([P, N_SUB, n])
                        t = ve("tt", ready + [read], xs_, s3(cb)[:, :, j:SUB], at_s(cb), ALU.subtract)
                        t = ac([t], xs_, xs_, ACT.Exp)
                        t = ve("tt", [t], xs_, xs_, s3(gq)[:, :, j:SUB], ALU.mult)
                        t = ve("tt", [t], xs_, xs_, at_s(gk), ALU.mult)
                        PE.wait(t, taken[7])
                        pick = C("pickd")[:, 80 * c + 15 - j:80 * c + 15 - j + 64]
                        m = mm(bank[7][0:64, 0:T1], pick, x[:, c, :], j == SUB - 1 and c == 0, j == 0 and c == 1)
                        rd = PE.tick(m)
                        read_c[c] = rd
                    read = rd
                    yield
                tk["dg"] = taken[7] = ve("tt", [read, zeroed], dg[0:64, :], bank[7][0:64, 0:T1], C("dmask")[0:64, :], ALU.mult)
                for h in range(GLA_HEADS):
                    c, r = h // 2, slice(64 * (h % 2), 64 * (h % 2) + 64)
                    v3 = lambda a: a.rearrange("p (i j) -> p i j", j=SUB)
                    dst = qz[r, h, SUB:T1]
                    ref = cb[r, c, SUB - 1:T1 - 1:SUB].unsqueeze(2).broadcast_to([64, N_SUB - 1, SUB])
                    t = ve("tt", [zeroed], v3(dst), v3(cb[r, c, SUB:T1]), ref, ALU.subtract)
                    t = ac([t], dst, dst, ACT.Exp)
                    tk["qz", h] = ve("tt", [t], dst, dst, gq[r, c, SUB:T1], ALU.mult)
                yield

            def gla_heads():
                z = 0
                kz_read = [None, None]
                at_free = [None, None]
                for c in range(2):
                    if c == 1:
                        for zz in range(2):
                            kz_read[zz] = po("memset", [PE.now()], kz[:, zz, :], 0.0)
                    PE.wait(*[taken[b] for b in (2, 3, 4, 5)])
                    for i in range(N_SUB):
                        z = i % 2
                        t0 = SUB * i
                        if i > 0:
                            ref = cb[:, c, t0 - 1:t0]
                            t = ac([kz_read[z], zeroed], kz[:, z, 0:t0], cb[:, c, 0:t0], ACT.Exp, scale=-1.0, bias=ref)
                            t = ve("tt", [t], kz[:, z, 0:t0], kz[:, z, 0:t0], gk[:, c, 0:t0], ALU.mult)
                            PE.wait(t)
                        PE.wait(tk["dg"], tk["qz", 2 * c], tk["qz", 2 * c + 1])
                        for hh in range(2):
                            h = 2 * c + hh
                            for st in range(i // 8 + 1):
                                M = TOK_TILES1[st][1]
                                b = 2 + 2 * hh + (st > 0)
                                o = bank[b][0:M, t0:t0 + SUB] if st == 0 else bank[b][0:M, t0 - P:t0 - P + SUB] \
                                    if st == 1 else bank[b][0:M, 144:144 + SUB]
                                diag = st == i // 8
                                off = P * st < t0
                                if off:
                                    m = mm(o, kz[:, z, P * st:P * st + M], qz[:, h, t0:t0 + SUB], True, not diag)
                                if diag:
                                    a = 240 * h + 112 - 16 * (i % 8)
                                    m = mm(o, C("spread")[:, a:a + M], dg[:, t0:t0 + SUB], not off, True)
                        kz_read[z] = tpe = PE.tick(m)
                        if i % 2 == 1:
                            yield
                    for hh in range(2):
                        h = 2 * c + hh
                        b0, b1 = 2 + 2 * hh, 3 + 2 * hh
                        t = ac([tpe, at_free[hh]], AT[:, hh, 0:T1], bank[b0][:, 0:T1], ACT.Copy)
                        taken[b0] = t
                        ac([], AT[:, hh, T1:T1 + 144], bank[b1][:, 0:144], ACT.Copy)
                        t = taken[b1] = ac([], AT[0:16, hh, 416:432], bank[b1][0:16, 144:160], ACT.Copy)
                        PE.wait(t, taken[6], tk["gv", 0], tk["gv", 1], tk["gv", 2])
                        mm(bank[6][:, 0:T1], gv[:, 0, h * P:h * P + P], AT[:, hh, 0:T1], True, False)
                        mm(bank[6][:, P:T1], gv[:, 1, h * P:h * P + P], AT[:, hh, T1:T1 + 144], False, False)
                        m = mm(bank[6][:, 256:T1], gv[0:16, 2, h * P:h * P + P], AT[0:16, hh, 416:432], False, True)
                        t = PE.tick(m)
                        at_free[hh] = t
                        o = X[0][:, 0, :]
                        s = X[0][:, 1, :]
                        t1 = ac([t, o_free[0]], s, bank[6][:, 0:T1], ACT.Square)
                        t2 = taken[6] = ve("copy", [t, o_free[0], t1], o, bank[6][:, 0:T1])
                        PE.wait(t1, taken[7])
                        t = PE.tick(mm(bank[7][:, 0:T1], C("mean128"), s, True, True))
                        t = taken[7] = rsqrt(s, bank[7][:, 0:T1], [t])
                        t = ve("stt", [t, t2], o, o, gcur[:, 50 + h:51 + h], s, ALU.mult, ALU.mult)
                        if ("gr", h) in tk:
                            t = tk["og", h] = ve("tt", [t, tk["gr", h]], og[:, h, :], o, gr[:, h, :], ALU.mult)
                        else:
                            raise AssertionError("gate later than its head")
                        o_free[0] = t
                        yield

            o_free = [None]
            read_c = [None, None]

            def fox():
                units = []
                of_tok = {}

                def opener(pair, first):
                    def go():
                        if first:
                            PE.wait(taken[6 + pair % 2])
                    return go

                def closer(pair, last):
                    def go(t):
                        if last:
                            b = 6 + pair % 2
                            tk["of", pair] = taken[b] = ac([t], of[:, pair, :], bank[b][:, 0:T1], ACT.Copy)
                    return go

                for pair in range(4):
                    for i, (t0, n) in enumerate(TOK_TILES1):
                        for hh in range(2):
                            h = 2 * pair + hh
                            W = t0 + n
                            rows = slice(64 * hh, 64 * hh + 64)
                            units.append(dict(
                                n=n, W=W, need=[tk["aug"], tk["fq", 2 * pair], tk["fk", 2 * pair]],
                                qk=[(qa[:, h, t0:t0 + n], ka[:, h, 0:W], W, 0)],
                                mask=C("causal")[0:n, 256 - t0:256 - t0 + W],
                                turn=[(s0, ns, st) for st, (s0, ns) in enumerate(TOK_TILES1[:i + 1])],
                                open=opener(pair, i == 0 and hh == 0), close=closer(pair, i == 2 and hh == 1),
                                pv=[(bank[6 + pair % 2][rows, t0:t0 + n],
                                     [(st, ns, fv[0:ns, st, h * HD:h * HD + HD]) for st, (s0, ns) in enumerate(TOK_TILES1[:i + 1])])]))
                PE.wait(tk["fv", 2], taken[2], taken[3], taken[4], taken[5])
                yield from attention(units, (SS, PP, PT, small[:, 8:16]), (bank[2], bank[3]), (bank[4], bank[5]))
                for b in (2, 3, 4, 5):
                    taken[b] = None
                PE.wait(VE.now(), AC.now())

            drive(main_a(), [lazy(gla_diag, tk, ("gk", 1))])
            drive(main_b(), [fox(), gla_heads()])
            PE.wait(VE.now(), AC.now())
            wf = [ring.load(IN["w_fox_o"][L].rearrange("(k p) n -> p k n", p=P)[:, :, s * 512:s * 512 + 512]) for s in range(2)]
            wg = [ring.load(IN["w_gla_o"][L].rearrange("(k p) n -> p k n", p=P)[:, :, s * 512:s * 512 + 512]) for s in range(2)]
            yt = []
            f_free = [None, None]
            for d in range(KD):
                bf, bg = 2 + d % 2, 4 + d % 2
                (w, lt), (w2, lt2) = wf[d // 4], wg[d // 4]
                PE.wait(lt, f_free[d % 2])
                c = (d % 4) * P
                for k in range(4):
                    m = mm(bank[bf][:, 0:T1], w[:, k, c:c + P], of[:, k, :], k == 0, k == 3)
                ta = PE.tick(m)
                PE.wait(lt2)
                for k in range(4):
                    m = mm(bank[bg][:, 0:T1], w2[:, k, c:c + P], og[:, k, :], k == 0, k == 3)
                tb = PE.tick(m)
                t1 = ve("tt", [ta, tk["ma", d]], xn[:, d, :], bank[bf][:, 0:T1], sma[:, d, :], ALU.mult)
                t2 = ve("tt", [tb, tk["mb", d]], smb[:, d, :], bank[bg][:, 0:T1], smb[:, d, :], ALU.mult)
                f_free[d % 2] = t2
                yt.append(ve("tt", [t2, t1], xn[:, d, :], xn[:, d, :], smb[:, d, :], ALU.add))
            free_all(4, tb)
            PE.wait(*yt)
            done = []
            for s in range(4):
                w, lt = ring.load(columns(IN["w_out"][L], s * 256, 256))
                PE.wait(lt)
                for c in range(2):
                    d = 2 * s + c
                    for k in range(KD):
                        m = mm(bank[d][:, 0:T1], w[:, k, c * P:c * P + P], xn[:, k, :], k == 0, k == KD - 1)
                    done.append(ring.release(m) if c == 1 else PE.tick(m))
            postnorm(done, gain(3), 1.0, cols1)

        def lazy(gen, tk, key):
            while key not in tk:
                yield
            yield from gen()



        join()
        for ln in lanes:
            ln.seen = {}
        entry = {ln: ln.n for ln in lanes}
        r0 = ring.n
        p0 = par_n[0]
        PAR_LAYER = 16 * (2 + 4 * FOX_HEADS)
        with nc.Fori(0, DEPTH) as L:
            for ln in lanes:
                ln.loop = L * PER_LAYER
            ring.loop = L * LOADS
            ring.loop16 = L * (16 * LOADS // RING)
            par_n[1] = L * PAR_LAYER
            gu_layer[0] = L * (16 * 4)
            for ln in lanes:
                ln.wait(*[o.at(entry[o]) for o in lanes if o is not ln])
            for k in range(KD):
                h_tok[k] = VE.at(entry[VE])
            for b in range(8):
                taken[b] = None
            par_load(wau[:, :], IN["w_alpha_up"][L])
            par_load(small[0:FOX_HEADS, 0:1], IN["b_f"][L].rearrange("(p a) -> p a", a=1), slow=True)
            ve("copy", [], gcur[:, 0:48].rearrange("p (g k) -> p g k", g=6),
               gain1[:, 0:96].rearrange("p (g l k) -> p l g k", g=6, l=2)[:, L])
            ve("copy", [], gcur[:, 48:50], gain1[:, 96:100].rearrange("p (l k) -> p l k", l=2)[:, L])
            ve("copy", [], gcur[:, 50:54], gain1[:, 100:108].rearrange("p (l k) -> p l k", l=2)[:, L])
            PE.wait(par_all())
            VE.wait(par_all(), VE.now())
            g = lambda i: (lambda k: gcur[:, 8 * i + k:8 * i + k + 1])

            def gu1(name):
                w = IN[name][L].rearrange("(k p) n -> p k n", p=P)
                return lambda half, j: (w[:, :, bass.ds(half * (HALF * P) + j * P, P)],
                                        w[:, :, bass.ds(half * (HALF * P) + (D_FF + j * P), P)])

            def dn(w):
                w = w.rearrange("(m r p) n -> m p r n", p=P, r=2)
                return lambda m2: w[m2]

            ffn(gu1("w_ffn1_gu"), dn(IN["w_ffn1_down"][L]), g(0), cols1, g(1))
            join()
            mixer1(L)
            join()
            ffn(gu1("w_ffn2_gu"), dn(IN["w_ffn2_down"][L]), g(4), cols1, g(5))
            join()
            for ln in lanes:
                spent = ln.n - entry[ln]
                assert 0 < spent < PER_LAYER, spent
                ln.eng.wait_ge(ln.sem, ln.loop + ln.n)
                ln.eng.sem_inc(ln.sem, PER_LAYER - spent)
                ln.open = False
            assert ring.n - r0 == LOADS, ring.n - r0
            assert par_n[0] - p0 == PAR_LAYER
            assert gu_total[0] == 4
        for ln in lanes:
            ln.n, ln.loop, ln.seen = entry[ln] + DEPTH * PER_LAYER, 0, {}
        ring.n, ring.freed = r0 + DEPTH * LOADS, ring.freed + LOADS
        ring.loop = ring.loop16 = 0
        par_n[0], par_n[1] = p0 + DEPTH * PAR_LAYER, 0
        gu_total[0], gu_layer[0] = 4 * DEPTH, 0
        join()
        for ln in lanes:
            ln.wait(*[o.now() for o in lanes if o is not ln])
        for k in range(KD):
            h_tok[k] = None

        cols2 = (N_META, T1)
        T = SEQ
        keep = Layout(arena)
        memR = keep.take(KD, T)
        k_sh = keep.take(6, T)
        v_sh = keep.take(2, DIL_W)
        kept = keep.at
        ms = act[:, 0:8, :].rearrange("p a b -> p (a b)")[:, 0:2 * D].rearrange("p (t d) -> p t d", t=2)
        par_load(ms, IN["mem_2"][0].rearrange("(t p) d -> p t d", p=P))
        PE.wait(par_all())
        saved = list(h_tok)
        turn_rows(ms, P, 0, memR, 0)
        turn_rows(ms, P, 1, memR, P)
        mt = list(h_tok)
        for k in range(KD):
            h_tok[k] = saved[k]
        AC.wait(PE.now())
        t = rms_of(memR, mt, C("mean1024"), 0, (0, T))
        for k in range(KD):
            ve("tt", [t], memR[:, k, :], memR[:, k, :], rst[:, 0:T], ALU.mult)
        join()

        def gcol2(i):
            return lambda k: gain2[:, 8 * i + k:8 * i + k + 1]

        def gu2(pre, l):
            wg = IN[pre + "_w_gate_2"][l].rearrange("(k p) n -> p k n", p=P)
            wu = IN[pre + "_w_up_2"][l].rearrange("(k p) n -> p k n", p=P)
            return lambda half, j: (wg[:, :, bass.ds(half * (HALF * P) + j * P, P)],
                                    wu[:, :, bass.ds(half * (HALF * P) + j * P, P)])

        def ffn2(pre, l, gi):
            ffn(gu2(pre, l), dn(IN[pre + "_w_down_2"][l]), gcol2(gi), cols2, None)

        def headnorm_steps(items, zb=(sg[:, 0, 0:SEQ], sg[:, 1, 0:SEQ])):
            sqb = [rst[:, 0:T], rst2[:, 0:T]]
            pend = None
            out_free = [None, None]
            toks = []
            for i, (make, gaincol, dst) in enumerate(list(items) + [(None, None, None)]):
                new = None
                if make is not None:
                    z = i % 2
                    b, t = make()
                    t1 = ac([t, out_free[z]], sqb[z], bank[b][:, 0:T], ACT.Square)
                    t2 = taken[b] = ve("copy", [t, out_free[z], t1], zb[z], bank[b][:, 0:T])
                    new = (z, t1, t2, gaincol, dst)
                if pend is not None:
                    z, t1, t2, gc, dst = pend
                    PE.wait(t1, taken[7])
                    t = PE.tick(mm(bank[7][:, 0:T], C("mean64"), sqb[z], True, True))
                    t = taken[7] = rsqrt(sqb[z], bank[7][:, 0:T], [t])
                    out_free[z] = t = ve("stt", [t, t2], dst, zb[z], gc, sqb[z], ALU.mult, ALU.mult)
                    toks.append(t)
                pend = new
                yield

        def memory_kv(l, memn, kmem, vmem, **bufs):
            for k in range(KD):
                t = ve("ts", [], memn[:, k, :], memR[:, k, :], gain2[:, 48 + 8 * l + k:49 + 8 * l + k], None, ALU.mult)
            w, lt = ring.load(columns(IN["w_mem_kv_2"][l], 0, 256))
            PE.wait(t, lt)
            mk = lambda c: (lambda: project(w, memn, (0, T), c * P, P, c == 1))
            yield from headnorm_steps([(mk(c), gain2[:, 74 + l:75 + l], kmem[:, c, :]) for c in range(2)], **bufs)
            w, lt = ring.load(columns(IN["w_mem_kv_2"][l], 256, 256))
            PE.wait(lt)
            for i, (c0, n) in enumerate(TOK_TILES2):
                b, t = project_rows(w, memn, c0, n, 256, i == 1)
                taken[b] = ac([t], vmem[:, i, :], bank[b][:, 0:256], ACT.Copy)
                yield

        def memory_units(qmem, kmem, vmem, hm, tk_out):
            units = []

            def opener(pair, first):
                def go():
                    if first:
                        PE.wait(taken[6])
                return go

            def closer(pair, last):
                def go(t):
                    if last:
                        tk_out[pair] = taken[6] = ac([t], hm[:, pair, :], bank[6][:, 0:T], ACT.Copy)
                return go

            for pair in range(2):
                for i, (t0, n) in enumerate(TOK_TILES2):
                    for hh in range(2):
                        h = 2 * pair + hh
                        rows = slice(64 * hh, 64 * hh + 64)
                        units.append(dict(
                            n=n, W=T, need=[], qk=[(qmem[rows, pair, t0:t0 + n], kmem[rows, pair, :], T, 0)], mask=None,
                            turn=[(0, P, 0), (P, P, 1)], open=opener(pair, i == 0 and hh == 0),
                            close=closer(pair, i == 1 and hh == 1),
                            pv=[(bank[6][rows, t0:t0 + n], [(st, P, vmem[:, st, h * HD:h * HD + HD]) for st in range(2)])]))
            return units

        def out_proj(loads, rhs_of, hold=0):
            for s in range(4):
                w, lt = loads(s)
                PE.wait(lt)
                for c in range(2):
                    d = 2 * s + c
                    b = next_bank()
                    terms = rhs_of(w, c * P, d)
                    for x, (a, r) in enumerate(terms):
                        m = mm(bank[b][:, 0:T], a, r, x == 0, x == len(terms) - 1)
                    t = ring.release(m) if c == 1 and not hold else PE.tick(m)
                    h_tok[d] = taken[b] = ve("tt", [t], hT[:, d, N_META:T1], bank[b][:, 0:T], hT[:, d, N_META:T1], ALU.add)
            if hold:
                free_all(hold, t)

        def mixer2a():
            lay = Layout(arena, at=kept - 6 * T - 2 * DIL_W)
            qk = lay.take(16, T)
            v = lay.take(2, ML_W)
            og = lay.take(8, T)
            kmem, qmem, hm = lay.take(2, T), lay.take(2, T), lay.take(2, T)
            vmem = lay.take(2, 256)
            xb = [lay.take(T + 4), lay.take(T + 4)]
            rowg = lay.take(4, T)
            scr = Layout(act[:, :, :].rearrange("p a b -> p (a b)"), at=8 * T1)
            memn = scr.take(KD, T)
            WT = [[scr.take(T), scr.take(T)] for _ in range(2)]
            tmp = lay.take(3, T)
            w_in = IN["a_w_in_2"][0]
            R = slice(0, MH)
            xt = prenorm(gcol2(4), cols2)
            PE.wait(*xt)
            tz = [po("memset", [], xb[z][0:MH, 0:3], 0.0) for z in range(2)]
            par_load(small[0:4, 0:2], IN["a_gate_bias_2"][0].rearrange("(a p) -> p a", p=4), slow=True)
            tk = {}
            H4 = slice(0, ML_HEADS)

            def main():
                w, lt = ring.load(columns(w_in, 4 * ML_W, 2 * ML_HEADS))
                PE.wait(lt)
                VE.wait(par_all())
                for g in range(2):
                    b, t = project(w, xn, cols2, 4 * g, 4, g == 1)
                    tk["g", g] = taken[b] = ve("ts", [t], rowg[H4, g, :], bank[b][H4, 0:T], small[H4, g:g + 1], None, ALU.add)
                ci, cf, mu, em = (rowg[H4, x, :] for x in range(4))
                t = log_sigmoid(cf, cf, mu, [tk["g", 1]])
                t = ve("scan", [t], cf, C("ones")[H4, 0:T], cf, 0.0, ALU.mult, ALU.add)
                t = ve("tt", [t, tk["g", 0]], ci, ci, cf, ALU.subtract)
                t = ve("scan", [t], mu, C("ones")[H4, 0:T], ci, 0.0, ALU.mult, ALU.max)
                t = ve("tt", [t], em, cf, mu, ALU.add)
                tk["em"] = ac([t], em, em, ACT.Exp, scale=-1.0)
                tk["mu"] = ve("ts", [t], mu, mu, -1.0, None, ALU.mult)
                yield
                prev = [None, None]
                for s in range(8):
                    w, lt = ring.load(columns(w_in, s * ML_DK, ML_DK))
                    PE.wait(lt)
                    for c in range(2):
                        i = 2 * s + c
                        z = i % 2
                        b, t = project(w, xn, cols2, c * MH, MH, c == 1)
                        t = taken[b] = ac([t, tz[z], prev[z]], xb[z][R, 3:3 + T], bank[b][R, 0:T], ACT.Copy)
                        tap = lambda j: gain3[:, 8 + 16 * j + i:9 + 16 * j + i]
                        y = qk[R, i, :]
                        t = ve("ts", [t], y, xb[z][R, 0:T], tap(0), None, ALU.mult)
                        for j in range(1, 4):
                            t = ve("stt", [t], y, xb[z][R, j:j + T], tap(j), y, ALU.mult, ALU.add)
                        e = tmp[R, z, :]
                        t = ac([t, VE.now()], e, y, ACT.Exp, scale=-1.0)
                        t = ve("ts", [t], e, e, 1.0, None, ALU.add)
                        t = ve("recip", [t], e, e)
                        prev[z] = tk["qk", i] = ve("tt", [t], y, y, e, ALU.mult)
                        yield
                for s in range(3):
                    w, lt = ring.load(columns(w_in, 2 * ML_W + s * 256, 256))
                    PE.wait(lt)
                    for i, (c0, n) in enumerate(TOK_TILES2):
                        b, t = project_rows(w, xn, N_META + c0, n, 256, i == 1)
                        tk["v"] = taken[b] = ac([t], v[:, i, s * 256:s * 256 + 256], bank[b][:, 0:256], ACT.Copy)
                        yield
                for s in range(4):
                    w, lt = ring.load(columns(w_in, 3 * ML_W + s * ML_DK, ML_DK))
                    PE.wait(lt)
                    for c in range(2):
                        i = 2 * s + c
                        b, t = project(w, xn, cols2, c * MH, MH, c == 1)
                        t = taken[b] = ac([t], og[R, i, :], bank[b][R, 0:T], ACT.Exp, scale=-1.0)
                        t = ve("ts", [t], og[R, i, :], og[R, i, :], 1.0, None, ALU.add)
                        tk["o", i] = ve("recip", [t], og[R, i, :], og[R, i, :])
                        yield
                w, lt = ring.load(columns(w_in, 4 * ML_W + 2 * ML_HEADS, MEM_W))
                PE.wait(lt)
                mk = lambda c: (lambda: project(w, xn, cols2, c * P, P, c == 1))
                z2 = (xb[0][:, 0:T], xb[1][:, 0:T])
                yield from headnorm_steps([(mk(c), gain2[:, 72:73], qmem[:, c, :]) for c in range(2)], zb=z2)
                yield from memory_kv(0, memn, kmem, vmem, zb=z2)
                tk["mem"] = True

            def cells():
                for _ in range(24):
                    yield
                PE.wait(tk["mu"], taken[6])
                for i, (c0, n) in enumerate(TOK_TILES2):
                    m = nc.tensor.transpose(bank[6][:, 4 * i:4 * i + 4], rowg[H4, 0, c0:c0 + n], ident[0:4, 0:4])
                t = PE.tick(m)
                tcs = taken[6] = ve("copy", [t], small[:, 16:24], bank[6][:, 0:8])
                wt_free = [None, None]
                for h in range(ML_HEADS):
                    z = h % 2
                    sel = C("sel")[H4, h * P:h * P + P]
                    PE.wait(tk["em"], tk["mu"], taken[2])
                    t = PE.tick(mm(bank[2][:, 0:T], sel, rowg[H4, 2, :], True, True))
                    for s, (s0, n) in enumerate(TOK_TILES2):
                        wv = WT[z][s][:, s0:T]
                        t1 = taken[2] = ve("stt", [t, tcs, wt_free[z]], wv, bank[2][:, s0:T], small[:, 16 + 4 * s + h:17 + 4 * s + h],
                                           C("causalT")[:, 0:T - s0], ALU.add, ALU.min)
                        t1 = ac([t1], wv, wv, ACT.Exp)
                        PE.wait(taken[3], tk["qk", 2 * h + 1], tk["qk", 8 + 2 * h + 1])
                        for c in range(2):
                            m = mm(bank[3][:, s0:T], qk[R, 8 + 2 * h + c, s0:s0 + n], qk[R, 2 * h + c, s0:T], c == 0, c == 1)
                        tp = PE.tick(m)
                        taken[3] = tw = ve("stt", [t1, tp], wv, wv, ML_DK ** -0.5, bank[3][:, s0:T], ALU.mult, ALU.mult)
                        PE.wait(tw)
                    yield
                    PE.wait(tk["v"], taken[4], taken[5], taken[7])
                    def sums(o, lhs):
                        mm(o[R, 0:T], lhs(0), WT[z][0][:, 0:T], True, False)
                        return mm(o[R, P:T], lhs(1), WT[z][1][:, P:T], False, True)
                    sums(bank[4], lambda s: v[:, s, h * ML_DK:h * ML_DK + MH])
                    sums(bank[5], lambda s: v[:, s, h * ML_DK + MH:h * ML_DK + ML_DK])
                    m = sums(bank[7], lambda s: C("ones")[:, 0:MH])
                    tn = PE.tick(m)
                    wt_free[z] = tn
                    PE.wait(taken[6])
                    t = PE.tick(mm(bank[6][R, 0:T], sel[:, 0:MH], rowg[H4, 3, :], True, True))
                    den = tmp[R, 2, :]
                    t = taken[6] = ac([t, VE.now()], den, bank[6][R, 0:T], ACT.Copy)
                    t = taken[7] = ac([tn], tmp[R, 0, :], bank[7][R, 0:T], ACT.Abs)
                    t = ve("tt", [t], den, den, tmp[R, 0, :], ALU.max)
                    t = ve("recip", [t], den, den)
                    cell = [sg[R, 0, 0:T], sg[R, 1, 0:T]]
                    taken[4] = ve("tt", [t, c_free[0]], cell[0], bank[4][R, 0:T], den, ALU.mult)
                    taken[5] = tc = ve("tt", [t], cell[1], bank[5][R, 0:T], den, ALU.mult)
                    sq = [WT[z][0][R, 0:T], WT[z][1][R, 0:T]]
                    for c in range(2):
                        t = ac([tc, tn], sq[c], cell[c], ACT.Square)
                        PE.wait(t, taken[6])
                        m = mm(bank[6][R, 0:T], C("mean192")[R, 0:MH], sq[c], c == 0, c == 1)
                    wt_free[z] = t = PE.tick(m)
                    t = taken[6] = rsqrt(den, bank[6][R, 0:T], [t])
                    for c in range(2):
                        i = 2 * h + c
                        while ("o", i) not in tk:
                            yield
                        t1 = ve("stt", [t, tc], cell[c], cell[c], gain3[:, i:i + 1], den, ALU.mult, ALU.mult)
                        c_free[0] = tk["cell", i] = ve("tt", [t1, tk["o", i]], og[R, i, :], og[R, i, :], cell[c], ALU.mult)
                    yield

            c_free = [None]
            drive(main(), [cells()])
            hmt = {}
            bufs = ([WT[0][0], WT[0][1]], [WT[1][0], WT[1][1]], [xb[0][:, 0:T], xb[1][:, 0:T]], small[:, 8:16])
            join()
            for _ in attention(memory_units(qmem, kmem, vmem, hm, hmt), bufs, (bank[2], bank[3]), (bank[4], bank[5])):
                pass
            w_out = IN["a_w_out_2"][0]
            PE.wait(AC.now(), VE.now())
            wm, ltm = ring.load(w_out[ML_W:D, :].rearrange("(k p) n -> p k n", p=P))
            PE.wait(ltm)
            def loads(s):
                return ring.load(w_out[0:ML_W, s * 256:s * 256 + 256].rearrange("(k p) n -> p k n", p=MH), rows=MH)

            def terms(w, c, d):
                return [(w[:, k, c:c + P], og[R, k, :]) for k in range(8)] + \
                       [(wm[:, k, d * P:d * P + P], hm[:, k, :]) for k in range(2)]

            out_proj(loads, terms, hold=5)

        def shared_kv():
            w_kv = IN["w_kv_2"]
            xt = prenorm(lambda k: gain2[:, 64 + k:65 + k], cols2)
            PE.wait(*xt)

            def make(c):
                def go():
                    if c % 2 == 0:
                        cur[0], lt = ring.load(columns(w_kv, c * P, 256))
                        PE.wait(lt)
                    return project(cur[0], xn, cols2, (c % 2) * P, P, c % 2 == 1)
                return go

            cur = [None]
            for _ in headnorm_steps([(make(c), gain2[:, 77:78], k_sh[:, c, :]) for c in range(6)]):
                pass
            for s in range(3):
                w, lt = ring.load(columns(w_kv, DIL_W + s * 256, 256))
                PE.wait(lt)
                for i, (c0, n) in enumerate(TOK_TILES2):
                    b, t = project_rows(w, xn, N_META + c0, n, 256, i == 1)
                    taken[b] = ac([t], v_sh[:, i, s * 256:s * 256 + 256], bank[b][:, 0:256], ACT.Copy)

        bias_rows = IN["scratch"]

        def mixer2b():
            lay = Layout(arena, at=kept)
            q = lay.take(8, T)
            bias = lay.take(12, T)
            hd = lay.take(6, T)
            kmem, hm = lay.take(2, T), lay.take(2, T)
            vmem = lay.take(2, 256)
            scr = Layout(act[:, :, :].rearrange("p a b -> p (a b)"), at=8 * T1)
            memn = scr.take(KD, T)
            t2 = scr.take(1536)
            ohv = t2[0:BUCKETS + 1, :]
            tab = small[0:BUCKETS + 1, 32:44]
            xt = prenorm(gcol2(5), cols2)
            PE.wait(*xt)
            t = po("memset", [], small[:, 32:44], NEG)
            par_load(small[0:BUCKETS, 32:44], IN["rel_bias_2"], [t])
            par_load(ohv, IN["onehot"])
            PE.wait(par_all())
            tabb = rst2[0:BUCKETS + 1, 0:P]
            VE.wait(par_all())
            for h in range(12):
                g = h // 4
                b = next_bank()
                tt = ve("ts", [PE.now()], tabb, C("ones")[0:BUCKETS + 1, 0:P], small[0:BUCKETS + 1, 32 + h:33 + h], None, ALU.mult)
                PE.wait(tt)
                t = PE.tick(mm(bank[b][:, :], tabb, ohv[:, 512 * g:512 * g + 512], True, True))
                st = bias[:, 2 * (h % 6):2 * (h % 6) + 2, :].rearrange("p a b -> p (a b)")
                if h >= 6:
                    AC.wait((s_bias, 0, 16 * 6))
                taken[b] = ac([t], st, bank[b][:, :], ACT.Copy)
                nc.scalar.wait_ge(AC.sem, AC.n)
                nc.scalar.dma_start(bias_rows[h], st).then_inc(s_bias, 16)
            PO.wait((s_bias, 0, 16 * 12))
            for h in range(12):
                src = bias_rows[h].rearrange("p u -> (p u)")[0:P * 511].rearrange("(p u) -> p u", u=511)[:, 127:127 + T]
                par_load(bias[:, h, :], src)
            tk_bias = par_all()

            def make(c):
                def go():
                    if c % 2 == 0:
                        cur[0], lt = ring.load(columns(IN["b_w_q_2"][0], c * P, 256))
                        PE.wait(lt)
                    return project(cur[0], xn, cols2, (c % 2) * P, P, c % 2 == 1)
                return go

            cur = [None]
            items = [(make(c), gain2[:, 76:77] if c < 6 else gain2[:, 73:74], q[:, c, :]) for c in range(8)]
            for _ in headnorm_steps(items):
                pass
            for _ in memory_kv(1, memn, kmem, vmem):
                pass
            join()
            for b in range(8):
                taken[b] = None
            ab = Layout(act[:, :, :].rearrange("p a b -> p (a b)"), at=8 * T1)
            SS = [ab.take(3 * T), ab.take(3 * T)]
            PP = [ab.take(3 * T)] * 2
            PT = [xn[:, 0:3, :].rearrange("p a b -> p (a b)")[:, 0:768], xn[:, 3:6, :].rearrange("p a b -> p (a b)")[:, 0:768]]
            VE.wait(tk_bias)
            for hh_ in range(DIL_HEADS):
                for i, (t0, n) in enumerate(TOK_TILES2):
                    W = t0 + n
                    z = i
                    rows = slice(64 * (hh_ % 2), 64 * (hh_ % 2) + 64)
                    pair = hh_ // 2
                    PE.wait(AC.now(), VE.now())
                    for g in range(3):
                        m = mm(bank[g][0:n, 0:W], q[rows, 2 * g + pair, t0:t0 + n], k_sh[rows, 2 * g + pair, 0:W], True, True)
                    t = PE.tick(m)
                    for g in range(3):
                        tt = ve("tt", [t], SS[z][:, g * W:g * W + W], bank[g][:, 0:W], bias[:, 4 * g + hh_, T - W:T], ALU.add)
                    mx, nm, den, rd = (small[:, 8 + x:9 + x] for x in range(4))
                    t = ve("rmax", [tt], mx, SS[z][:, 0:3 * W], AX_X)
                    t = ve("ts", [t], nm, mx, -1.0, None, ALU.mult)
                    t = ac([t, PE.now()], PP[z][:, 0:3 * W], SS[z][:, 0:3 * W], ACT.Exp, bias=nm, accum_out=den)
                    t = ve("recip", [t], rd, den)
                    t = ve("ts", [t], PP[z][:, 0:3 * W], PP[z][:, 0:3 * W], rd, None, ALU.mult)
                    PE.wait(t)
                    ns = W // P
                    for s in range(3 * ns):
                        m = nc.tensor.transpose(bank[4 + s // 4][:, (s % 4) * P:(s % 4) * P + P], PP[z][:, s * P:s * P + P], ident)
                    t = PE.tick(m)
                    nt = 3 * ns
                    tc = ac([t], PT[z][:, 0:min(nt, 4) * P], bank[4][:, 0:min(nt, 4) * P], ACT.Copy)
                    if nt > 4:
                        tc = ac([], PT[z][:, 4 * P:nt * P], bank[5][:, 0:(nt - 4) * P], ACT.Copy)
                    PE.wait(tc, taken[6], taken[7], taken[3])
                    for g in range(3):
                        o = (bank[6], bank[7], bank[3])[g]
                        for s in range(ns):
                            m = mm(o[rows, t0:t0 + n], v_sh[:, s, (4 * g + hh_) * HD:(4 * g + hh_) * HD + HD],
                                   PT[z][:, (g * ns + s) * P:(g * ns + s) * P + P], s == 0, s == ns - 1)
                    t = PE.tick(m)
                    if hh_ % 2 == 1 and i == 1:
                        for g in range(3):
                            o = (bank[6], bank[7], bank[3])[g]
                            taken[(6, 7, 3)[g]] = ac([t], hd[:, 2 * g + pair, :], o[:, 0:T], ACT.Copy)
            join()
            for b in range(8):
                taken[b] = None
            hmt = {}
            bufs = ([SS[0], SS[1]], [PP[0][:, 0:T], PP[0][:, T:2 * T]], PT, small[:, 8:16])
            for _ in attention(memory_units(q[:, 6:8, :], kmem, vmem, hm, hmt), bufs, (bank[2], bank[3]), (bank[4], bank[5])):
                pass
            PE.wait(AC.now(), VE.now())
            out_proj(lambda s: ring.load(columns(IN["b_w_out_2"][0], s * 256, 256)),
                     lambda w, c, d: [(w[:, k, c:c + P], hd[:, k, :] if k < 6 else hm[:, k - 6, :]) for k in range(8)])

        ffn2("ffn1", 0, 0)
        join()
        mixer2a()
        join()
        ffn2("ffn2", 0, 2)
        join()
        shared_kv()
        join()
        ffn2("ffn1", 1, 1)
        join()
        mixer2b()
        join()
        ffn2("ffn2", 1, 3)

        join()
        ob = xn[:, :, :].rearrange("p a b -> p (a b)")
        for i in range(2):
            ov = (ob if i == 0 else act[:, :, :].rearrange("p a b -> p (a b)"))[:, 0:D]
            for k in range(KD):
                b = k % 4
                PE.wait(h_tok[k], taken[b] if i or k >= 4 else None)
                t = PE.tick(nc.tensor.transpose(bank[b][:, 0:P], hT[:, k, N_META + i * P:N_META + i * P + P], ident))
                taken[b] = ve("copy", [t], ov[:, k * P:k * P + P], bank[b][:, 0:P])
            nc.sync.wait_ge(VE.sem, VE.n)
            nc.sync.dma_start(out[0, i * P:i * P + P, :], ov).then_inc(s_out, 16)
        nc.sync.wait_ge(s_out, 32)


_SHAPE = (1, SEQ, D)


def kernel(**inputs):
    import numpy as _np
    import concourse.bacc as _bacc
    from concourse import mybir as _mybir
    from concourse.bass_utils import run_bass_kernel_spmd as _run

    nc = _bacc.Bacc("TRN2", target_bir_lowering=False, num_devices=1)
    arrays, args = {}, {}
    given = dict(inputs)
    given["consts"] = constants()
    given["onehot"] = bucket_rows()
    for name, value in given.items():
        a = _np.ascontiguousarray(value)
        arrays[f"in_{name}"] = a
        args[name] = nc.dram_tensor(f"in_{name}", a.shape, _mybir.dt.from_np(a.dtype), kind="ExternalInput").ap()
    args["scratch"] = nc.dram_tensor("bias_scratch", (12, P, 512), F32).ap()
    out = nc.dram_tensor("out_0", _SHAPE, F32, kind="ExternalOutput").ap()
    program(nc, args, out)
    r = _run(nc, [arrays], core_ids=[0])
    return r.results[0]["out_0"]
```

```python
import math
from contextlib import ExitStack

import numpy as np

import concourse.bass as bass
from concourse import mybir

F32 = mybir.dt.float32
F32R = mybir.dt.float32r
ALU = mybir.AluOpType
ACT = mybir.ActivationFunctionType
AX_X = mybir.AxisListType.X

P = 128
D = 1024
KD = D // P
SEQ = 256
N_META = 16
T1 = N_META + SEQ
DEPTH = 2
D_FF = 2816
NF = D_FF // P
EPS = 1e-6
NEG = -1e30
RING = 4
SLOT = 1024
LEAD = 2
TURNS = NF // 2
assert NF % 2 == 0 and RING == 4
UNITS_PER_LAYER = 192
UNITS = DEPTH * UNITS_PER_LAYER + 4 * 3 * NF + 49 + 12 + 20
assert UNITS_PER_LAYER % RING == 0

FOX_HEADS, HD = 8, 64
FOX_W = FOX_HEADS * HD
GLA_HEADS, GLA_DK, GLA_DV = 4, 64, 128
GLA_KW, GLA_W, GATE_RANK = GLA_HEADS * GLA_DK, GLA_HEADS * GLA_DV, 16
SUB = 16
N_SUB = T1 // SUB
SPLIT = (FOX_W, FOX_W, FOX_W, FOX_HEADS, GLA_KW, GLA_KW, GLA_W, GATE_RANK, GLA_W, D, D)
SPLIT_AT = [sum(SPLIT[:i]) for i in range(len(SPLIT))]

ML_HEADS, ML_DK = 4, 192
ML_W = ML_HEADS * ML_DK
MH = ML_DK // 2
MEM_W = 256
DIL_GROUPS = ((128, 1), (512, 4), (2048, 16))
DIL_HEADS = 4
DIL_W = 3 * DIL_HEADS * HD
BUCKETS, MAX_DIST = 32, 2048

TOK_TILES1 = [(0, 128), (128, 128), (256, 16)]
TOK_TILES2 = [(0, 128), (128, 128)]


CONST_W = [("ident", 128), ("mean1024", 128), ("mean128", 128), ("mean64", 128), ("mean192", 128), ("ones", T1),
           ("causal", 384), ("causalT", 256), ("pickd", 2 * 80), ("rep", GLA_HEADS * 128), ("blocks", 4 * 128),
           ("sel", 4 * 128)]
CONST_AT = {}
_at = 0
for _n, _w in CONST_W:
    CONST_AT[_n] = (_at, _w)
    _at += _w
CONST_N = _at


def constants():
    c = {n: np.zeros((P, w), np.float32) for n, w in CONST_W}
    p = np.arange(P)
    c["ident"][p, p] = 1.0
    c["mean1024"][:] = 1.0 / D
    c["mean128"][:] = 1.0 / GLA_DV
    c["mean64"][:] = (p[:, None] // HD == p[None, :] // HD) / HD
    c["mean192"][:] = 1.0 / ML_DK
    c["ones"][:] = 1.0
    c["causal"][:] = np.where(np.arange(384)[None, :] <= p[:, None] + 256, 0.0, NEG)
    c["causalT"][:] = np.where(np.arange(256)[None, :] >= p[:, None], 0.0, NEG)
    for ct in range(2):
        for half in range(2):
            c["pickd"][half * 64:half * 64 + 64, ct * 80 + 15 + 16 * (2 * ct + half)] = 1.0
    for h in range(GLA_HEADS):
        for j in range(SUB):
            c["rep"][16 * h + j, 128 * h + j:128 * h + 128:SUB] = 1.0
    t = np.arange(128)
    c["blocks"][:, 0:128] = p[:, None] // SUB == t[None, :] // SUB
    for l in range(1, 4):
        ps, pt = p[:, None] // (8 << l), t[None, :] // (8 << l)
        c["blocks"][:, 128 * l:128 * l + 128] = (pt % 2 == 1) & (ps == pt - 1)
    for h in range(4):
        c["sel"][h, 128 * h:128 * h + 128] = 1.0
    return np.ascontiguousarray(np.concatenate([c[n] for n, _ in CONST_W], axis=1))


def bucket_rows():
    oh = np.zeros((BUCKETS + 1, 3 * 512), np.float32)
    for g, (window, dil) in enumerate(DIL_GROUPS):
        for u in range(512):
            d = 255 - u
            if d < 0 or d % dil or d > window:
                b = BUCKETS
            elif d < BUCKETS // 2:
                b = d
            else:
                e = BUCKETS // 2
                b = min(e + int(math.log(d / e) / math.log(MAX_DIST / e) * (BUCKETS - e)), BUCKETS - 1)
            oh[b, 512 * g + u] = 1.0
    return oh


class Lane:

    def __init__(self, name, eng, sem, spare):
        self.name, self.eng, self.sem = name, eng, sem
        self.n = 0
        self.open = False
        self.spare = spare
        self.loop = 0
        self.seen = {}

    def at(self, n):
        return (self.sem, self.loop, n)

    def now(self):
        return self.at(self.n)

    def wait(self, *toks):
        for tok in toks:
            if tok is None:
                continue
            sem, loop, n = tok
            if isinstance(loop, int) and loop + n <= 0:
                continue
            key = sem.name
            if self.seen.get(key, -10 ** 9) >= n:
                continue
            self.seen[key] = n
            self.eng.wait_ge(sem, loop + n)
            self.open = not isinstance(loop, int)

    def settle(self):
        if self.open:
            self.eng.sem_inc(self.spare, 1)
            self.open = False

    def tick(self, ins):
        ins.then_inc(self.sem, 1)
        self.n += 1
        return self.now()


class Ring:

    def __init__(self, nc, raw, hi, lo, full, hi_ready, lo_ready, used, spare):
        self.nc, self.raw, self.hi, self.lo = nc, raw, hi, lo
        self.full, self.hi_ready, self.lo_ready, self.used, self.spare = full, hi_ready, lo_ready, used, spare
        self.loads = self.splits = self.freed = 0
        self.loop = self.loop16 = 0
        self.hold = False

    def split(self, AC, VE):
        n, slot = self.splits, self.splits % RING
        AC.wait((self.full[slot], self.loop16, 16 * (n // RING + 1)), (self.used, self.loop, n + 1))
        self.nc.scalar.activation(self.hi[:, slot, :], self.raw[:, slot, :], ACT.Copy).then_inc(self.hi_ready, 1)
        VE.wait((self.hi_ready, self.loop, n + 1))
        self.nc.vector.tensor_tensor(self.lo[:, slot, :], self.raw[:, slot, :], self.hi[:, slot, :].bitcast(F32),
                                     ALU.subtract).then_inc(self.lo_ready, 1)
        self.splits += 1

    def catch_up(self, AC, VE, count=None):
        while self.splits < min(self.loads + LEAD, self.limit) and count != 0:
            self.split(AC, VE)
            count = None if count is None else count - 1

    def take(self, src, AC, VE, rows=P):
        n, slot = self.loads, self.loads % RING
        a, b = src.shape[1], src.shape[2]

        def view(t):
            return t[0:rows, slot, 0:a * b].rearrange("p (a b) -> p a b", a=a)

        self.nc.sync.wait_ge(self.lo_ready, self.loop + n + 1)
        if not isinstance(self.loop, int):
            self.nc.sync.sem_inc(self.spare, 1)
        self.nc.sync.dma_start(view(self.raw), src).then_inc(self.full[slot], 16)
        self.loads += 1
        if not self.hold:
            self.catch_up(AC, VE)
        return dict(w=(view(self.hi), view(self.lo)), hi=(self.hi_ready, self.loop, n + 1),
                    lo=(self.lo_ready, self.loop, RING + n + 1))

    def release(self, ins):
        ins.then_inc(self.used, 1)
        self.freed += 1
        return (self.used, self.loop, RING + self.freed)


def program(nc, IN, out):
    ctx = ExitStack()
    with ctx:
        def sb(name, shape, dt=F32):
            return ctx.enter_context(nc.sbuf_tensor(name, shape, dt))

        def sem(name):
            return ctx.enter_context(nc.semaphore(name))

        bank = [ctx.enter_context(nc.psum_tensor(f"bank{i}", [P, 512], F32)) for i in range(8)]
        wraw = sb("wraw", [P, RING, SLOT])
        whi = sb("whi", [P, RING, SLOT], F32R)
        wlo = sb("wlo", [P, RING, SLOT], F32R)
        hT = sb("hT", [P, KD, T1])
        xh, xl = sb("xhi", [P, KD, T1], F32R), sb("xlo", [P, KD, T1], F32R)
        rst = sb("rst", [P, T1])
        rst2 = sb("rst2", [P, T1])
        rz = sb("rz", [P, T1])
        ry = sb("ry", [P, T1])
        ssum = sb("ssum", [P, T1])
        sqb = sb("sqb", [P, 2, T1])
        cst = sb("cst", [P, CONST_N])
        gain1 = sb("gain1", [P, 108])
        gain2 = sb("gain2", [P, 80])
        gain3 = sb("gain3", [MH, 72])
        gcur = sb("gcur", [P, 56])
        small = sb("small", [P, 64])
        wau = sb("wau", [GATE_RANK, GLA_KW])

        def C(name):
            a, w = CONST_AT[name]
            return cst[:, a:a + w]

        full = [sem(f"full{i}") for i in range(RING)]
        hi_ready, lo_ready, used = sem("hi_ready"), sem("lo_ready"), sem("used")
        par = sem("par")
        s_in = sem("s_in")
        s_bias = sem("s_bias")
        s_out = sem("s_out")
        spare = sem("spare")
        PE = Lane("pe", nc.tensor, sem("pe_done"), spare)
        AC = Lane("act", nc.scalar, sem("act_done"), spare)
        VE = Lane("dve", nc.vector, sem("dve_done"), spare)
        PO = Lane("pool", nc.gpsimd, sem("pool_done"), spare)
        lanes = [PE, AC, VE, PO]
        nc.sync.sem_inc(lo_ready, RING)
        nc.sync.sem_inc(used, RING)
        ring = Ring(nc, wraw, whi, wlo, full, hi_ready, lo_ready, used, spare)
        ring.limit = UNITS
        par_n = [0, 0]

        def ve(fn, toks, *a, **k):
            VE.wait(*toks)
            return VE.tick(getop(nc.vector, fn)(*a, **k))

        def po(fn, toks, *a, **k):
            PO.wait(*toks)
            PO.settle()
            return PO.tick(getop(nc.gpsimd, fn)(*a, **k))

        def getop(eng, fn):
            return {"tt": eng.tensor_tensor, "ts": eng.tensor_scalar, "copy": eng.tensor_copy, "memset": eng.memset,
                    "stt": nc.vector.scalar_tensor_tensor, "ttr": nc.vector.tensor_tensor_reduce,
                    "scan": nc.vector.tensor_tensor_scan, "rmax": nc.vector.reduce_max,
                    "recip": nc.vector.reciprocal}[fn]

        act_set = [None]

        def ac(toks, out_, in_, func, **k):
            if func in (ACT.Exp, ACT.Ln) and act_set[0] != "exp_ln":
                nc.scalar.preload_act_table_set("natural_log_exp_and_others")
                act_set[0] = "exp_ln"
            elif func in (ACT.Silu, ACT.Sigmoid):
                act_set[0] = func
            AC.wait(*toks)
            return AC.tick(nc.scalar.activation(out_, in_, func, **k))

        def mm(out_, lhsT, rhs, start, stop):
            return nc.tensor.matmul(out_, lhsT, rhs, start=start, stop=stop, skip_group_check=True)

        def rsqrt(dst, src, toks):
            z = rz[0:src.shape[0], 0:src.shape[1]]
            rd = ve("ts", toks, z, src, EPS, None, ALU.add)
            t = ac([rd], dst, z, ACT.Ln)
            t = ac([t], dst, dst, ACT.Exp, scale=-0.5)
            u = ry[0:src.shape[0], 0:src.shape[1]]
            t = ve("stt", [t], u, dst, -0.5, dst, ALU.mult, ALU.mult)
            t = ve("tt", [t], u, u, z, ALU.mult)
            return ve("stt", [t], dst, u, 1.5, dst, ALU.add, ALU.mult)

        def par_load(dst, src, toks=(), slow=False):
            PO.wait(*toks)
            PO.settle()
            if slow:
                with nc.allow_non_contiguous_dma(reason="a few small columns"):
                    nc.gpsimd.dma_start(dst, src).then_inc(par, 16)
            else:
                nc.gpsimd.dma_start(dst, src).then_inc(par, 16)
            par_n[0] += 16

        def par_all():
            return (par, par_n[1], par_n[0])

        def forget():
            for ln in lanes:
                ln.seen = {}

        def join():
            toks = [ln.now() for ln in lanes]
            for ln in lanes:
                ln.wait(*[t for t in toks if t[0] is not ln.sem])

        scopes = [0]

        class Scope:

            def __init__(self):
                self.stack = ExitStack()
                scopes[0] += 1
                self.id = scopes[0]
                self.count = 0

            def take(self, *shape, dt=F32):
                self.count += 1
                t = self.stack.enter_context(nc.sbuf_tensor(f"s{self.id}_{self.count}", [P] + list(shape), dt))
                return t[tuple([slice(None)] * (1 + len(shape)))]

            def pair(self, *shape):
                return self.take(*shape, dt=F32R), self.take(*shape, dt=F32R)

            def close(self):
                self.stack.close()

        h_tok = [None] * KD

        start = Scope()
        g1 = start.take(P)
        g2 = start.take(P)
        g3 = start.take(P)
        xs = start.take(3, D)
        nc.scalar.dma_start(cst[:, :], IN["consts"]).then_inc(s_in, 16)
        nc.scalar.dma_start(xs[0:N_META, 2, :], IN["meta_tokens"]).then_inc(s_in, 16)
        nc.scalar.dma_start(xs[:, 0:2, :], IN["x"][0].rearrange("(t p) d -> p t d", p=P)).then_inc(s_in, 16)
        for i, name in enumerate(("g_pre_ffn1", "g_post_ffn1", "g_pre_mix", "g_post_mix", "g_pre_ffn2", "g_post_ffn2")):
            par_load(g1[16 * i:16 * i + 16, :], IN[name].rearrange("l (k p) -> (l k) p", p=P))
        par_load(g1[96:100, :], IN["b_alpha"].rearrange("l (k p) -> (l k) p", p=P))
        par_load(g1[100:108, :], IN["g_gla_out"].rearrange("l (k p) -> (l k) p", p=P))
        for i, name in enumerate(("ffn1_norm_2", "ffn2_norm_2", "mix_norm_2", "mem_norm_2")):
            par_load(g2[16 * i:16 * i + 16, :], IN[name].rearrange("l (k p) -> (l k) p", p=P))
        par_load(g2[64:72, :], IN["kv_norm_2"].rearrange("(k p) -> k p", p=P))
        for c in (0, HD):
            par_load(g2[72:74, c:c + HD], IN["mem_q_norm_2"])
            par_load(g2[74:76, c:c + HD], IN["mem_k_norm_2"])
            par_load(g2[76:77, c:c + HD], IN["b_q_norm_2"])
            par_load(g2[77:78, c:c + HD], IN["kv_k_norm_2"].rearrange("(a p) -> a p", a=1))
        par_load(g3[0:8, 0:MH], IN["a_h_norm_2"].rearrange("l h (j p) -> (l h j) p", p=MH))
        par_load(g3[8:72, 0:MH], IN["a_conv_2"].rearrange("l j (c p) -> (l j c) p", p=MH))
        PE.wait(par_all(), (s_in, 0, 48))
        VE.wait((s_in, 0, 48))
        AC.wait((s_in, 0, 48))
        ident = C("ident")
        for b, (src, rows, w, dst) in enumerate(((g1, 108, P, gain1), (g2, 78, P, gain2), (g3, 72, MH, gain3))):
            t = PE.tick(nc.tensor.transpose(bank[b][0:w, 0:rows], src[0:rows, 0:w], ident[0:rows, 0:rows]))
            ve("copy", [t], dst[:, 0:rows], bank[b][0:w, 0:rows])
        ve("ts", [VE.now()], gain2[:, 72:74], gain2[:, 72:74], HD ** -0.5, None, ALU.mult)
        ve("ts", [VE.now()], gain2[:, 76:77], gain2[:, 76:77], HD ** -0.5, None, ALU.mult)
        for c in (16, 80):
            ve("ts", [VE.now()], gain1[:, c:c + 16], gain1[:, c:c + 16], 0.5, None, ALU.mult)
        taken = [None] * 8

        def turn_rows(src, rows, t, dst, c0):
            for k in range(KD):
                b = 4 + k % 4
                PE.wait(taken[b])
                tk = PE.tick(nc.tensor.transpose(bank[b][:, 0:rows], src[0:rows, t, k * P:k * P + P], ident[0:rows, 0:rows]))
                taken[b] = ve("copy", [tk], dst[:, k, c0:c0 + rows], bank[b][:, 0:rows])
                h_tok[k] = taken[b]

        turn_rows(xs, N_META, 2, hT, 0)
        turn_rows(xs, P, 0, hT, N_META)
        turn_rows(xs, P, 1, hT, N_META + P)
        start.close()

        rtok = [None]
        xt = [[None] * KD, [None] * KD]

        def take(src, rows=P):
            return ring.take(src, AC, VE, rows)

        def to_pair(dst, k, src, toks, gain=1.0):
            th = ac(toks, dst[0][k], src, ACT.Copy, scale=gain)
            tl = ve("stt", [th], dst[1][k], src, gain, dst[0][k].bitcast(F32), ALU.mult, ALU.subtract)
            return th, tl

        def squares(src, toks, cols, part, lane):
            c0, c1 = cols
            for k in part:
                if k == 0:
                    t = sum_tok[0] = ac([toks[k]], ssum[:, 0:c1 - c0], src[:, k, c0:c1], ACT.Square)
                else:
                    t = ac([toks[k], sq_free[k % 2]], sqb[:, k % 2, 0:c1 - c0], src[:, k, c0:c1], ACT.Square)
                    t = sq_free[k % 2] = sum_tok[0] = lane("tt", [t, sum_tok[0]], ssum[:, 0:c1 - c0], ssum[:, 0:c1 - c0], sqb[:, k % 2, 0:c1 - c0], ALU.add)
            return t

        sq_free = [None, None]
        sum_tok = [None]

        def stats(t, cols, b):
            c0, c1 = cols
            PE.wait(t)
            t = PE.tick(mm(bank[b][:, 0:c1 - c0], C("mean1024"), ssum[:, 0:c1 - c0], True, True))
            rtok[0] = rsqrt(rst[:, c0:c1], bank[b][:, 0:c1 - c0], [t])

        def norm_in(gain, cols):
            c0, c1 = cols
            for k in range(KD):
                h = hT[:, k, c0:c1]
                xt[0][k], xt[1][k] = to_pair(([None] * k + [xh[:, k, c0:c1]], [None] * k + [xl[:, k, c0:c1]]), k, h, [h_tok[k]], gain(k))

        def products(out_, U, w, x, n_k=KD, start=True, stop=True, toks=None):
            passes = ((0, 0), (1, 0), (0, 1))
            for i, (a, b) in enumerate(passes):
                PE.wait(U["hi"] if i == 0 else U["lo"])
                for k in range(n_k):
                    if toks is not None and i != 1:
                        PE.wait(toks[b][k])
                    m = mm(out_, w(k, a), x(k, b), start and i == 0 and k == 0, stop and i == 2 and k == n_k - 1)
            return m

        def xin(cols):
            c0, c1 = cols
            return lambda k, part: (xh, xl)[part][:, k, c0:c1]

        def ffn(gate_src, up_src, down_src, gain, cols, post):
            c0, c1 = cols
            T = c1 - c0
            sc = Scope()
            ah, al = sc.pair(NF, T1)
            sg, su = sc.take(2, T1), sc.take(2, T1)
            y = sc.take(KD, T1) if post is not None else None
            norm_in(gain, cols)
            x = xin(cols)
            evac = {}

            def half(src, i, toks=None):
                U = take(src)
                m = products(bank[i][:, 0:T], U, lambda k, part: U["w"][part][:, k, :], x, toks=toks)
                return ring.release(m)

            def part1(j, tg, tu):
                t1 = ve("tt", [tg, rtok[0]], sg[:, j, 0:T], bank[2 * j][:, 0:T], rst[:, c0:c1], ALU.mult)
                t2 = ac([t1], sg[:, j, 0:T], sg[:, j, 0:T], ACT.Silu)
                evac[j] = ve("tt", [tu, al_tok[j]], su[:, j, 0:T], bank[2 * j + 1][:, 0:T], rst[:, c0:c1], ALU.mult)
                return t2

            def part2(f, j, t):
                t = ve("tt", [t, evac[j]], su[:, j, 0:T], su[:, j, 0:T], sg[:, j, 0:T], ALU.mult)
                return ac([t], ah[:, f, c0:c1], su[:, j, 0:T], ACT.Copy)

            def part3(f, j, t):
                al_tok[j] = ve("tt", [t], al[:, f, c0:c1], su[:, j, 0:T], ah[:, f, c0:c1].bitcast(F32), ALU.subtract)

            al_tok = [None, None]
            tg0 = half(gate_src(0, 0), 0, xt)
            squares(hT, h_tok, cols, range(0, 4), po)
            tu0 = half(up_src(0, 0), 1)
            tq = squares(hT, h_tok, cols, range(4, 8), po)
            tg1 = half(gate_src(0, 1), 2)
            stats(tq, cols, 7)
            t = part1(0, tg0, tu0)
            tu1 = half(up_src(0, 1), 3)
            t = part2(0, 0, t)
            t1 = part1(1, tg1, tu1)
            part3(0, 0, t)
            part3(1, 1, part2(1, 1, t1))
            for ln in lanes:
                ln.settle()
            forget()
            entry = {ln: (ln.n, ln.loop) for ln in lanes}
            r_entry = (ring.loads, ring.splits, ring.freed, ring.loop, ring.loop16)
            PER = {PE: 0, AC: 4, VE: 8}
            with nc.Fori(0, TURNS - 1) as i:
                act_set[0] = None
                for ln in (AC, VE):
                    ln.loop = nc.snap(ln.loop + i * PER[ln])
                ring.loop = nc.snap(ring.loop + i * RING)
                ring.loop16 = nc.snap(ring.loop16 + i * 16)
                f = i * 2 + 2
                v0 = VE.n
                PE.wait(VE.at(v0 - 6))
                tg = half(gate_src(i + 1, 0), 0)
                tu = half(up_src(i + 1, 0), 1)
                al_tok[0] = al_tok[1] = None
                VE.wait(VE.at(v0))
                t = part1(0, tg, tu)
                PE.wait(VE.at(v0))
                tg = half(gate_src(i + 1, 1), 2)
                t = part2(f, 0, t)
                tu = half(up_src(i + 1, 1), 3)
                part3(f, 0, t)
                t = part1(1, tg, tu)
                part3(f + 1, 1, part2(f + 1, 1, t))
                a_last, v_last, v_bank = AC.n, VE.n, VE.n - 2
            for ln in (PE, AC, VE):
                assert ln.n - entry[ln][0] == PER[ln], (ln.name, ln.n - entry[ln][0])
                ln.n, ln.loop = entry[ln][0] + (TURNS - 1) * PER[ln], entry[ln][1]
            more = RING * (TURNS - 1)
            ring.loads, ring.splits, ring.freed, ring.loop, ring.loop16 = \
                r_entry[0] + more, r_entry[1] + more, r_entry[2] + more, r_entry[3], r_entry[4]
            forget()
            order = [4, 5, 6, 7, 0, 1, 2, 3]
            PE.wait(AC.at(AC.n - PER[AC]), VE.at(VE.n - PER[VE]))
            LAST = RING
            for f in range(NF - LAST):
                U = take(down_src(f))
                if f == NF - LAST - 1:
                    ring.hold = True
                PE.wait(U["hi"], U["lo"])
                for d in order:
                    if f == 0 and d == 0:
                        PE.wait(VE.now())
                    for z, (a, b) in enumerate(((0, 0), (1, 0), (0, 1))):
                        m = mm(bank[d][:, 0:T], U["w"][a][:, 0, d * P:d * P + P], (ah, al)[b][:, f, c0:c1], f == 0 and z == 0, False)
                ring.release(m)
            PE.wait(AC.now(), VE.now())
            us = []
            for z in range(LAST):
                us.append(take(down_src(NF - LAST + z)))
            ring.hold = False
            while ring.splits < ring.loads:
                ring.split(AC, VE)
            done = []
            for d in range(KD):
                for q, U in enumerate(us):
                    PE.wait(U["hi"], U["lo"])
                    f = NF - LAST + q
                    for z, (a, b) in enumerate(((0, 0), (1, 0), (0, 1))):
                        m = mm(bank[d][:, 0:T], U["w"][a][:, 0, d * P:d * P + P], (ah, al)[b][:, f, c0:c1], False,
                               q == LAST - 1 and z == 2)
                    if d == KD - 1:
                        t = ring.release(m)
                done.append(t if d == KD - 1 else PE.tick(m))
            if post is None:
                for d in range(KD):
                    h_tok[d] = ve("stt", [done[d]], hT[:, d, c0:c1], bank[d][:, 0:T], 0.5, hT[:, d, c0:c1], ALU.mult, ALU.add)
                ring.catch_up(AC, VE)
            else:
                postnorm(done, post, cols, y)
            sc.close()

        def postnorm(done, gain, cols, y):
            c0, c1 = cols
            T = c1 - c0
            tv = []
            for d in range(KD):
                tv.append(ve("copy", [done[d]], y[:, d, c0:c1], bank[d][:, 0:T]))
                t = squares(y, tv + [None] * (KD - 1 - d), cols, [d], ve)
            ring.catch_up(AC, VE, 1)
            PE.wait(tv[0])
            stats(t, cols, 0)
            for d in range(KD):
                yd = y[:, d, c0:c1]
                ty = ve("stt", [rtok[0], tv[d]], yd, yd, gain(d), rst[:, c0:c1], ALU.mult, ALU.mult)
                h_tok[d] = ve("tt", [ty], hT[:, d, c0:c1], hT[:, d, c0:c1], yd, ALU.add)
            ring.catch_up(AC, VE)

        def columns(wd, a, w=P):
            return wd.rearrange("(k p) n -> p k n", p=P)[:, :, a:a + w]

        proj_bank = [0]

        def next_bank():
            b = proj_bank[0]
            proj_bank[0] = 1 - b
            PE.wait(taken[b])
            return b

        def project(U, x, T, M=P, c=0, last=True, toks=None):
            b = next_bank()
            m = products(bank[b][0:M, 0:T], U, lambda k, part: U["w"][part][:, k, c:c + M], x, toks=toks)
            return b, ring.release(m) if last else PE.tick(m)

        def turned_steps(items, zb, tiles, tb):
            VE.wait(PE.now(), VE.now())
            free = [None, None]
            pend = None
            for i, item in enumerate(list(items) + [None]):
                new = None
                if item is not None:
                    make, scaled, dst, finish = item
                    z = i % 2
                    b, t = make()
                    w = tiles[-1][0] + tiles[-1][1]
                    if scaled is not None:
                        t = taken[b] = ve("tt", [t, rtok[0], free[z]], zb[z][:, 0:w], bank[b][:, 0:w], scaled, ALU.mult)
                    else:
                        t = taken[b] = ve("copy", [t, free[z]], zb[z][:, 0:w], bank[b][:, 0:w])
                    new = (z, t, dst, finish)
                if pend is not None:
                    z, t, dst, finish = pend
                    PE.wait(t, taken[tb])
                    for j, (c0, n) in enumerate(tiles):
                        m = nc.tensor.transpose(bank[tb][0:n, j * P:j * P + P], zb[z][:, c0:c0 + n], ident)
                    t = free[z] = PE.tick(m)
                    for j, (c0, n) in enumerate(tiles):
                        t2 = ac([t], dst[j][0:n], bank[tb][0:n, j * P:j * P + P], ACT.Copy)
                    taken[tb] = t2
                    finish(t2)
                pend = new
                yield

        def attention(units, bufs, s_banks, t_banks):
            SS, PP, PT, st = bufs
            p_free = [None, None]
            pt_free = [None, None]
            state = {}
            for i in range(len(units) + 2):
                if i < len(units):
                    u = units[i]
                    z = i % 2
                    n, W = u["n"], u["W"]
                    sb_ = bank[s_banks[z]]
                    PE.wait(taken[s_banks[z]], *u["need"])
                    for (q, k, w, c) in u["qk"]:
                        m = mm(sb_[0:n, c:c + w], q, k, True, True)
                    t = PE.tick(m)
                    mx, nm, den, rd = (st[0:n, 4 * z + x:4 * z + x + 1] for x in range(4))
                    if u["mask"] is not None:
                        t = ve("tt", [t, p_free[z]], SS[z][0:n, 0:W], sb_[0:n, 0:W], u["mask"], ALU.add)
                        taken[s_banks[z]] = t
                        src = SS[z][0:n, 0:W]
                    else:
                        src = sb_[0:n, 0:W]
                    t = ve("rmax", [t], mx, src, AX_X)
                    t = ve("ts", [t], nm, mx, -1.0, None, ALU.mult)
                    t = ac([t, p_free[z]], PP[z][0:n, 0:W], src, ACT.Exp, bias=nm, accum_out=den)
                    if u["mask"] is None:
                        taken[s_banks[z]] = t
                    t = ve("recip", [t], rd, den)
                    t = ve("ts", [t], PP[z][0:n, 0:W], PP[z][0:n, 0:W], rd, None, ALU.mult)
                    state[i] = t
                if 0 <= i - 1 < len(units):
                    u = units[i - 1]
                    z = (i - 1) % 2
                    n = u["n"]
                    tb_ = bank[t_banks[z]]
                    PE.wait(state[i - 1], taken[t_banks[z]])
                    PE.settle()
                    for (c, ns, slot) in u["turn"]:
                        m = nc.tensor.transpose(tb_[0:ns, slot * P:slot * P + n], PP[z][0:n, c:c + ns], ident[0:n, 0:n])
                    t = PE.tick(m)
                    p_free[z] = t
                    fulls = [s for s in u["turn"] if s[1] == P]
                    rest = [s for s in u["turn"] if s[1] != P]
                    nf = len(fulls)
                    if nf:
                        a = tb_[:, 0:nf * P].rearrange("p (s c) -> p s c", c=P)[:, :, 0:n]
                        o = PT[z][:, 0:nf * P].rearrange("p (s c) -> p s c", c=P)[:, :, 0:n]
                        tc = ac([t, pt_free[z]], o, a, ACT.Copy)
                    for (c, ns, slot) in rest:
                        tc = ac([t, pt_free[z]], PT[z][0:ns, slot * P:slot * P + n], tb_[0:ns, slot * P:slot * P + n], ACT.Copy)
                    taken[t_banks[z]] = tc
                    state[i - 1] = tc
                if 0 <= i - 2 < len(units):
                    u = units[i - 2]
                    z = (i - 2) % 2
                    n = u["n"]
                    PE.wait(state[i - 2])
                    u["open"]()
                    for (o, terms) in u["pv"]:
                        for x, (slot, ns, v) in enumerate(terms):
                            m = mm(o, v, PT[z][0:ns, slot * P:slot * P + n], x == 0, x == len(terms) - 1)
                    t = PE.tick(m)
                    pt_free[z] = t
                    u["close"](t)
                yield

        def drive(main, sides):
            sides = list(sides)

            def side_steps():
                for g in list(sides):
                    if next(g, sides) is sides:
                        sides.remove(g)

            for _ in main:
                side_steps()
            while sides:
                side_steps()

        def log_sigmoid(dst, z, scr, toks):
            t = ve("stt", toks, scr, z, -1.0, z, ALU.mult, ALU.max)
            t = ac([t], scr, scr, ACT.Exp, scale=-1.0)
            t = ac([t], scr, scr, ACT.Ln, bias=1.0)
            return ve("stt", [t], dst, z, 0.0, scr, ALU.min, ALU.subtract)

        cols1 = (0, T1)
        PER_LAYER = 4096

        w_in_at = dict(zip(("fq", "fk", "fv", "ff", "gq", "gk", "gv", "ga", "gr", "ma", "mb"), SPLIT_AT))

        def mixer1(L):
            lay = Scope()
            qa = lay.take(FOX_HEADS, T1)
            ka = lay.take(FOX_HEADS, T1)
            fv = lay.take(3, FOX_W)
            gq = lay.take(2, T1)
            gk = lay.take(2, T1)
            gv = lay.take(3, GLA_W)
            cb = lay.take(2, T1)
            qz, kz = lay.take(2, T1), lay.take(2, T1)
            at = lay.take(GLA_HEADS, 2 * T1)
            gr = lay.take(4, T1)
            ofp, ogp = lay.pair(4, T1), lay.pair(4, T1)
            dg = lay.take(T1)
            sg = lay.take(2, T1)
            cums = lay.take(2, T1)
            ybuf = lay.take(KD, T1)
            lay_x = rst2
            X = [sg[:, 0:2, :], ybuf[:, 5:7, :]]
            SS = [ybuf[:, 0, :], ybuf[:, 1, :]]
            PP = [lay.take(T1), lay.take(T1)]
            zb1 = (sqb[:, 0, :], sqb[:, 1, :])
            ptv = ybuf[:, 2:5, :].rearrange("p a b -> p (a b)")
            PT = [ptv[:, 0:384], ptv[:, 384:768]]
            smh = lay.take(2 * KD, T1)
            w_in = IN["w_in"][L]
            gain = lambda g: (lambda k: gcur[:, 8 * g + k:8 * g + k + 1])
            x = xin(cols1)
            norm_in(gain(2), cols1)
            tzx = [po("memset", [], x_, 0.0) for x_ in X][-1]
            po("memset", [], qa, 0.0)
            po("memset", [], ka, 0.0)
            zeroed = PO.now()
            tk = {}
            sc = small

            def load(name, a):
                return take(columns(w_in, w_in_at[name] + a))

            def halves(name, out_, toks=None):
                b = next_bank()
                for z in range(2):
                    U = take(columns(w_in, w_in_at[name])[:, 4 * z:4 * z + 4, :])
                    m = products(bank[b][:, 0:T1], U, lambda k, part: U["w"][part][:, k, :],
                                 lambda k, part: x(4 * z + k, part), n_k=4, start=z == 0, stop=z == 1,
                                 toks=None if toks is None else [tt[4 * z:4 * z + 4] for tt in toks])
                    t = ring.release(m)
                return b, t

            def main():
                b, t = halves("ga", None, xt)
                tq = squares(hT, h_tok, cols1, range(KD), ve)
                U = load("gq", 0)
                b1, t1 = project(U, x, T1)
                stats(tq, cols1, 7)
                taken[7] = VE.now()
                tga = taken[b] = ve("tt", [t, rtok[0]], lay_x[0:GATE_RANK, :], bank[b][0:GATE_RANK, 0:T1], rst[0:GATE_RANK, :], ALU.mult)
                tk["gq", 0] = taken[b1] = ve("stt", [t1], gq[:, 0, :], bank[b1][:, 0:T1], GLA_DK ** -0.5, rst[:, :], ALU.mult, ALU.mult)
                b1, t1 = project(load("gq", P), x, T1)
                tk["gq", 1] = taken[b1] = ve("stt", [t1], gq[:, 1, :], bank[b1][:, 0:T1], GLA_DK ** -0.5, rst[:, :], ALU.mult, ALU.mult)
                PE.wait(tga)
                for c in range(2):
                    b = next_bank()
                    t = PE.tick(mm(bank[b][:, 0:T1], wau[:, c * P:c * P + P], lay_x[0:GATE_RANK, :], True, True))
                    t = taken[b] = ve("ts", [t], cb[:, c, :], bank[b][:, 0:T1], gcur[:, 48 + c:49 + c], None, ALU.add)
                    t = log_sigmoid(cb[:, c, :], cb[:, c, :], ssum[:, :], [t])
                    t = ve("ts", [t], cb[:, c, :], cb[:, c, :], 1.0 / 16.0, None, ALU.mult)
                    tk["cb", c] = ve("scan", [t], cb[:, c, :], C("ones"), cb[:, c, :], 0.0, ALU.mult, ALU.add)
                for c in range(2):
                    b, t = project(load("gk", c * P), x, T1)
                    tk["gk", c] = taken[b] = ve("tt", [t], gk[:, c, :], bank[b][:, 0:T1], rst[:, :], ALU.mult)
                    yield
                b, t = halves("ff", None)
                H8 = slice(0, FOX_HEADS)
                cum, ncum = cums[H8, 0, :], cums[H8, 1, :]
                t = taken[b] = ve("tt", [t], cum, bank[b][H8, 0:T1], rst[H8, :], ALU.mult)
                t = ve("ts", [t], cum, cum, small[H8, 0:1], None, ALU.add)
                t = log_sigmoid(cum, cum, ncum, [t])
                t = ve("scan", [t], cum, C("ones")[H8, :], cum, 0.0, ALU.mult, ALU.add)
                tk["cum"] = ve("ts", [t], ncum, cum, -1.0, None, ALU.mult)
                yield
                for name, dst, scale in (("fq", qa, HD ** -0.5), ("fk", ka, 1.0)):
                    for s in range(4):
                        b, t = project(load(name, s * P), x, T1)
                        h = 2 * s
                        VE.wait(zeroed)
                        ve("stt", [t], dst[0:64, h, :], bank[b][0:64, 0:T1], scale, rst[0:64, :], ALU.mult, ALU.mult)
                        tk[name, h] = taken[b] = ve("stt", [t], dst[64:128, h + 1, :], bank[b][64:128, 0:T1], scale,
                                                    rst[64:128, :], ALU.mult, ALU.mult)
                        yield
                one = C("ones")[0:1, :]
                for h in range(FOX_HEADS):
                    r = 64 if h % 2 == 0 else 0
                    for dst, row, src in ((qa, r, cums[h:h + 1, 0, :]), (qa, r + 1, one), (ka, r, one), (ka, r + 1, cums[h:h + 1, 1, :])):
                        par_load(dst[row:row + 1, h, :], src, [tk["cum"], zeroed])
                tk["aug"] = par_all()
                def value(name, dst, s):
                    def done(t):
                        tk[name, s] = t
                    return (lambda: project(load(name, s * P), x, T1), rst[:, :],
                            [dst[:, i, s * P:s * P + P] for i in range(3)], done)
                yield from turned_steps([value(name, dst, s) for name, dst in (("fv", fv), ("gv", gv)) for s in range(4)],
                                        zb1, TOK_TILES1, 3)
                for i in range(4):
                    b, t = project(load("gr", i * P), x, T1)
                    t1 = taken[b] = ve("tt", [t], gr[:, i, :], bank[b][:, 0:T1], rst[:, :], ALU.mult)
                    t1 = ac([t1], rst2[:, 0:T1], gr[:, i, :], ACT.Exp, scale=-1.0)
                    t1 = ve("ts", [t1], rst2[:, 0:T1], rst2[:, 0:T1], 1.0, None, ALU.add)
                    t1 = ve("recip", [t1], rst2[:, 0:T1], rst2[:, 0:T1])
                    tk["gr", i] = ve("tt", [t1], gr[:, i, :], gr[:, i, :], rst2[:, 0:T1], ALU.mult)
                    AC.wait(tk["gr", i])
                    yield
                for i in range(2 * KD):
                    b, t = project(load("ma", i * P), x, T1)
                    tk["m", i] = taken[b] = ve("tt", [t], smh[:, i, :], bank[b][:, 0:T1], rst[:, :], ALU.mult)
                    yield

            def gla():
                yield from gla_diag()
                yield from gla_levels()
                yield from gla_outputs()

            def gla_diag():
                s4 = lambda a: a.rearrange("p c (i j) -> p c i j", j=SUB)
                ready = [tk[n, c] for n in ("gq", "gk", "cb") for c in range(2)] + [tzx]
                read = [None, None]
                pend = None
                for j in list(reversed(range(SUB))) + [None]:
                    if j is not None:
                        n, z = SUB - j, j % 2
                        xs_ = s4(X[z])[:, :, :, j:SUB]
                        at_s = lambda a: s4(a)[:, :, :, j:j + 1].broadcast_to([P, 2, N_SUB, n])
                        t = ve("tt", ready + [read[z]], xs_, s4(cb)[:, :, :, j:SUB], at_s(cb), ALU.subtract)
                        t = ac([t], xs_, xs_, ACT.Exp)
                        t = ve("tt", [t], xs_, xs_, s4(gq)[:, :, :, j:SUB], ALU.mult)
                        t = ve("tt", [t], xs_, xs_, at_s(gk), ALU.mult)
                    if pend is not None:
                        jj, tt = pend
                        PE.wait(tt, taken[7])
                        for c in range(2):
                            pick = C("pickd")[:, 80 * c + 15 - jj:80 * c + 15 - jj + 64]
                            m = mm(bank[7][0:64, 0:T1], pick, X[jj % 2][:, c, :], jj == SUB - 1 and c == 0, jj == 0 and c == 1)
                        read[jj % 2] = PE.tick(m)
                    pend = (j, t) if j is not None else None
                    if j is not None:
                        yield
                tk["dg"] = taken[7] = ve("copy", [read[0]], dg[0:64, :], bank[7][0:64, 0:T1])

            def gla_levels():
                scr = ybuf[:, 5:7, :].rearrange("p a b -> p (a b)")[:, 0:512]
                e = X[0]
                H = range(GLA_HEADS)
                rows = lambda h: slice(64 * (h % 2), 64 * (h % 2) + 64)

                def prep(L):
                    if L < 256:
                        w = 2 * L
                        v = lambda a: a[:, :, 0:256].rearrange("p c (m l) -> p c m l", l=w)
                        ref = v(cb)[:, :, :, L - 1:L].broadcast_to([P, 2, 256 // w, w])
                    else:
                        v = lambda a: a
                        ref = cb[:, :, 255:256].broadcast_to([P, 2, T1])
                    t = ve("tt", [PE.now(), VE.now()], v(e), v(cb), ref, ALU.subtract)
                    t = ac([t], v(e), v(e), ACT.Abs)
                    t = ac([t], v(e), v(e), ACT.Exp, scale=-1.0)
                    ve("tt", [t], v(qz), v(gq), v(e), ALU.mult)
                    return ve("tt", [t], v(kz), v(gk), v(e), ALU.mult)

                def masked(level, first):
                    mask = C("blocks")[:, 128 * level:128 * level + 128].unsqueeze(1).unsqueeze(1).broadcast_to([P, 2, 2, P])
                    for b in range(2):
                        src = bank[4 + b][:, 0:512].rearrange("p (h i t) -> p h i t", h=2, i=2)
                        dst = at.rearrange("p (h b) (i t) -> p b h i t", b=2, i=2)[:, b, :, :, 0:P]
                        if first:
                            taken[4 + b] = t = ve("tt", [read_at], dst, src, mask, ALU.mult)
                        else:
                            s4 = scr.rearrange("p (h i t) -> p h i t", h=2, i=2)
                            taken[4 + b] = t = ve("tt", [read_at, VE.now()], s4, src, mask, ALU.mult)
                            t = ve("tt", [t], dst, dst, s4, ALU.add)
                    tk["at"] = t

                tp = prep(SUB)
                PE.wait(tk["dg"], taken[4], taken[5])
                cell = lambda h, i: bank[4 + h % 2][:, (h // 2) * 256 + i * P:(h // 2) * 256 + i * P + P]
                for h in H:
                    for i in range(2):
                        m = mm(cell(h, i), C("rep")[0:64, h * P:h * P + P], dg[0:64, i * P:i * P + P], True, True)
                read_at = PE.tick(m)
                masked(0, True)
                yield
                for level in range(1, 4):
                    PE.wait(tp, taken[4], taken[5])
                    for h in H:
                        for c0 in (0, P):
                            m = mm(cell(h, c0 // P), kz[rows(h), h // 2, c0:c0 + P], qz[rows(h), h // 2, c0:c0 + P], True, True)
                    read_at = PE.tick(m)
                    tp = prep(SUB << level)
                    masked(level, False)
                    yield
                PE.wait(tp, taken[4], taken[5])
                for h in H:
                    mm(bank[4 + h % 2][:, (h // 2) * P:(h // 2) * P + P], kz[rows(h), h // 2, 0:P], qz[rows(h), h // 2, P:2 * P], True, True)
                PE.wait(taken[7])
                for h in H:
                    m = mm(bank[7][0:SUB, h * SUB:h * SUB + SUB], C("rep")[0:64, h * P:h * P + SUB], dg[0:64, 256:T1], True, True)
                t = PE.tick(m)
                tp = prep(256)
                odd = lambda a, b: a.rearrange("p (h b) t -> p b h t", b=2)[:, b]
                for b in range(2):
                    taken[4 + b] = ac([t], odd(at, b)[:, :, P:2 * P], bank[4 + b][:, 0:2 * P].rearrange("p (h t) -> p h t", h=2), ACT.Copy)
                taken[7] = ac([t], at[0:SUB, :, 416:432], bank[7][0:SUB, 0:4 * SUB].rearrange("p (h t) -> p h t", h=4), ACT.Copy)
                yield
                PE.wait(tp, taken[4], taken[5])
                for h in H:
                    for i in range(2):
                        a = (2 * i + h // 2) * SUB
                        m = mm(bank[4 + h % 2][:, a:a + SUB], kz[rows(h), h // 2, i * P:i * P + P], qz[rows(h), h // 2, 256:T1], True, True)
                t = PE.tick(m)
                for b in range(2):
                    for i, a in ((0, 256), (1, 400)):
                        taken[4 + b] = ac([t], odd(at, b)[:, :, a:a + SUB],
                                          bank[4 + b][:, 2 * SUB * i:2 * SUB * i + 2 * SUB].rearrange("p (h t) -> p h t", h=2), ACT.Copy)
                tk["at2"] = AC.now()
                yield

            def gla_outputs():
                o, sq = X[0][:, 0, :], X[0][:, 1, :]
                free = PE.now()
                for h in range(GLA_HEADS):
                    while ("gv", 3) not in tk or ("gr", h) not in tk:
                        yield
                    PE.wait(tk["at"], tk["at2"], taken[7], tk["gv", 3])
                    mm(bank[7][:, 0:T1], gv[:, 0, h * P:h * P + P], at[:, h, 0:T1], True, False)
                    mm(bank[7][:, P:T1], gv[:, 1, h * P:h * P + P], at[:, h, T1:416], False, False)
                    m = mm(bank[7][:, 256:T1], gv[0:16, 2, h * P:h * P + P], at[0:16, h, 416:432], False, True)
                    t = PE.tick(m)
                    t1 = ac([t, VE.now(), free], sq, bank[7][:, 0:T1], ACT.Square)
                    t2 = taken[7] = ve("copy", [t, t1], o, bank[7][:, 0:T1])
                    yield
                    PE.wait(t1, taken[4])
                    free = t = PE.tick(mm(bank[4][:, 0:T1], C("mean128"), sq, True, True))
                    t = taken[4] = rsqrt(sq, bank[4][:, 0:T1], [t])
                    t = ve("stt", [t, t2], o, o, gcur[:, 50 + h:51 + h], sq, ALU.mult, ALU.mult)
                    t = ve("tt", [t, tk["gr", h]], o, o, gr[:, h, :], ALU.mult)
                    to_pair(([ogp[0][:, h, :]], [ogp[1][:, h, :]]), 0, o, [t])

            def fox():
                units = []
                of_tok = {}

                def opener(pair, first):
                    def go():
                        if first:
                            PE.wait(taken[6])
                    return go

                def closer(pair, last):
                    def go(t):
                        if last:
                            taken[6] = to_pair(([ofp[0][:, pair, :]], [ofp[1][:, pair, :]]), 0, bank[6][:, 0:T1], [t])[1]
                    return go

                for pair in range(4):
                    for i, (t0, n) in enumerate(TOK_TILES1):
                        for hh in range(2):
                            h = 2 * pair + hh
                            W = t0 + n
                            rows = slice(64 * hh, 64 * hh + 64)
                            units.append(dict(
                                n=n, W=W, need=[tk["aug"], tk["fq", 2 * pair], tk["fk", 2 * pair]],
                                qk=[(qa[:, h, t0:t0 + n], ka[:, h, 0:W], W, 0)],
                                mask=C("causal")[0:n, 256 - t0:256 - t0 + W],
                                turn=[(s0, ns, st) for st, (s0, ns) in enumerate(TOK_TILES1[:i + 1])],
                                open=opener(pair, i == 0 and hh == 0), close=closer(pair, i == 2 and hh == 1),
                                pv=[(bank[6][rows, t0:t0 + n],
                                     [(st, ns, fv[0:ns, st, h * HD:h * HD + HD]) for st, (s0, ns) in enumerate(TOK_TILES1[:i + 1])])]))
                PE.wait(tk["fv", 3])
                yield from attention(units, (SS, PP, PT, small[:, 8:16]), (2, 2), (3, 3))

            drive(main(), [lazy(gla, tk, ("gk", 1)), lazy(fox, tk, ("fv", 3))])
            for b in range(2, 8):
                taken[b] = None
            PE.wait(VE.now(), AC.now())
            f_free = [None] * 4
            yt = [[None] * KD, [None] * KD]
            quarter = lambda wd, s: wd.rearrange("(k p) n -> p k n", p=P)[:, :, s * 256:s * 256 + 256]
            for s in range(4):
                ts = []
                for z, (name, o) in enumerate((("w_fox_o", ofp), ("w_gla_o", ogp))):
                    U = take(quarter(IN[name][L], s))
                    for c in range(2):
                        b = 4 * (s % 2) + 2 * c + z
                        PE.wait(f_free[b // 2])
                        m = products(bank[b][:, 0:T1], U, lambda k, part: U["w"][part][:, k, c * P:c * P + P],
                                     lambda k, part: o[part][:, k, :], n_k=4)
                        ts.append(ring.release(m) if c == 1 else PE.tick(m))
                for c in range(2):
                    d = 2 * s + c
                    a, bb = smh[:, d, :], smh[:, KD + d, :]
                    sa = ac([tk["m", d]], a, a, ACT.Sigmoid)
                    sb2 = ac([tk["m", KD + d]], bb, bb, ACT.Sigmoid)
                    b = 4 * (s % 2) + 2 * c
                    t1 = ve("tt", [ts[c], sa], a, bank[b][:, 0:T1], a, ALU.mult)
                    t2 = f_free[b // 2] = ve("tt", [ts[2 + c], sb2], bb, bank[b + 1][:, 0:T1], bb, ALU.mult)
                    t = ve("tt", [t2, t1], a, a, bb, ALU.add)
                    yt[0][d], yt[1][d] = to_pair(([xh[:, d, :]], [xl[:, d, :]]), 0, a, [t])
            done = []
            for d in range(KD):
                U = take(columns(IN["w_out"][L], d * P))
                PE.wait(f_free[d // 2])
                m = products(bank[d][:, 0:T1], U, lambda k, part: U["w"][part][:, k, :], x, toks=yt if d == 0 else None)
                done.append(ring.release(m))
            postnorm(done, gain(3), cols1, ybuf)
            lay.close()

        def rows_of(wd, f):
            return wd.rearrange("(f a p) n -> f p a n", p=P, a=1)[f]

        def lazy(gen, tk, key):
            while key not in tk:
                yield
            yield from gen()



        join()
        for ln in lanes:
            ln.seen = {}
        entry = {ln: ln.n for ln in lanes}
        ring.catch_up(AC, VE)
        r0 = (ring.loads, ring.splits, ring.freed)
        p0 = par_n[0]
        PAR_LAYER = 16 * (2 + 4 * FOX_HEADS)
        nc.disable_value_cache = True
        with nc.Fori(0, DEPTH) as L:
            act_set[0] = None
            share = nc.snap(L * PER_LAYER)
            for ln in lanes:
                ln.loop = share
            ring.loop = nc.snap(L * UNITS_PER_LAYER)
            ring.loop16 = nc.snap(L * (16 * UNITS_PER_LAYER // RING))
            par_n[1] = nc.snap(L * PAR_LAYER)
            for ln in lanes:
                ln.wait(*[o.at(entry[o]) for o in lanes if o is not ln])
            for k in range(KD):
                h_tok[k] = VE.at(entry[VE])
            for b in range(8):
                taken[b] = None
            par_load(wau[:, :], IN["w_alpha_up"][L])
            par_load(small[0:FOX_HEADS, 0:1], IN["b_f"][L].rearrange("(p a) -> p a", a=1), slow=True)
            ve("copy", [], gcur[:, 0:48].rearrange("p (g k) -> p g k", g=6),
               gain1[:, 0:96].rearrange("p (g l k) -> p l g k", g=6, l=2)[:, L])
            ve("copy", [], gcur[:, 48:50], gain1[:, 96:100].rearrange("p (l k) -> p l k", l=2)[:, L])
            ve("copy", [], gcur[:, 50:54], gain1[:, 100:108].rearrange("p (l k) -> p l k", l=2)[:, L])
            PE.wait(par_all())
            VE.wait(par_all(), VE.now())
            AC.wait(VE.now())
            g = lambda i: (lambda k: gcur[:, 8 * i + k:8 * i + k + 1])

            def gu1(name):
                w = IN[name][L].rearrange("(k p) n -> p k n", p=P)
                return [lambda i, j, c=c: w[:, :, bass.ds(i * (2 * P) + (c + j * P), P)] for c in (0, D_FF)]

            ffn(*gu1("w_ffn1_gu"), lambda f: rows_of(IN["w_ffn1_down"][L], f), g(0), cols1, g(1))
            join()
            mixer1(L)
            join()
            ffn(*gu1("w_ffn2_gu"), lambda f: rows_of(IN["w_ffn2_down"][L], f), g(4), cols1, g(5))
            join()
            for ln in lanes:
                spent = ln.n - entry[ln]
                assert 0 < spent < PER_LAYER, spent
                ln.eng.wait_ge(ln.sem, ln.loop + ln.n)
                ln.eng.sem_inc(ln.sem, PER_LAYER - spent)
                ln.open = False
            assert ring.loads - r0[0] == ring.splits - r0[1] == ring.freed - r0[2] == UNITS_PER_LAYER, ring.loads
            assert par_n[0] - p0 == PAR_LAYER
        for ln in lanes:
            ln.n, ln.loop, ln.seen = entry[ln] + DEPTH * PER_LAYER, 0, {}
        act_set[0] = None
        ring.loads, ring.splits, ring.freed = (r + DEPTH * UNITS_PER_LAYER for r in r0)
        ring.loop = ring.loop16 = 0
        par_n[0], par_n[1] = p0 + DEPTH * PAR_LAYER, 0
        join()
        for ln in lanes:
            ln.wait(*[o.now() for o in lanes if o is not ln])
        for k in range(KD):
            h_tok[k] = None

        cols2 = (N_META, T1)
        T = SEQ
        keep = Scope()
        memR = keep.take(KD, T)
        k_sh = keep.take(6, T)
        v_sh = keep.take(2, DIL_W)
        start = Scope()
        ms = start.take(2, D)
        par_load(ms, IN["mem_2"][0].rearrange("(t p) d -> p t d", p=P))
        PE.wait(par_all())
        saved = list(h_tok)
        turn_rows(ms, P, 0, memR, 0)
        turn_rows(ms, P, 1, memR, P)
        mt = list(h_tok)
        for k in range(KD):
            h_tok[k] = saved[k]
        t = squares(memR, mt, (0, T), range(KD), ve)
        stats(t, (0, T), 0)
        for k in range(KD):
            ve("tt", [rtok[0]], memR[:, k, :], memR[:, k, :], rst[:, 0:T], ALU.mult)
        join()
        start.close()

        def gcol2(i):
            return lambda k: gain2[:, 8 * i + k:8 * i + k + 1]

        def ffn2(pre, l, gi):
            wg = IN[pre + "_w_gate_2"][l].rearrange("(k p) n -> p k n", p=P)
            wu = IN[pre + "_w_up_2"][l].rearrange("(k p) n -> p k n", p=P)
            at = lambda w: (lambda i, j: w[:, :, bass.ds(i * (2 * P) + j * P, P)])
            ffn(at(wg), at(wu), lambda f: rows_of(IN[pre + "_w_down_2"][l], f), gcol2(gi), cols2, None)

        def headnorm_steps(items, zb, scaled=True):
            sb2 = [sqb[:, 0, 0:T], sqb[:, 1, 0:T]]
            pend = None
            out_free = [None, None]
            for i, (make, gaincol, dst) in enumerate(list(items) + [(None, None, None)]):
                new = None
                if make is not None:
                    z = i % 2
                    b, t = make()
                    if scaled:
                        t2 = taken[b] = ve("tt", [t, rtok[0], out_free[z]], zb[z], bank[b][:, 0:T], rst[:, N_META:T1], ALU.mult)
                    else:
                        t2 = taken[b] = ve("copy", [t, out_free[z]], zb[z], bank[b][:, 0:T])
                    t1 = ac([t2], sb2[z], zb[z], ACT.Square)
                    new = (z, t1, t2, gaincol, dst)
                if pend is not None:
                    z, t1, t2, gc, dst = pend
                    PE.wait(t1, taken[7])
                    t = PE.tick(mm(bank[7][:, 0:T], C("mean64"), sb2[z], True, True))
                    t = taken[7] = rsqrt(sb2[z], bank[7][:, 0:T], [t])
                    out_free[z] = t = ve("stt", [t, t2], dst, zb[z], gc, sb2[z], ALU.mult, ALU.mult)
                pend = new
                yield

        def memory_kv(l, mem, kmem, vmem, zb):
            for k in range(KD):
                to_pair(([mem[0][:, k, :]], [mem[1][:, k, :]]), 0, memR[:, k, :], [], gain2[:, 48 + 8 * l + k:49 + 8 * l + k])
            PE.wait(AC.now(), VE.now())
            xm = lambda k, part: mem[part][:, k, :]
            mk = lambda c: (lambda: project(take(columns(IN["w_mem_kv_2"][l], c * P)), xm, T))
            yield from headnorm_steps([(mk(c), gain2[:, 74 + l:75 + l], kmem[:, c, :]) for c in range(2)], zb, scaled=False)
            val = lambda s: (lambda: project(take(columns(IN["w_mem_kv_2"][l], MEM_W + s * P)), xm, T), None,
                             [vmem[:, i, s * P:s * P + P] for i in range(2)], lambda t: None)
            yield from turned_steps([val(s) for s in range(2)], zb, TOK_TILES2, 7)

        def memory_units(qmem, kmem, vmem, hm, tk_out):
            units = []

            def opener(pair, first):
                def go():
                    if first:
                        PE.wait(taken[6])
                return go

            def closer(pair, last):
                def go(t):
                    if last:
                        taken[6] = to_pair(([hm[0][:, pair, :]], [hm[1][:, pair, :]]), 0, bank[6][:, 0:T], [t])[1]
                return go

            for pair in range(2):
                for i, (t0, n) in enumerate(TOK_TILES2):
                    for hh in range(2):
                        h = 2 * pair + hh
                        rows = slice(64 * hh, 64 * hh + 64)
                        units.append(dict(
                            n=n, W=T, need=[], qk=[(qmem[rows, pair, t0:t0 + n], kmem[rows, pair, :], T, 0)], mask=None,
                            turn=[(0, P, 0), (P, P, 1)], open=opener(pair, i == 0 and hh == 0),
                            close=closer(pair, i == 1 and hh == 1),
                            pv=[(bank[6][rows, t0:t0 + n], [(st, P, vmem[:, st, h * HD:h * HD + HD]) for st in range(2)])]))
            return units

        def free_bank_add(d, b, t):
            h_tok[d] = taken[b] = ve("tt", [t], hT[:, d, N_META:T1], bank[b][:, 0:T], hT[:, d, N_META:T1], ALU.add)

        def mixer2a():
            lay = Scope()
            qk = lay.take(16, T)
            v = lay.take(2, ML_W)
            og = lay.take(8, T)
            cellp = lay.pair(8, T)
            hm = lay.pair(2, T)
            kmem, qmem = lay.take(2, T), lay.take(2, T)
            vmem = lay.take(2, 256)
            xb = [lay.take(T + 4), lay.take(T + 4)]
            rowg = lay.take(4, T)
            memp = lay.pair(KD, T)
            WT = [[lay.take(T), lay.take(T)] for _ in range(2)]
            tmp = lay.take(3, T)
            sg = lay.take(2, T)
            w_in = IN["a_w_in_2"][0]
            R = slice(0, MH)
            x = xin(cols2)
            norm_in(gcol2(4), cols2)
            tz = [po("memset", [], xb[z][0:MH, 0:3], 0.0) for z in range(2)]
            par_load(small[0:4, 0:2], IN["a_gate_bias_2"][0].rearrange("(a p) -> p a", p=4), slow=True)
            tk = {}
            H4 = slice(0, ML_HEADS)

            def main():
                U = take(columns(w_in, 4 * ML_W))
                tq = squares(hT, h_tok, cols2, range(KD), ve)
                b0, t0_ = project(U, x, T, last=False, toks=xt)
                b1, t1_ = project(U, x, T, M=P - 4, c=4)
                stats(tq, cols2, 7)
                taken[7] = VE.now()
                VE.wait(par_all(), rtok[0])
                for g, b, t in ((0, b0, t0_), (1, b1, t1_)):
                    t = taken[b] = ve("tt", [t], rowg[H4, g, :], bank[b][H4, 0:T], rst[H4, N_META:T1], ALU.mult)
                    tk["g", g] = ve("ts", [t], rowg[H4, g, :], rowg[H4, g, :], small[H4, g:g + 1], None, ALU.add)
                ci, cf, mu, em = (rowg[H4, x, :] for x in range(4))
                t = log_sigmoid(cf, cf, mu, [tk["g", 1]])
                t = ve("scan", [t], cf, C("ones")[H4, 0:T], cf, 0.0, ALU.mult, ALU.add)
                t = ve("tt", [t, tk["g", 0]], ci, ci, cf, ALU.subtract)
                t = ve("scan", [t], mu, C("ones")[H4, 0:T], ci, 0.0, ALU.mult, ALU.max)
                t = ve("tt", [t], em, cf, mu, ALU.add)
                tk["em"] = ac([t], em, em, ACT.Exp, scale=-1.0)
                tk["mu"] = ve("ts", [t], mu, mu, -1.0, None, ALU.mult)
                yield
                prev = [None, None]
                for i in range(16):
                    z = i % 2
                    b, t = project(take(columns(w_in, i * MH, MH)), x, T, M=MH)
                    t = taken[b] = ve("tt", [t, tz[z], prev[z]], xb[z][R, 3:3 + T], bank[b][R, 0:T], rst[R, N_META:T1], ALU.mult)
                    tap = lambda j: gain3[:, 8 + 16 * j + i:9 + 16 * j + i]
                    y = qk[R, i, :]
                    t = ve("ts", [t], y, xb[z][R, 0:T], tap(0), None, ALU.mult)
                    for j in range(1, 4):
                        t = prev[z] = ve("stt", [t], y, xb[z][R, j:j + T], tap(j), y, ALU.mult, ALU.add)
                    tk["qk", i] = ac([t], y, y, ACT.Silu)
                    yield
                def value(s):
                    def done(t):
                        tk["v"] = t
                    return (lambda: project(take(columns(w_in, 2 * ML_W + s * P)), x, T), rst[:, N_META:T1],
                            [v[:, i, s * P:s * P + P] for i in range(2)], done)
                yield from turned_steps([value(s) for s in range(6)], (xb[0][:, 0:T], xb[1][:, 0:T]), TOK_TILES2, 7)
                for i in range(8):
                    b, t = project(take(columns(w_in, 3 * ML_W + i * MH, MH)), x, T, M=MH)
                    t = taken[b] = ve("tt", [t], og[R, i, :], bank[b][R, 0:T], rst[R, N_META:T1], ALU.mult)
                    t = ac([t], og[R, i, :], og[R, i, :], ACT.Exp, scale=-1.0)
                    t = ve("ts", [t], og[R, i, :], og[R, i, :], 1.0, None, ALU.add)
                    tk["o", i] = ve("recip", [t], og[R, i, :], og[R, i, :])
                    yield
                z2 = (xb[0][:, 0:T], xb[1][:, 0:T])
                mk = lambda c: (lambda: project(take(columns(w_in, 4 * ML_W + 2 * ML_HEADS + c * P)), x, T))
                yield from headnorm_steps([(mk(c), gain2[:, 72:73], qmem[:, c, :]) for c in range(2)], z2)
                yield from memory_kv(0, memp, kmem, vmem, z2)

            def cells():
                for _ in range(24):
                    yield
                PE.wait(tk["mu"], taken[6])
                for i, (c0, n) in enumerate(TOK_TILES2):
                    m = nc.tensor.transpose(bank[6][:, 4 * i:4 * i + 4], rowg[H4, 0, c0:c0 + n], ident[0:4, 0:4])
                t = PE.tick(m)
                tcs = taken[6] = ve("copy", [t], small[:, 16:24], bank[6][:, 0:8])
                wt_free = [None, None]
                for h in range(ML_HEADS):
                    z = h % 2
                    sel = C("sel")[H4, h * P:h * P + P]
                    PE.wait(tk["em"], tk["mu"], taken[2])
                    t = PE.tick(mm(bank[2][:, 0:T], sel, rowg[H4, 2, :], True, True))
                    for s, (s0, n) in enumerate(TOK_TILES2):
                        wv = WT[z][s][:, s0:T]
                        t1 = taken[2] = ve("stt", [t, tcs, wt_free[z]], wv, bank[2][:, s0:T], small[:, 16 + 4 * s + h:17 + 4 * s + h],
                                           C("causalT")[:, 0:T - s0], ALU.add, ALU.min)
                        t1 = ac([t1], wv, wv, ACT.Exp)
                        PE.wait(taken[3], tk["qk", 2 * h + 1], tk["qk", 8 + 2 * h + 1])
                        for c in range(2):
                            m = mm(bank[3][:, s0:T], qk[R, 8 + 2 * h + c, s0:s0 + n], qk[R, 2 * h + c, s0:T], c == 0, c == 1)
                        tp = PE.tick(m)
                        taken[3] = tw = ve("stt", [t1, tp], wv, wv, ML_DK ** -0.5, bank[3][:, s0:T], ALU.mult, ALU.mult)
                        PE.wait(tw)
                    yield
                    PE.wait(tk["v"], taken[4], taken[5], taken[7])
                    def sums(o, lhs):
                        mm(o[R, 0:T], lhs(0), WT[z][0][:, 0:T], True, False)
                        return mm(o[R, P:T], lhs(1), WT[z][1][:, P:T], False, True)
                    sums(bank[4], lambda s: v[:, s, h * ML_DK:h * ML_DK + MH])
                    sums(bank[5], lambda s: v[:, s, h * ML_DK + MH:h * ML_DK + ML_DK])
                    m = sums(bank[7], lambda s: C("ones")[:, 0:MH])
                    tn = PE.tick(m)
                    wt_free[z] = tn
                    PE.wait(taken[6])
                    t = PE.tick(mm(bank[6][R, 0:T], sel[:, 0:MH], rowg[H4, 3, :], True, True))
                    den = tmp[R, 2, :]
                    t = taken[6] = ac([t, VE.now()], den, bank[6][R, 0:T], ACT.Copy)
                    t = taken[7] = ac([tn], tmp[R, 0, :], bank[7][R, 0:T], ACT.Abs)
                    t = ve("tt", [t], den, den, tmp[R, 0, :], ALU.max)
                    t = ve("recip", [t], den, den)
                    cell = [sg[R, 0, 0:T], sg[R, 1, 0:T]]
                    taken[4] = ve("tt", [t, c_free[0]], cell[0], bank[4][R, 0:T], den, ALU.mult)
                    taken[5] = tc = ve("tt", [t], cell[1], bank[5][R, 0:T], den, ALU.mult)
                    sq = [WT[z][0][R, 0:T], WT[z][1][R, 0:T]]
                    for c in range(2):
                        t = ac([tc, tn], sq[c], cell[c], ACT.Square)
                        PE.wait(t, taken[6])
                        m = mm(bank[6][R, 0:T], C("mean192")[R, 0:MH], sq[c], c == 0, c == 1)
                    wt_free[z] = t = PE.tick(m)
                    t = taken[6] = rsqrt(den, bank[6][R, 0:T], [t])
                    for c in range(2):
                        i = 2 * h + c
                        while ("o", i) not in tk:
                            yield
                        t1 = ve("stt", [t, tc], cell[c], cell[c], gain3[:, i:i + 1], den, ALU.mult, ALU.mult)
                        t1 = ve("tt", [t1, tk["o", i]], og[R, i, :], og[R, i, :], cell[c], ALU.mult)
                        to_pair(([cellp[0][R, i, :]], [cellp[1][R, i, :]]), 0, og[R, i, :], [t1])
                        c_free[0] = VE.now()
                    yield

            c_free = [None]
            drive(main(), [cells()])
            hmt = {}
            bufs = ([WT[0][0], WT[0][1]], [WT[1][0], WT[1][1]], [xb[0][:, 0:T], xb[1][:, 0:T]], small[:, 8:16])
            join()
            for _ in attention(memory_units(qmem, kmem, vmem, hm, hmt), bufs, (2, 3), (4, 5)):
                pass
            w_out = IN["a_w_out_2"][0]
            PE.wait(AC.now(), VE.now())
            for s in range(4):
                UM = take(w_out[ML_W:D, s * 256:s * 256 + 256].rearrange("(k p) n -> p k n", p=P))
                bs = [next_bank(), next_bank()]
                for c in range(2):
                    m = products(bank[bs[c]][:, 0:T], UM, lambda k, part: UM["w"][part][:, k, c * P:c * P + P],
                                 lambda k, part: hm[part][:, k, :], n_k=2, stop=False)
                ring.release(m)
                for c in range(2):
                    d = 2 * s + c
                    U = take(w_out[0:ML_W, d * P:d * P + P].rearrange("(k p) n -> p k n", p=MH), rows=MH)
                    m = products(bank[bs[c]][:, 0:T], U, lambda k, part: U["w"][part][:, k, :],
                                 lambda k, part: cellp[part][R, k, :], start=False)
                    free_bank_add(d, bs[c], ring.release(m))
            lay.close()

        def shared_kv():
            w_kv = IN["w_kv_2"]
            x = xin(cols2)
            lay = Scope()
            zb = (lay.take(T), lay.take(T))
            norm_in(lambda k: gain2[:, 64 + k:65 + k], cols2)
            make = first_of(lambda c: take(columns(w_kv, c * P)), x)
            for i, _ in enumerate(headnorm_steps([(make(c), gain2[:, 77:78], k_sh[:, c, :]) for c in range(6)], zb)):
                pass
            val = lambda s: (lambda: project(take(columns(w_kv, DIL_W + s * P)), x, T), rst[:, N_META:T1],
                             [v_sh[:, i, s * P:s * P + P] for i in range(2)], lambda t: None)
            for _ in turned_steps([val(s) for s in range(6)], zb, TOK_TILES2, 7):
                pass
            lay.close()

        def first_of(unit, x):
            def make(c):
                def go():
                    if c == 0:
                        U = unit(0)
                        tq = squares(hT, h_tok, cols2, range(KD), ve)
                        r = project(U, x, T, toks=xt)
                        stats(tq, cols2, 7)
                        taken[7] = VE.now()
                        return r
                    return project(unit(c), x, T)
                return go
            return make

        bias_rows = IN["scratch"]

        def mixer2b():
            lay = Scope()
            q = lay.take(8, T)
            bias = lay.take(12, T)
            hd = lay.pair(6, T)
            hm = lay.pair(2, T)
            kmem = lay.take(2, T)
            vmem = lay.take(2, 256)
            memp = lay.pair(KD, T)
            SS = [lay.take(3 * T), lay.take(3 * T)]
            PP = [lay.take(3 * T)] * 2
            PT = [lay.take(3 * T), lay.take(3 * T)]
            ohv = lay.take(1536)[0:BUCKETS + 1, :]
            x = xin(cols2)
            tab = small[0:BUCKETS + 1, 32:44]
            norm_in(gcol2(5), cols2)
            t = po("memset", [], small[:, 32:44], NEG)
            par_load(small[0:BUCKETS, 32:44], IN["rel_bias_2"], [t])
            par_load(ohv, IN["onehot"])
            PE.wait(par_all())
            tabb = rst2[0:BUCKETS + 1, 0:P]
            VE.wait(par_all())
            for h in range(12):
                g = h // 4
                b = next_bank()
                tt = ve("ts", [PE.now()], tabb, C("ones")[0:BUCKETS + 1, 0:P], small[0:BUCKETS + 1, 32 + h:33 + h], None, ALU.mult)
                PE.wait(tt)
                t = PE.tick(mm(bank[b][:, :], tabb, ohv[:, 512 * g:512 * g + 512], True, True))
                st = bias[:, 2 * (h % 6):2 * (h % 6) + 2, :].rearrange("p a b -> p (a b)")
                if h >= 6:
                    AC.wait((s_bias, 0, 16 * 6))
                taken[b] = ac([t], st, bank[b][:, :], ACT.Copy)
                nc.scalar.wait_ge(AC.sem, AC.n)
                nc.scalar.dma_start(bias_rows[h], st).then_inc(s_bias, 16)
            PO.wait((s_bias, 0, 16 * 12))
            for h in range(12):
                src = bias_rows[h].rearrange("p u -> (p u)")[0:P * 511].rearrange("(p u) -> p u", u=511)[:, 127:127 + T]
                par_load(bias[:, h, :], src)
            tk_bias = par_all()

            make = first_of(lambda c: take(columns(IN["b_w_q_2"][0], c * P)), x)
            zb = (SS[0][:, 0:T], SS[1][:, 0:T])
            items = [(make(c), gain2[:, 76:77] if c < 6 else gain2[:, 73:74], q[:, c, :]) for c in range(8)]
            for _ in headnorm_steps(items, zb):
                pass
            for _ in memory_kv(1, memp, kmem, vmem, zb):
                pass
            join()
            for b in range(8):
                taken[b] = None
            VE.wait(tk_bias)
            for hh_ in range(DIL_HEADS):
                for i, (t0, n) in enumerate(TOK_TILES2):
                    W = t0 + n
                    z = i
                    rows = slice(64 * (hh_ % 2), 64 * (hh_ % 2) + 64)
                    pair = hh_ // 2
                    PE.wait(AC.now(), VE.now())
                    for g in range(3):
                        m = mm(bank[g][0:n, 0:W], q[rows, 2 * g + pair, t0:t0 + n], k_sh[rows, 2 * g + pair, 0:W], True, True)
                    t = PE.tick(m)
                    for g in range(3):
                        tt = ve("tt", [t], SS[z][:, g * W:g * W + W], bank[g][:, 0:W], bias[:, 4 * g + hh_, T - W:T], ALU.add)
                    mx, nm, den, rd = (small[:, 8 + x:9 + x] for x in range(4))
                    t = ve("rmax", [tt], mx, SS[z][:, 0:3 * W], AX_X)
                    t = ve("ts", [t], nm, mx, -1.0, None, ALU.mult)
                    t = ac([t, PE.now()], PP[z][:, 0:3 * W], SS[z][:, 0:3 * W], ACT.Exp, bias=nm, accum_out=den)
                    t = ve("recip", [t], rd, den)
                    t = ve("ts", [t], PP[z][:, 0:3 * W], PP[z][:, 0:3 * W], rd, None, ALU.mult)
                    PE.wait(t)
                    ns = W // P
                    for s in range(3 * ns):
                        m = nc.tensor.transpose(bank[4 + s // 4][:, (s % 4) * P:(s % 4) * P + P], PP[z][:, s * P:s * P + P], ident)
                    t = PE.tick(m)
                    nt = 3 * ns
                    tc = ac([t], PT[z][:, 0:min(nt, 4) * P], bank[4][:, 0:min(nt, 4) * P], ACT.Copy)
                    if nt > 4:
                        tc = ac([], PT[z][:, 4 * P:nt * P], bank[5][:, 0:(nt - 4) * P], ACT.Copy)
                    PE.wait(tc, taken[6], taken[7], taken[3])
                    for g in range(3):
                        o = (bank[6], bank[7], bank[3])[g]
                        for s in range(ns):
                            m = mm(o[rows, t0:t0 + n], v_sh[:, s, (4 * g + hh_) * HD:(4 * g + hh_) * HD + HD],
                                   PT[z][:, (g * ns + s) * P:(g * ns + s) * P + P], s == 0, s == ns - 1)
                    t = PE.tick(m)
                    if hh_ % 2 == 1 and i == 1:
                        for g in range(3):
                            o = (bank[6], bank[7], bank[3])[g]
                            taken[(6, 7, 3)[g]] = to_pair(([hd[0][:, 2 * g + pair, :]], [hd[1][:, 2 * g + pair, :]]), 0, o[:, 0:T], [t])[1]
            join()
            for b in range(8):
                taken[b] = None
            hmt = {}
            bufs = ([SS[0], SS[1]], [PP[0][:, 0:T], PP[0][:, T:2 * T]], PT, small[:, 8:16])
            for _ in attention(memory_units(q[:, 6:8, :], kmem, vmem, hm, hmt), bufs, (2, 3), (4, 5)):
                pass
            PE.wait(AC.now(), VE.now())
            for d in range(KD):
                b, t = project(take(columns(IN["b_w_out_2"][0], d * P)),
                               lambda k, part: hd[part][:, k, :] if k < 6 else hm[part][:, k - 6, :], T)
                free_bank_add(d, b, t)
            lay.close()

        ffn2("ffn1", 0, 0)
        join()
        mixer2a()
        join()
        ffn2("ffn2", 0, 2)
        join()
        shared_kv()
        join()
        ffn2("ffn1", 1, 1)
        join()
        mixer2b()
        join()
        ffn2("ffn2", 1, 3)

        join()
        lay = Scope()
        obuf = lay.take(2, D)
        for i in range(2):
            ov = obuf[:, i, :]
            for k in range(KD):
                b = k % 4
                PE.wait(h_tok[k], taken[b] if i or k >= 4 else None)
                t = PE.tick(nc.tensor.transpose(bank[b][:, 0:P], hT[:, k, N_META + i * P:N_META + i * P + P], ident))
                taken[b] = ve("copy", [t], ov[:, k * P:k * P + P], bank[b][:, 0:P])
            nc.sync.wait_ge(VE.sem, VE.n)
            nc.sync.dma_start(out[0, i * P:i * P + P, :], ov).then_inc(s_out, 16)
        nc.sync.wait_ge(s_out, 32)
        assert ring.loads == ring.splits == UNITS
        lay.close()
        keep.close()


_SHAPE = (1, SEQ, D)


def kernel(**inputs):
    import numpy as _np
    import concourse.bacc as _bacc
    from concourse import mybir as _mybir
    from concourse.bass_utils import run_bass_kernel_spmd as _run

    nc = _bacc.Bacc("TRN2", target_bir_lowering=False, num_devices=1)
    arrays, args = {}, {}
    given = dict(inputs)
    given["consts"] = constants()
    given["onehot"] = bucket_rows()
    for name, value in given.items():
        a = _np.ascontiguousarray(value)
        arrays[f"in_{name}"] = a
        args[name] = nc.dram_tensor(f"in_{name}", a.shape, _mybir.dt.from_np(a.dtype), kind="ExternalInput").ap()
    args["scratch"] = nc.dram_tensor("bias_scratch", (12, P, 512), F32).ap()
    out = nc.dram_tensor("out_0", _SHAPE, F32, kind="ExternalOutput").ap()
    program(nc, args, out)
    r = _run(nc, [arrays], core_ids=[0])
    return r.results[0]["out_0"]
```

```python
import math
from contextlib import ExitStack

import numpy as np

import concourse.bass as bass
from concourse import mybir

F32 = mybir.dt.float32
F32R = mybir.dt.float32r
ALU = mybir.AluOpType
ACT = mybir.ActivationFunctionType
AX_X = mybir.AxisListType.X

P = 128
D = 1024
KD = D // P
SEQ = 256
N_META = 16
T1 = N_META + SEQ
DEPTH = 2
D_FF = 2816
NF = D_FF // P
EPS = 1e-6
NEG = -1e30
RING = 4
SLOT = 1024
LEAD = 3
TURNS = NF // 2
assert NF % 2 == 0 and RING == 4
UNITS_PER_LAYER = 192
UNITS = DEPTH * UNITS_PER_LAYER + 4 * 3 * NF + 49 + 12 + 20
assert UNITS_PER_LAYER % RING == 0

FOX_HEADS, HD = 8, 64
FOX_W = FOX_HEADS * HD
GLA_HEADS, GLA_DK, GLA_DV = 4, 64, 128
GLA_KW, GLA_W, GATE_RANK = GLA_HEADS * GLA_DK, GLA_HEADS * GLA_DV, 16
SUB = 16
N_SUB = T1 // SUB
SPLIT = (FOX_W, FOX_W, FOX_W, FOX_HEADS, GLA_KW, GLA_KW, GLA_W, GATE_RANK, GLA_W, D, D)
SPLIT_AT = [sum(SPLIT[:i]) for i in range(len(SPLIT))]

ML_HEADS, ML_DK = 4, 192
ML_W = ML_HEADS * ML_DK
MH = ML_DK // 2
MEM_W = 256
DIL_GROUPS = ((128, 1), (512, 4), (2048, 16))
DIL_HEADS = 4
DIL_W = 3 * DIL_HEADS * HD
BUCKETS, MAX_DIST = 32, 2048

TOK_TILES1 = [(0, 128), (128, 128), (256, 16)]
TOK_TILES2 = [(0, 128), (128, 128)]


CONST_W = [("ident", 128), ("mean1024", 128), ("mean128", 128), ("mean64", 128), ("mean192", 128), ("ones", T1),
           ("causal", 384), ("causalT", 256), ("pickd", 2 * 80), ("rep", GLA_HEADS * 128), ("blocks", 4 * 128),
           ("sel", 4 * 128)]
CONST_AT = {}
_at = 0
for _n, _w in CONST_W:
    CONST_AT[_n] = (_at, _w)
    _at += _w
CONST_N = _at


def constants():
    c = {n: np.zeros((P, w), np.float32) for n, w in CONST_W}
    p = np.arange(P)
    c["ident"][p, p] = 1.0
    c["mean1024"][:] = 1.0 / D
    c["mean128"][:] = 1.0 / GLA_DV
    c["mean64"][:] = (p[:, None] // HD == p[None, :] // HD) / HD
    c["mean192"][:] = 1.0 / ML_DK
    c["ones"][:] = 1.0
    c["causal"][:] = np.where(np.arange(384)[None, :] <= p[:, None] + 256, 0.0, NEG)
    c["causalT"][:] = np.where(np.arange(256)[None, :] >= p[:, None], 0.0, NEG)
    for ct in range(2):
        for half in range(2):
            c["pickd"][half * 64:half * 64 + 64, ct * 80 + 15 + 16 * (2 * ct + half)] = 1.0
    for h in range(GLA_HEADS):
        for j in range(SUB):
            c["rep"][16 * h + j, 128 * h + j:128 * h + 128:SUB] = 1.0
    t = np.arange(128)
    c["blocks"][:, 0:128] = p[:, None] // SUB == t[None, :] // SUB
    for l in range(1, 4):
        ps, pt = p[:, None] // (8 << l), t[None, :] // (8 << l)
        c["blocks"][:, 128 * l:128 * l + 128] = (pt % 2 == 1) & (ps == pt - 1)
    for h in range(4):
        c["sel"][h, 128 * h:128 * h + 128] = 1.0
    return np.ascontiguousarray(np.concatenate([c[n] for n, _ in CONST_W], axis=1))


def bucket_rows():
    oh = np.zeros((BUCKETS + 1, 3 * 512), np.float32)
    for g, (window, dil) in enumerate(DIL_GROUPS):
        for u in range(512):
            d = 255 - u
            if d < 0 or d % dil or d > window:
                b = BUCKETS
            elif d < BUCKETS // 2:
                b = d
            else:
                e = BUCKETS // 2
                b = min(e + int(math.log(d / e) / math.log(MAX_DIST / e) * (BUCKETS - e)), BUCKETS - 1)
            oh[b, 512 * g + u] = 1.0
    return oh


class Lane:

    def __init__(self, name, eng, sem, spare):
        self.name, self.eng, self.sem = name, eng, sem
        self.n = 0
        self.open = False
        self.spare = spare
        self.loop = 0
        self.seen = {}

    def at(self, n):
        return (self.sem, self.loop, n)

    def now(self):
        return self.at(self.n)

    def wait(self, *toks):
        for tok in toks:
            if tok is None:
                continue
            sem, loop, n = tok
            if isinstance(loop, int) and loop + n <= 0:
                continue
            key = sem.name
            if self.seen.get(key, -10 ** 9) >= n:
                continue
            self.seen[key] = n
            self.eng.wait_ge(sem, loop + n)
            self.open = not isinstance(loop, int)

    def settle(self):
        if self.open:
            self.eng.sem_inc(self.spare, 1)
            self.open = False

    def tick(self, ins):
        ins.then_inc(self.sem, 1)
        self.n += 1
        return self.now()


class Ring:

    def __init__(self, nc, raw, hi, lo, full, hi_ready, lo_ready, used, spare):
        self.nc, self.raw, self.hi, self.lo = nc, raw, hi, lo
        self.full, self.hi_ready, self.lo_ready, self.used, self.spare = full, hi_ready, lo_ready, used, spare
        self.loads = self.splits = self.freed = 0
        self.loop = self.loop_slot = self.loop16 = 0
        self.hold = False

    def split(self, AC, VE, PO):
        n, slot = self.splits, self.splits % RING
        AC.wait((self.full[slot], self.loop16, 16 * (n // RING + 1)), (self.used, self.loop, n + 1))
        self.nc.scalar.activation(self.hi[:, slot, :], self.raw[:, slot, :], ACT.Copy).then_inc(self.hi_ready, 1)
        lane = PO if slot == RING - 1 else VE
        lane.wait((self.hi_ready, self.loop, n + 1))
        if lane is PO:
            lane.settle()
        lane.eng.tensor_tensor(self.lo[:, slot, :], self.raw[:, slot, :], self.hi[:, slot, :].bitcast(F32),
                               ALU.subtract).then_inc(self.lo_ready[slot], 1)
        self.splits += 1

    def catch_up(self, AC, VE, PO, count=None):
        while self.splits < min(self.loads + LEAD, self.limit) and count != 0:
            self.split(AC, VE, PO)
            count = None if count is None else count - 1

    def take(self, src, AC, VE, PO, rows=P):
        n, slot = self.loads, self.loads % RING
        a, b = src.shape[1], src.shape[2]

        def view(t):
            return t[0:rows, slot, 0:a * b].rearrange("p (a b) -> p a b", a=a)

        self.nc.sync.wait_ge(self.lo_ready[slot], self.loop_slot + n // RING + 1)
        if not isinstance(self.loop, int):
            self.nc.sync.sem_inc(self.spare, 1)
        self.nc.sync.dma_start(view(self.raw), src).then_inc(self.full[slot], 16)
        self.loads += 1
        if not self.hold:
            self.catch_up(AC, VE, PO)
        return dict(w=(view(self.hi), view(self.lo)), hi=(self.hi_ready, self.loop, n + 1),
                    lo=(self.lo_ready[slot], self.loop_slot, n // RING + 2))

    def release(self, ins):
        ins.then_inc(self.used, 1)
        self.freed += 1
        return (self.used, self.loop, RING + self.freed)


def program(nc, IN, out):
    ctx = ExitStack()
    with ctx:
        def sb(name, shape, dt=F32):
            return ctx.enter_context(nc.sbuf_tensor(name, shape, dt))

        def sem(name):
            return ctx.enter_context(nc.semaphore(name))

        bank = [ctx.enter_context(nc.psum_tensor(f"bank{i}", [P, 512], F32)) for i in range(8)]
        wraw = sb("wraw", [P, RING, SLOT])
        whi = sb("whi", [P, RING, SLOT], F32R)
        wlo = sb("wlo", [P, RING, SLOT], F32R)
        hT = sb("hT", [P, KD, T1])
        xh, xl = sb("xhi", [P, KD, T1], F32R), sb("xlo", [P, KD, T1], F32R)
        rst = sb("rst", [P, T1])
        rst2 = sb("rst2", [P, T1])
        ry = sb("ry", [P, T1])
        eps = sb("eps", [P, 1])
        ssum = sb("ssum", [P, T1])
        sqb = sb("sqb", [P, 2, T1])
        cst = sb("cst", [P, CONST_N])
        gain1 = sb("gain1", [P, 108])
        gain2 = sb("gain2", [P, 80])
        gain3 = sb("gain3", [MH, 72])
        gcur = sb("gcur", [P, 56])
        small = sb("small", [P, 64])
        wau = sb("wau", [GATE_RANK, GLA_KW])

        def C(name):
            a, w = CONST_AT[name]
            return cst[:, a:a + w]

        full = [sem(f"full{i}") for i in range(RING)]
        hi_ready, used = sem("hi_ready"), sem("used")
        lo_ready = [sem(f"lo_ready{i}") for i in range(RING)]
        par = sem("par")
        s_in = sem("s_in")
        s_bias = sem("s_bias")
        s_aug = sem("s_aug")
        s_out = sem("s_out")
        spare = sem("spare")
        PE = Lane("pe", nc.tensor, sem("pe_done"), spare)
        AC = Lane("act", nc.scalar, sem("act_done"), spare)
        VE = Lane("dve", nc.vector, sem("dve_done"), spare)
        PO = Lane("pool", nc.gpsimd, sem("pool_done"), spare)
        lanes = [PE, AC, VE, PO]
        for slot in range(RING):
            nc.sync.sem_inc(lo_ready[slot], 1)
        nc.sync.sem_inc(used, RING)
        ring = Ring(nc, wraw, whi, wlo, full, hi_ready, lo_ready, used, spare)
        ring.limit = UNITS
        par_n = [0, 0]

        def ve(fn, toks, *a, **k):
            VE.wait(*toks)
            return VE.tick(getop(nc.vector, fn)(*a, **k))

        def po(fn, toks, *a, **k):
            PO.wait(*toks)
            PO.settle()
            return PO.tick(getop(nc.gpsimd, fn)(*a, **k))

        def getop(eng, fn):
            return {"tt": eng.tensor_tensor, "ts": eng.tensor_scalar, "copy": eng.tensor_copy, "memset": eng.memset,
                    "stt": nc.vector.scalar_tensor_tensor, "ttr": nc.vector.tensor_tensor_reduce,
                    "scan": nc.vector.tensor_tensor_scan, "rmax": nc.vector.reduce_max,
                    "recip": nc.vector.reciprocal}[fn]

        act_set = [None]

        def ac(toks, out_, in_, func, **k):
            if func in (ACT.Exp, ACT.Ln) and act_set[0] != "exp_ln":
                nc.scalar.preload_act_table_set("natural_log_exp_and_others")
                act_set[0] = "exp_ln"
            elif func in (ACT.Silu, ACT.Sigmoid):
                act_set[0] = func
            AC.wait(*toks)
            return AC.tick(nc.scalar.activation(out_, in_, func, **k))

        def mm(out_, lhsT, rhs, start, stop):
            return nc.tensor.matmul(out_, lhsT, rhs, start=start, stop=stop, skip_group_check=True)

        def rsqrt(dst, src, toks):
            t = ac(toks, dst, src, ACT.Ln, bias=eps[0:src.shape[0], :])
            t = ac([t], dst, dst, ACT.Exp, scale=-0.5)
            u = ry[0:src.shape[0], 0:src.shape[1]]
            t = ve("stt", [t, VE.now()], u, src, EPS, dst, ALU.add, ALU.mult)
            t = ve("stt", [t], u, u, -0.5, dst, ALU.mult, ALU.mult)
            return ve("stt", [t], dst, u, 1.5, dst, ALU.add, ALU.mult)

        def par_load(dst, src, toks=(), slow=False):
            PO.wait(*toks)
            PO.settle()
            if slow:
                with nc.allow_non_contiguous_dma(reason="a few small columns"):
                    nc.gpsimd.dma_start(dst, src).then_inc(par, 16)
            else:
                nc.gpsimd.dma_start(dst, src).then_inc(par, 16)
            par_n[0] += 16

        def par_all():
            return (par, par_n[1], par_n[0])

        def forget():
            for ln in lanes:
                ln.seen = {}

        def join(but=None):
            toks = [ln.now() for ln in lanes]
            for ln in lanes:
                if ln is not but:
                    ln.wait(*[t for t in toks if t[0] is not ln.sem])

        scopes = [0]

        class Scope:

            def __init__(self):
                self.stack = ExitStack()
                scopes[0] += 1
                self.id = scopes[0]
                self.count = 0

            def take(self, *shape, dt=F32):
                self.count += 1
                t = self.stack.enter_context(nc.sbuf_tensor(f"s{self.id}_{self.count}", [P] + list(shape), dt))
                return t[tuple([slice(None)] * (1 + len(shape)))]

            def pair(self, *shape):
                return self.take(*shape, dt=F32R), self.take(*shape, dt=F32R)

            def close(self):
                self.stack.close()

        h_tok = [None] * KD

        start = Scope()
        g1 = start.take(P)
        g2 = start.take(P)
        g3 = start.take(P)
        xs = start.take(3, D)
        nc.scalar.dma_start(cst[:, :], IN["consts"]).then_inc(s_in, 16)
        nc.scalar.dma_start(xs[0:N_META, 2, :], IN["meta_tokens"]).then_inc(s_in, 16)
        nc.scalar.dma_start(xs[:, 0:2, :], IN["x"][0].rearrange("(t p) d -> p t d", p=P)).then_inc(s_in, 16)
        for i, name in enumerate(("g_pre_ffn1", "g_post_ffn1", "g_pre_mix", "g_post_mix", "g_pre_ffn2", "g_post_ffn2")):
            par_load(g1[16 * i:16 * i + 16, :], IN[name].rearrange("l (k p) -> (l k) p", p=P))
        par_load(g1[96:100, :], IN["b_alpha"].rearrange("l (k p) -> (l k) p", p=P))
        par_load(g1[100:108, :], IN["g_gla_out"].rearrange("l (k p) -> (l k) p", p=P))
        for i, name in enumerate(("ffn1_norm_2", "ffn2_norm_2", "mix_norm_2", "mem_norm_2")):
            par_load(g2[16 * i:16 * i + 16, :], IN[name].rearrange("l (k p) -> (l k) p", p=P))
        par_load(g2[64:72, :], IN["kv_norm_2"].rearrange("(k p) -> k p", p=P))
        for c in (0, HD):
            par_load(g2[72:74, c:c + HD], IN["mem_q_norm_2"])
            par_load(g2[74:76, c:c + HD], IN["mem_k_norm_2"])
            par_load(g2[76:77, c:c + HD], IN["b_q_norm_2"])
            par_load(g2[77:78, c:c + HD], IN["kv_k_norm_2"].rearrange("(a p) -> a p", a=1))
        par_load(g3[0:8, 0:MH], IN["a_h_norm_2"].rearrange("l h (j p) -> (l h j) p", p=MH))
        par_load(g3[8:72, 0:MH], IN["a_conv_2"].rearrange("l j (c p) -> (l j c) p", p=MH))
        AC.wait(po("memset", [], eps[:, :], EPS))
        PE.wait((s_in, 0, 48))
        VE.wait((s_in, 0, 48))
        AC.wait((s_in, 0, 48))
        ident = C("ident")
        taken = [None] * 8

        def turn_rows(src, rows, t, dst, c0):
            for k in range(KD):
                b = 4 + k % 4
                PE.wait(taken[b])
                tk = PE.tick(nc.tensor.transpose(bank[b][:, 0:rows], src[0:rows, t, k * P:k * P + P], ident[0:rows, 0:rows]))
                taken[b] = ve("copy", [tk], dst[:, k, c0:c0 + rows], bank[b][:, 0:rows])
                h_tok[k] = taken[b]

        turn_rows(xs, N_META, 2, hT, 0)
        turn_rows(xs, P, 0, hT, N_META)
        turn_rows(xs, P, 1, hT, N_META + P)
        PE.wait(par_all())
        for b, (src, rows, w, dst) in enumerate(((g1, 108, P, gain1), (g2, 78, P, gain2), (g3, 72, MH, gain3))):
            t = PE.tick(nc.tensor.transpose(bank[b][0:w, 0:rows], src[0:rows, 0:w], ident[0:rows, 0:rows]))
            ve("copy", [t], dst[:, 0:rows], bank[b][0:w, 0:rows])
        ve("ts", [VE.now()], gain2[:, 72:74], gain2[:, 72:74], HD ** -0.5, None, ALU.mult)
        ve("ts", [VE.now()], gain2[:, 76:77], gain2[:, 76:77], HD ** -0.5, None, ALU.mult)
        for c in (16, 80):
            ve("ts", [VE.now()], gain1[:, c:c + 16], gain1[:, c:c + 16], 0.5, None, ALU.mult)
        start.close()

        rtok = [None]
        xt = [[None] * KD, [None] * KD]

        def take(src, rows=P):
            return ring.take(src, AC, VE, PO, rows)

        def to_pair(dst, k, src, toks, gain=1.0):
            th = ac(toks, dst[0][k], src, ACT.Copy, scale=gain)
            tl = ve("stt", [th], dst[1][k], src, gain, dst[0][k].bitcast(F32), ALU.mult, ALU.subtract)
            return th, tl

        def squares(src, toks, cols, part, lane):
            c0, c1 = cols
            for k in part:
                if k == 0:
                    t = sum_tok[0] = ac([toks[k]], ssum[:, 0:c1 - c0], src[:, k, c0:c1], ACT.Square)
                else:
                    t = ac([toks[k], sq_free[k % 2]], sqb[:, k % 2, 0:c1 - c0], src[:, k, c0:c1], ACT.Square)
                    t = sq_free[k % 2] = sum_tok[0] = lane("tt", [t, sum_tok[0]], ssum[:, 0:c1 - c0], ssum[:, 0:c1 - c0], sqb[:, k % 2, 0:c1 - c0], ALU.add)
            return t

        sq_free = [None, None]
        sum_tok = [None]

        def stats(t, cols, b):
            c0, c1 = cols
            PE.wait(t, taken[b])
            t = PE.tick(mm(bank[b][:, 0:c1 - c0], C("mean1024"), ssum[:, 0:c1 - c0], True, True))
            rtok[0] = rsqrt(rst[:, c0:c1], bank[b][:, 0:c1 - c0], [t])

        def norm_in(gain, cols):
            c0, c1 = cols
            for k in range(KD):
                xt[0][k] = ac([h_tok[k]], xh[:, k, c0:c1], hT[:, k, c0:c1], ACT.Copy, scale=gain(k))
            for k in range(KD):
                xt[1][k] = ve("stt", [xt[0][k]], xl[:, k, c0:c1], hT[:, k, c0:c1], gain(k), xh[:, k, c0:c1].bitcast(F32),
                              ALU.mult, ALU.subtract)

        def products(out_, U, w, x, n_k=KD, start=True, stop=True, toks=None):
            passes = ((0, 0), (1, 0), (0, 1))
            for i, (a, b) in enumerate(passes):
                PE.wait(U["hi"] if i == 0 else U["lo"])
                for k in range(n_k):
                    if toks is not None and i != 1:
                        PE.wait(toks[b][k])
                    m = mm(out_, w(k, a), x(k, b), start and i == 0 and k == 0, stop and i == 2 and k == n_k - 1)
            return m

        def xin(cols):
            c0, c1 = cols
            return lambda k, part: (xh, xl)[part][:, k, c0:c1]

        def ffn(gate_src, up_src, down_src, cols, post, then):
            c0, c1 = cols
            T = c1 - c0
            sc = Scope()
            ah, al = sc.pair(NF, T1)
            sg, su = sc.take(2, T1), sc.take(2, T1)
            y = sc.take(KD, T1) if post is not None else None
            x = xin(cols)
            evac = {}

            def half(src, i, toks=None):
                U = take(src)
                m = products(bank[i][:, 0:T], U, lambda k, part: U["w"][part][:, k, :], x, toks=toks)
                return ring.release(m)

            def part1(j, tg, tu):
                t1 = ve("tt", [tg, rtok[0]], sg[:, j, 0:T], bank[2 * j][:, 0:T], rst[:, c0:c1], ALU.mult)
                t2 = ac([t1], sg[:, j, 0:T], sg[:, j, 0:T], ACT.Silu)
                evac[j] = ve("tt", [tu, al_tok[j]], su[:, j, 0:T], bank[2 * j + 1][:, 0:T], rst[:, c0:c1], ALU.mult)
                return t2

            def part2(f, j, t):
                t = ve("tt", [t, evac[j]], su[:, j, 0:T], su[:, j, 0:T], sg[:, j, 0:T], ALU.mult)
                return ac([t], ah[:, f, c0:c1], su[:, j, 0:T], ACT.Copy)

            def part3(f, j, t):
                al_tok[j] = ve("tt", [t], al[:, f, c0:c1], su[:, j, 0:T], ah[:, f, c0:c1].bitcast(F32), ALU.subtract)

            al_tok = [None, None]
            PE.wait(*taken)
            tg0 = half(gate_src(0, 0), 0, xt)
            squares(hT, h_tok, cols, range(0, 4), po)
            tu0 = half(up_src(0, 0), 1)
            tq = squares(hT, h_tok, cols, range(4, 8), po)
            tg1 = half(gate_src(0, 1), 2)
            stats(tq, cols, 7)
            t = part1(0, tg0, tu0)
            tu1 = half(up_src(0, 1), 3)
            t = part2(0, 0, t)
            t1 = part1(1, tg1, tu1)
            part3(0, 0, t)
            part3(1, 1, part2(1, 1, t1))
            for ln in lanes:
                ln.settle()
            forget()
            entry = {ln: (ln.n, ln.loop) for ln in lanes}
            r_entry = (ring.loads, ring.splits, ring.freed, ring.loop, ring.loop_slot, ring.loop16)
            PER = {PE: 0, AC: 4, VE: 8}
            with nc.Fori(0, TURNS - 1) as i:
                act_set[0] = None
                for ln in (AC, VE):
                    ln.loop = nc.snap(ln.loop + i * PER[ln])
                ring.loop = nc.snap(ring.loop + i * RING)
                ring.loop_slot = nc.snap(ring.loop_slot + i)
                ring.loop16 = nc.snap(ring.loop16 + i * 16)
                f = i * 2 + 2
                v0 = VE.n
                PE.wait(VE.at(v0 - 6))
                tg = half(gate_src(i + 1, 0), 0)
                tu = half(up_src(i + 1, 0), 1)
                al_tok[0] = al_tok[1] = None
                VE.wait(VE.at(v0))
                t = part1(0, tg, tu)
                PE.wait(VE.at(v0))
                tg = half(gate_src(i + 1, 1), 2)
                t = part2(f, 0, t)
                tu = half(up_src(i + 1, 1), 3)
                part3(f, 0, t)
                t = part1(1, tg, tu)
                part3(f + 1, 1, part2(f + 1, 1, t))
                a_last, v_last, v_bank = AC.n, VE.n, VE.n - 2
            for ln in (PE, AC, VE):
                assert ln.n - entry[ln][0] == PER[ln], (ln.name, ln.n - entry[ln][0])
                ln.n, ln.loop = entry[ln][0] + (TURNS - 1) * PER[ln], entry[ln][1]
            more = RING * (TURNS - 1)
            ring.loads, ring.splits, ring.freed = (r + more for r in r_entry[:3])
            ring.loop, ring.loop_slot, ring.loop16 = r_entry[3:]
            forget()
            order = [4, 5, 6, 7, 0, 1, 2, 3]
            PE.wait(AC.at(AC.n - PER[AC]), VE.at(VE.n - PER[VE]))
            LAST = RING
            first = [take(down_src(0)), take(down_src(1))]
            for d in order:
                if d == 0:
                    PE.wait(VE.now())
                for f, U in enumerate(first):
                    PE.wait(U["hi"], U["lo"])
                    for z, (a, b) in enumerate(((0, 0), (1, 0), (0, 1))):
                        m = mm(bank[d][:, 0:T], U["w"][a][:, 0, d * P:d * P + P], (ah, al)[b][:, f, c0:c1], f == 0 and z == 0, False)
                    if d == order[-1]:
                        ring.release(m)
            for f in range(2, NF - LAST):
                U = take(down_src(f))
                if f == NF - LAST - 1:
                    ring.hold = True
                PE.wait(U["hi"], U["lo"])
                for d in order:
                    for z, (a, b) in enumerate(((0, 0), (1, 0), (0, 1))):
                        m = mm(bank[d][:, 0:T], U["w"][a][:, 0, d * P:d * P + P], (ah, al)[b][:, f, c0:c1], False, False)
                ring.release(m)
            PE.wait(AC.now(), VE.now())
            us = []
            for z in range(LAST):
                us.append(take(down_src(NF - LAST + z)))
            ring.hold = False
            while ring.splits < ring.loads:
                ring.split(AC, VE, PO)
            done = []
            for d in range(KD):
                for q, U in enumerate(us):
                    PE.wait(U["hi"], U["lo"])
                    f = NF - LAST + q
                    for z, (a, b) in enumerate(((0, 0), (1, 0), (0, 1))):
                        m = mm(bank[d][:, 0:T], U["w"][a][:, 0, d * P:d * P + P], (ah, al)[b][:, f, c0:c1], False,
                               q == LAST - 1 and z == 2)
                    if d == KD - 1:
                        t = ring.release(m)
                done.append(t if d == KD - 1 else PE.tick(m))
            if post is None:
                for d in range(KD):
                    h_tok[d] = taken[d] = ve("stt", [done[d]], hT[:, d, c0:c1], bank[d][:, 0:T], 0.5, hT[:, d, c0:c1], ALU.mult, ALU.add)
                then()
                ring.catch_up(AC, VE, PO)
            else:
                postnorm(done, post, cols, y, then)
            sc.close()

        def postnorm(done, gain, cols, y, then):
            c0, c1 = cols
            T = c1 - c0
            tv = []
            for d in range(KD):
                taken[d] = ve("copy", [done[d]], y[:, d, c0:c1], bank[d][:, 0:T])
                tv.append(taken[d])
                t = squares(y, tv + [None] * (KD - 1 - d), cols, [d], ve)
            ring.catch_up(AC, VE, PO, 1)
            stats(t, cols, 0)
            taken[0] = rtok[0]
            for d in range(KD):
                yd = y[:, d, c0:c1]
                ty = ve("stt", [rtok[0], tv[d]], yd, yd, gain(d), rst[:, c0:c1], ALU.mult, ALU.mult)
                lane = po if d % 2 else ve
                h_tok[d] = lane("tt", [ty], hT[:, d, c0:c1], hT[:, d, c0:c1], yd, ALU.add)
            then()
            ring.catch_up(AC, VE, PO)

        def columns(wd, a, w=P):
            return wd.rearrange("(k p) n -> p k n", p=P)[:, :, a:a + w]

        proj_bank = [0]

        def next_bank():
            b = proj_bank[0]
            proj_bank[0] = 1 - b
            PE.wait(taken[b])
            return b

        def project(U, x, T, M=P, c=0, last=True, toks=None):
            b = next_bank()
            m = products(bank[b][0:M, 0:T], U, lambda k, part: U["w"][part][:, k, c:c + M], x, toks=toks)
            return b, ring.release(m) if last else PE.tick(m)

        def turned_steps(items, zb, tiles, tb):
            VE.wait(PE.now(), VE.now())
            free = [None, None]
            pend = None
            for i, item in enumerate(list(items) + [None]):
                new = None
                if item is not None:
                    make, scaled, dst, finish = item
                    z = i % 2
                    b, t = make()
                    w = tiles[-1][0] + tiles[-1][1]
                    if scaled is not None:
                        t = taken[b] = ve("tt", [t, rtok[0], free[z]], zb[z][:, 0:w], bank[b][:, 0:w], scaled, ALU.mult)
                    else:
                        t = taken[b] = ve("copy", [t, free[z]], zb[z][:, 0:w], bank[b][:, 0:w])
                    new = (z, t, dst, finish)
                if pend is not None:
                    z, t, dst, finish = pend
                    PE.wait(t, taken[tb])
                    for j, (c0, n) in enumerate(tiles):
                        m = nc.tensor.transpose(bank[tb][0:n, j * P:j * P + P], zb[z][:, c0:c0 + n], ident)
                    t = free[z] = PE.tick(m)
                    for j, (c0, n) in enumerate(tiles):
                        t2 = ac([t], dst[j][0:n], bank[tb][0:n, j * P:j * P + P], ACT.Copy)
                    taken[tb] = t2
                    finish(t2)
                pend = new
                yield

        def attention(units, bufs, s_banks, t_banks):
            SS, PP, PT, st = bufs
            p_free = [None, None]
            pt_free = [None, None]
            state = {}
            for i in range(len(units) + 2):
                if i < len(units):
                    u = units[i]
                    z = i % 2
                    n, W = u["n"], u["W"]
                    sb_ = bank[s_banks[z]]
                    PE.wait(taken[s_banks[z]], *u["need"])
                    for (q, k, w, c) in u["qk"]:
                        m = mm(sb_[0:n, c:c + w], q, k, True, True)
                    t = PE.tick(m)
                    mx, nm, den, rd = (st[0:n, 4 * z + x:4 * z + x + 1] for x in range(4))
                    if u["mask"] is not None:
                        t = ve("tt", [t, p_free[z]], SS[z][0:n, 0:W], sb_[0:n, 0:W], u["mask"], ALU.add)
                        taken[s_banks[z]] = t
                        src = SS[z][0:n, 0:W]
                    else:
                        src = sb_[0:n, 0:W]
                    t = ve("rmax", [t], mx, src, AX_X)
                    t = ve("ts", [t], nm, mx, -1.0, None, ALU.mult)
                    t = ac([t, p_free[z]], PP[z][0:n, 0:W], src, ACT.Exp, bias=nm, accum_out=den)
                    if u["mask"] is None:
                        taken[s_banks[z]] = t
                    t = ve("recip", [t], rd, den)
                    t = ve("ts", [t], PP[z][0:n, 0:W], PP[z][0:n, 0:W], rd, None, ALU.mult)
                    state[i] = t
                if 0 <= i - 1 < len(units):
                    u = units[i - 1]
                    z = (i - 1) % 2
                    n = u["n"]
                    tb_ = bank[t_banks[z]]
                    PE.wait(state[i - 1], taken[t_banks[z]])
                    PE.settle()
                    for (c, ns, slot) in u["turn"]:
                        m = nc.tensor.transpose(tb_[0:ns, slot * P:slot * P + n], PP[z][0:n, c:c + ns], ident[0:n, 0:n])
                    t = PE.tick(m)
                    p_free[z] = t
                    fulls = [s for s in u["turn"] if s[1] == P]
                    rest = [s for s in u["turn"] if s[1] != P]
                    nf = len(fulls)
                    if nf:
                        a = tb_[:, 0:nf * P].rearrange("p (s c) -> p s c", c=P)[:, :, 0:n]
                        o = PT[z][:, 0:nf * P].rearrange("p (s c) -> p s c", c=P)[:, :, 0:n]
                        tc = ac([t, pt_free[z]], o, a, ACT.Copy)
                    for (c, ns, slot) in rest:
                        tc = ac([t, pt_free[z]], PT[z][0:ns, slot * P:slot * P + n], tb_[0:ns, slot * P:slot * P + n], ACT.Copy)
                    taken[t_banks[z]] = tc
                    state[i - 1] = tc
                if 0 <= i - 2 < len(units):
                    u = units[i - 2]
                    z = (i - 2) % 2
                    n = u["n"]
                    PE.wait(state[i - 2])
                    u["open"]()
                    for (o, terms) in u["pv"]:
                        for x, (slot, ns, v) in enumerate(terms):
                            m = mm(o, v, PT[z][0:ns, slot * P:slot * P + n], x == 0, x == len(terms) - 1)
                    t = PE.tick(m)
                    pt_free[z] = t
                    u["close"](t)
                yield

        def drive(main, sides):
            sides = list(sides)

            def side_steps():
                for g in list(sides):
                    if next(g, sides) is sides:
                        sides.remove(g)

            for _ in main:
                side_steps()
            while sides:
                side_steps()

        def log_sigmoid(dst, z, scr, toks):
            t = ve("stt", toks, scr, z, -1.0, z, ALU.mult, ALU.max)
            t = ac([t], scr, scr, ACT.Exp, scale=-1.0)
            t = ac([t], scr, scr, ACT.Ln, bias=1.0)
            return ve("stt", [t], dst, z, 0.0, scr, ALU.min, ALU.subtract)

        cols1 = (0, T1)
        PER_LAYER = 4096

        w_in_at = dict(zip(("fq", "fk", "fv", "ff", "gq", "gk", "gv", "ga", "gr", "ma", "mb"), SPLIT_AT))

        def mixer1(L, then):
            lay = Scope()
            qa = lay.take(FOX_HEADS, T1)
            ka = lay.take(FOX_HEADS, T1)
            fv = lay.take(3, FOX_W)
            gq = lay.take(2, T1)
            gk = lay.take(2, T1)
            gv = lay.take(3, GLA_W)
            cb = lay.take(2, T1)
            qz, kz = lay.take(2, T1), lay.take(2, T1)
            at = lay.take(GLA_HEADS, 2 * T1)
            gr = lay.take(4, T1)
            ofp, ogp = lay.pair(4, T1), lay.pair(4, T1)
            dg = lay.take(T1)
            sg = lay.take(2, T1)
            cums = lay.take(2, T1)
            ybuf = lay.take(KD, T1)
            lay_x = rst2
            X = [sg[:, 0:2, :], ybuf[:, 5:7, :]]
            SS = [ybuf[:, 0, :], ybuf[:, 1, :]]
            PP = [lay.take(T1), lay.take(T1)]
            zb1 = (sqb[:, 0, :], sqb[:, 1, :])
            ptv = ybuf[:, 2:5, :].rearrange("p a b -> p (a b)")
            PT = [ptv[:, 0:384], ptv[:, 384:768]]
            smh = lay.take(2 * KD, T1)
            w_in = IN["w_in"][L]
            gain = lambda g: (lambda k: gcur[:, 8 * g + k:8 * g + k + 1])
            x = xin(cols1)
            tzx = [po("memset", [], x_, 0.0) for x_ in X][-1]
            po("memset", [], qa, 0.0)
            po("memset", [], ka, 0.0)
            zeroed = PO.now()
            tk = {}
            sc = small

            def load(name, a):
                return take(columns(w_in, w_in_at[name] + a))

            def halves(name, out_, toks=None):
                b = next_bank()
                for z in range(2):
                    U = take(columns(w_in, w_in_at[name])[:, 4 * z:4 * z + 4, :])
                    m = products(bank[b][:, 0:T1], U, lambda k, part: U["w"][part][:, k, :],
                                 lambda k, part: x(4 * z + k, part), n_k=4, start=z == 0, stop=z == 1,
                                 toks=None if toks is None else [tt[4 * z:4 * z + 4] for tt in toks])
                    t = ring.release(m)
                return b, t

            def main():
                b, t = halves("ga", None, xt)
                tq = squares(hT, h_tok, cols1, range(KD), ve)
                U = load("gq", 0)
                b1, t1 = project(U, x, T1)
                stats(tq, cols1, 7)
                taken[7] = VE.now()
                tga = taken[b] = ve("tt", [t, rtok[0]], lay_x[0:GATE_RANK, :], bank[b][0:GATE_RANK, 0:T1], rst[0:GATE_RANK, :], ALU.mult)
                tk["gq", 0] = taken[b1] = ve("stt", [t1], gq[:, 0, :], bank[b1][:, 0:T1], GLA_DK ** -0.5, rst[:, :], ALU.mult, ALU.mult)
                b1, t1 = project(load("gq", P), x, T1)
                tk["gq", 1] = taken[b1] = ve("stt", [t1], gq[:, 1, :], bank[b1][:, 0:T1], GLA_DK ** -0.5, rst[:, :], ALU.mult, ALU.mult)
                PE.wait(tga, loaded[0])
                for c in range(2):
                    b = next_bank()
                    t = PE.tick(mm(bank[b][:, 0:T1], wau[:, c * P:c * P + P], lay_x[0:GATE_RANK, :], True, True))
                    t = taken[b] = ve("ts", [t], cb[:, c, :], bank[b][:, 0:T1], gcur[:, 48 + c:49 + c], None, ALU.add)
                    t = log_sigmoid(cb[:, c, :], cb[:, c, :], ssum[:, :], [t])
                    t = ve("ts", [t], cb[:, c, :], cb[:, c, :], 1.0 / 16.0, None, ALU.mult)
                    tk["cb", c] = ve("scan", [t], cb[:, c, :], C("ones"), cb[:, c, :], 0.0, ALU.mult, ALU.add)
                for c in range(2):
                    b, t = project(load("gk", c * P), x, T1)
                    tk["gk", c] = taken[b] = ve("tt", [t], gk[:, c, :], bank[b][:, 0:T1], rst[:, :], ALU.mult)
                    yield
                b, t = halves("ff", None)
                H8 = slice(0, FOX_HEADS)
                cum, ncum = cums[H8, 0, :], cums[H8, 1, :]
                t = taken[b] = ve("tt", [t], cum, bank[b][H8, 0:T1], rst[H8, :], ALU.mult)
                t = ve("ts", [t, loaded[0]], cum, cum, small[H8, 0:1], None, ALU.add)
                t = log_sigmoid(cum, cum, ncum, [t])
                t = ve("scan", [t], cum, C("ones")[H8, :], cum, 0.0, ALU.mult, ALU.add)
                tk["cum"] = ve("ts", [t], ncum, cum, -1.0, None, ALU.mult)
                yield
                for name, dst, scale in (("fq", qa, HD ** -0.5), ("fk", ka, 1.0)):
                    for s in range(4):
                        b, t = project(load(name, s * P), x, T1)
                        h = 2 * s
                        VE.wait(zeroed)
                        ve("stt", [t], dst[0:64, h, :], bank[b][0:64, 0:T1], scale, rst[0:64, :], ALU.mult, ALU.mult)
                        tk[name, h] = taken[b] = ve("stt", [t], dst[64:128, h + 1, :], bank[b][64:128, 0:T1], scale,
                                                    rst[64:128, :], ALU.mult, ALU.mult)
                        yield
                for tok in (tk["cum"], zeroed):
                    nc.sync.wait_ge(tok[0], tok[1] + tok[2])
                    nc.sync.sem_inc(spare, 1)
                half_ones = C("ones")[0:1, :].unsqueeze(1).broadcast_to([1, FOX_HEADS // 2, T1])
                for odd, r in ((0, 64), (1, 0)):
                    for dst, row in ((qa, r + 1), (ka, r)):
                        nc.sync.dma_start(dst[row:row + 1, odd::2, :], half_ones).then_inc(s_aug, 16)
                for h in range(FOX_HEADS):
                    r = 64 if h % 2 == 0 else 0
                    nc.sync.dma_start(qa[r:r + 1, h, :], cums[h:h + 1, 0, :]).then_inc(s_aug, 16)
                    nc.sync.dma_start(ka[r + 1:r + 2, h, :], cums[h:h + 1, 1, :]).then_inc(s_aug, 16)
                tk["aug"] = (s_aug, aug_loop[0], 16 * AUG_LOADS)
                def value(name, dst, s):
                    def done(t):
                        tk[name, s] = t
                    return (lambda: project(load(name, s * P), x, T1), rst[:, :],
                            [dst[:, i, s * P:s * P + P] for i in range(3)], done)
                yield from turned_steps([value(name, dst, s) for name, dst in (("fv", fv), ("gv", gv)) for s in range(4)],
                                        zb1, TOK_TILES1, 3)
                for i in range(4):
                    b, t = project(load("gr", i * P), x, T1)
                    t1 = taken[b] = ve("tt", [t], gr[:, i, :], bank[b][:, 0:T1], rst[:, :], ALU.mult)
                    t1 = ac([t1], rst2[:, 0:T1], gr[:, i, :], ACT.Exp, scale=-1.0)
                    t1 = ve("ts", [t1], rst2[:, 0:T1], rst2[:, 0:T1], 1.0, None, ALU.add)
                    t1 = ve("recip", [t1], rst2[:, 0:T1], rst2[:, 0:T1])
                    tk["gr", i] = ve("tt", [t1], gr[:, i, :], gr[:, i, :], rst2[:, 0:T1], ALU.mult)
                    AC.wait(tk["gr", i])
                    yield
                for i in range(2 * KD):
                    b, t = project(load("ma", i * P), x, T1)
                    tk["m", i] = taken[b] = ve("tt", [t], smh[:, i, :], bank[b][:, 0:T1], rst[:, :], ALU.mult)
                    yield

            def gla():
                yield from gla_diag()
                yield from gla_levels()
                yield from gla_outputs()

            def gla_diag():
                s4 = lambda a: a.rearrange("p c (i j) -> p c i j", j=SUB)
                ready = [tk[n, c] for n in ("gq", "gk", "cb") for c in range(2)] + [tzx]
                read = [None, None]
                pend = None
                for j in list(reversed(range(SUB))) + [None]:
                    if j is not None:
                        n, z = SUB - j, j % 2
                        xs_ = s4(X[z])[:, :, :, j:SUB]
                        at_s = lambda a: s4(a)[:, :, :, j:j + 1].broadcast_to([P, 2, N_SUB, n])
                        t = ve("tt", ready + [read[z]], xs_, s4(cb)[:, :, :, j:SUB], at_s(cb), ALU.subtract)
                        t = ac([t], xs_, xs_, ACT.Exp)
                        t = ve("tt", [t], xs_, xs_, s4(gq)[:, :, :, j:SUB], ALU.mult)
                        t = ve("tt", [t], xs_, xs_, at_s(gk), ALU.mult)
                    if pend is not None:
                        jj, tt = pend
                        PE.wait(tt, taken[7])
                        for c in range(2):
                            pick = C("pickd")[:, 80 * c + 15 - jj:80 * c + 15 - jj + 64]
                            m = mm(bank[7][0:64, 0:T1], pick, X[jj % 2][:, c, :], jj == SUB - 1 and c == 0, jj == 0 and c == 1)
                        read[jj % 2] = PE.tick(m)
                    pend = (j, t) if j is not None else None
                    if j is not None:
                        yield
                tk["dg"] = taken[7] = ve("copy", [read[0]], dg[0:64, :], bank[7][0:64, 0:T1])

            def gla_levels():
                scr = ybuf[:, 5:7, :].rearrange("p a b -> p (a b)")[:, 0:512]
                e = X[0]
                H = range(GLA_HEADS)
                rows = lambda h: slice(64 * (h % 2), 64 * (h % 2) + 64)

                def prep(L):
                    if L < 256:
                        w = 2 * L
                        v = lambda a: a[:, :, 0:256].rearrange("p c (m l) -> p c m l", l=w)
                        ref = v(cb)[:, :, :, L - 1:L].broadcast_to([P, 2, 256 // w, w])
                    else:
                        v = lambda a: a
                        ref = cb[:, :, 255:256].broadcast_to([P, 2, T1])
                    t = ve("tt", [PE.now(), VE.now()], v(e), v(cb), ref, ALU.subtract)
                    t = ac([t], v(e), v(e), ACT.Abs)
                    t = ac([t], v(e), v(e), ACT.Exp, scale=-1.0)
                    ve("tt", [t], v(qz), v(gq), v(e), ALU.mult)
                    return ve("tt", [t], v(kz), v(gk), v(e), ALU.mult)

                def masked(level, first):
                    mask = C("blocks")[:, 128 * level:128 * level + 128].unsqueeze(1).unsqueeze(1).broadcast_to([P, 2, 2, P])
                    for b in range(2):
                        src = bank[4 + b][:, 0:512].rearrange("p (h i t) -> p h i t", h=2, i=2)
                        dst = at.rearrange("p (h b) (i t) -> p b h i t", b=2, i=2)[:, b, :, :, 0:P]
                        if first:
                            taken[4 + b] = t = ve("tt", [read_at], dst, src, mask, ALU.mult)
                        else:
                            s4 = scr.rearrange("p (h i t) -> p h i t", h=2, i=2)
                            taken[4 + b] = t = ve("tt", [read_at, VE.now()], s4, src, mask, ALU.mult)
                            t = ve("tt", [t], dst, dst, s4, ALU.add)
                    tk["at"] = t

                tp = prep(SUB)
                PE.wait(tk["dg"], taken[4], taken[5])
                cell = lambda h, i: bank[4 + h % 2][:, (h // 2) * 256 + i * P:(h // 2) * 256 + i * P + P]
                for h in H:
                    for i in range(2):
                        m = mm(cell(h, i), C("rep")[0:64, h * P:h * P + P], dg[0:64, i * P:i * P + P], True, True)
                read_at = PE.tick(m)
                masked(0, True)
                yield
                for level in range(1, 4):
                    PE.wait(tp, taken[4], taken[5])
                    for h in H:
                        for c0 in (0, P):
                            m = mm(cell(h, c0 // P), kz[rows(h), h // 2, c0:c0 + P], qz[rows(h), h // 2, c0:c0 + P], True, True)
                    read_at = PE.tick(m)
                    tp = prep(SUB << level)
                    masked(level, False)
                    yield
                PE.wait(tp, taken[4], taken[5])
                for h in H:
                    mm(bank[4 + h % 2][:, (h // 2) * P:(h // 2) * P + P], kz[rows(h), h // 2, 0:P], qz[rows(h), h // 2, P:2 * P], True, True)
                PE.wait(taken[7])
                for h in H:
                    m = mm(bank[7][0:SUB, h * SUB:h * SUB + SUB], C("rep")[0:64, h * P:h * P + SUB], dg[0:64, 256:T1], True, True)
                t = PE.tick(m)
                tp = prep(256)
                odd = lambda a, b: a.rearrange("p (h b) t -> p b h t", b=2)[:, b]
                for b in range(2):
                    taken[4 + b] = ac([t], odd(at, b)[:, :, P:2 * P], bank[4 + b][:, 0:2 * P].rearrange("p (h t) -> p h t", h=2), ACT.Copy)
                taken[7] = ac([t], at[0:SUB, :, 416:432], bank[7][0:SUB, 0:4 * SUB].rearrange("p (h t) -> p h t", h=4), ACT.Copy)
                yield
                PE.wait(tp, taken[4], taken[5])
                for h in H:
                    for i in range(2):
                        a = (2 * i + h // 2) * SUB
                        m = mm(bank[4 + h % 2][:, a:a + SUB], kz[rows(h), h // 2, i * P:i * P + P], qz[rows(h), h // 2, 256:T1], True, True)
                t = PE.tick(m)
                for b in range(2):
                    for i, a in ((0, 256), (1, 400)):
                        taken[4 + b] = ac([t], odd(at, b)[:, :, a:a + SUB],
                                          bank[4 + b][:, 2 * SUB * i:2 * SUB * i + 2 * SUB].rearrange("p (h t) -> p h t", h=2), ACT.Copy)
                tk["at2"] = AC.now()
                yield

            def gla_outputs():
                o, sq = X[0][:, 0, :], X[0][:, 1, :]
                free = PE.now()
                for h in range(GLA_HEADS):
                    while ("gv", 3) not in tk or ("gr", h) not in tk:
                        yield
                    PE.wait(tk["at"], tk["at2"], taken[7], tk["gv", 3])
                    mm(bank[7][:, 0:T1], gv[:, 0, h * P:h * P + P], at[:, h, 0:T1], True, False)
                    mm(bank[7][:, P:T1], gv[:, 1, h * P:h * P + P], at[:, h, T1:416], False, False)
                    m = mm(bank[7][:, 256:T1], gv[0:16, 2, h * P:h * P + P], at[0:16, h, 416:432], False, True)
                    t = PE.tick(m)
                    t1 = ac([t, VE.now(), free], sq, bank[7][:, 0:T1], ACT.Square)
                    t2 = taken[7] = ve("copy", [t, t1], o, bank[7][:, 0:T1])
                    yield
                    PE.wait(t1, taken[4])
                    free = t = PE.tick(mm(bank[4][:, 0:T1], C("mean128"), sq, True, True))
                    t = taken[4] = rsqrt(sq, bank[4][:, 0:T1], [t])
                    t = ve("stt", [t, t2], o, o, gcur[:, 50 + h:51 + h], sq, ALU.mult, ALU.mult)
                    t = ve("tt", [t, tk["gr", h]], o, o, gr[:, h, :], ALU.mult)
                    to_pair(([ogp[0][:, h, :]], [ogp[1][:, h, :]]), 0, o, [t])

            def fox():
                units = []
                of_tok = {}

                def opener(pair, first):
                    def go():
                        if first:
                            PE.wait(taken[6])
                    return go

                def closer(pair, last):
                    def go(t):
                        if last:
                            taken[6] = to_pair(([ofp[0][:, pair, :]], [ofp[1][:, pair, :]]), 0, bank[6][:, 0:T1], [t])[1]
                    return go

                for pair in range(4):
                    for i, (t0, n) in enumerate(TOK_TILES1):
                        for hh in range(2):
                            h = 2 * pair + hh
                            W = t0 + n
                            rows = slice(64 * hh, 64 * hh + 64)
                            units.append(dict(
                                n=n, W=W, need=[tk["aug"], tk["fq", 2 * pair], tk["fk", 2 * pair]],
                                qk=[(qa[:, h, t0:t0 + n], ka[:, h, 0:W], W, 0)],
                                mask=C("causal")[0:n, 256 - t0:256 - t0 + W],
                                turn=[(s0, ns, st) for st, (s0, ns) in enumerate(TOK_TILES1[:i + 1])],
                                open=opener(pair, i == 0 and hh == 0), close=closer(pair, i == 2 and hh == 1),
                                pv=[(bank[6][rows, t0:t0 + n],
                                     [(st, ns, fv[0:ns, st, h * HD:h * HD + HD]) for st, (s0, ns) in enumerate(TOK_TILES1[:i + 1])])]))
                PE.wait(tk["fv", 3])
                yield from attention(units, (SS, PP, PT, small[:, 8:16]), (2, 2), (3, 3))

            drive(main(), [lazy(gla, tk, ("gk", 1)), lazy(fox, tk, ("fv", 3))])
            for b in range(2, 8):
                taken[b] = None
            PE.wait(VE.now(), AC.now())
            f_free = [None] * 4
            yt = [[None] * KD, [None] * KD]
            quarter = lambda wd, s: wd.rearrange("(k p) n -> p k n", p=P)[:, :, s * 256:s * 256 + 256]
            for s in range(4):
                ts = []
                for z, (name, o) in enumerate((("w_fox_o", ofp), ("w_gla_o", ogp))):
                    U = take(quarter(IN[name][L], s))
                    for c in range(2):
                        b = 4 * (s % 2) + 2 * c + z
                        PE.wait(f_free[b // 2])
                        m = products(bank[b][:, 0:T1], U, lambda k, part: U["w"][part][:, k, c * P:c * P + P],
                                     lambda k, part: o[part][:, k, :], n_k=4)
                        ts.append(ring.release(m) if c == 1 else PE.tick(m))
                for c in range(2):
                    d = 2 * s + c
                    a, bb = smh[:, d, :], smh[:, KD + d, :]
                    sa = ac([tk["m", d]], a, a, ACT.Sigmoid)
                    sb2 = ac([tk["m", KD + d]], bb, bb, ACT.Sigmoid)
                    b = 4 * (s % 2) + 2 * c
                    t1 = ve("tt", [ts[c], sa], a, bank[b][:, 0:T1], a, ALU.mult)
                    t2 = f_free[b // 2] = ve("tt", [ts[2 + c], sb2], bb, bank[b + 1][:, 0:T1], bb, ALU.mult)
                    t = ve("tt", [t2, t1], a, a, bb, ALU.add)
                    yt[0][d], yt[1][d] = to_pair(([xh[:, d, :]], [xl[:, d, :]]), 0, a, [t])
            done = []
            for d in range(KD):
                U = take(columns(IN["w_out"][L], d * P))
                PE.wait(f_free[d // 2])
                m = products(bank[d][:, 0:T1], U, lambda k, part: U["w"][part][:, k, :], x, toks=yt if d == 0 else None)
                done.append(ring.release(m))
            postnorm(done, gain(3), cols1, ybuf, then)
            lay.close()

        def rows_of(wd, f):
            return wd.rearrange("(f a p) n -> f p a n", p=P, a=1)[f]

        def lazy(gen, tk, key):
            while key not in tk:
                yield
            yield from gen()



        join()
        for ln in lanes:
            ln.seen = {}
        entry = {ln: ln.n for ln in lanes}
        ring.catch_up(AC, VE, PO)
        r0 = (ring.loads, ring.splits, ring.freed)
        p0 = par_n[0]
        loaded = [None]
        PAR_LAYER = 16 * 2
        AUG_LOADS = 4 + 2 * FOX_HEADS
        aug_loop = [0]
        nc.disable_value_cache = True
        with nc.Fori(0, DEPTH) as L:
            act_set[0] = None
            share = nc.snap(L * PER_LAYER)
            for ln in lanes:
                ln.loop = share
            ring.loop = nc.snap(L * UNITS_PER_LAYER)
            ring.loop_slot = nc.snap(L * (UNITS_PER_LAYER // RING))
            ring.loop16 = nc.snap(L * (16 * UNITS_PER_LAYER // RING))
            par_n[1] = nc.snap(L * PAR_LAYER)
            aug_loop[0] = nc.snap(L * (16 * AUG_LOADS))
            for ln in lanes:
                ln.wait(*[o.at(entry[o]) for o in lanes if o is not ln])
            for k in range(KD):
                h_tok[k] = VE.at(entry[VE])
            for b in range(8):
                taken[b] = None
            par_load(wau[:, :], IN["w_alpha_up"][L])
            par_load(small[0:FOX_HEADS, 0:1], IN["b_f"][L].rearrange("(p a) -> p a", a=1), slow=True)
            ve("copy", [], gcur[:, 0:48].rearrange("p (g k) -> p g k", g=6),
               gain1[:, 0:96].rearrange("p (g l k) -> p l g k", g=6, l=2)[:, L])
            ve("copy", [], gcur[:, 48:50], gain1[:, 96:100].rearrange("p (l k) -> p l k", l=2)[:, L])
            ve("copy", [], gcur[:, 50:54], gain1[:, 100:108].rearrange("p (l k) -> p l k", l=2)[:, L])
            loaded[0] = par_all()
            VE.wait(VE.now())
            AC.wait(VE.now())
            g = lambda i: (lambda k: gcur[:, 8 * i + k:8 * i + k + 1])

            def gu1(name):
                w = IN[name][L].rearrange("(k p) n -> p k n", p=P)
                return [lambda i, j, c=c: w[:, :, bass.ds(i * (2 * P) + (c + j * P), P)] for c in (0, D_FF)]

            norm_in(g(0), cols1)
            ffn(*gu1("w_ffn1_gu"), lambda f: rows_of(IN["w_ffn1_down"][L], f), cols1, g(1), lambda: norm_in(g(2), cols1))
            join(but=PE)
            mixer1(L, lambda: norm_in(g(4), cols1))
            join(but=PE)
            ffn(*gu1("w_ffn2_gu"), lambda f: rows_of(IN["w_ffn2_down"][L], f), cols1, g(5), lambda: None)
            join()
            for ln in lanes:
                spent = ln.n - entry[ln]
                assert 0 < spent < PER_LAYER, spent
                ln.eng.wait_ge(ln.sem, ln.loop + ln.n)
                ln.eng.sem_inc(ln.sem, PER_LAYER - spent)
                ln.open = False
            assert ring.loads - r0[0] == ring.splits - r0[1] == ring.freed - r0[2] == UNITS_PER_LAYER, ring.loads
            assert par_n[0] - p0 == PAR_LAYER
        for ln in lanes:
            ln.n, ln.loop, ln.seen = entry[ln] + DEPTH * PER_LAYER, 0, {}
        act_set[0] = None
        ring.loads, ring.splits, ring.freed = (r + DEPTH * UNITS_PER_LAYER for r in r0)
        ring.loop = ring.loop_slot = ring.loop16 = 0
        par_n[0], par_n[1] = p0 + DEPTH * PAR_LAYER, 0
        join()
        for ln in lanes:
            ln.wait(*[o.now() for o in lanes if o is not ln])
        for k in range(KD):
            h_tok[k] = None

        cols2 = (N_META, T1)
        T = SEQ
        keep = Scope()
        memR = keep.take(KD, T)
        k_sh = keep.take(6, T)
        v_sh = keep.take(2, DIL_W)
        start = Scope()
        ms = start.take(2, D)
        par_load(ms, IN["mem_2"][0].rearrange("(t p) d -> p t d", p=P))
        PE.wait(par_all())
        saved = list(h_tok)
        turn_rows(ms, P, 0, memR, 0)
        turn_rows(ms, P, 1, memR, P)
        mt = list(h_tok)
        for k in range(KD):
            h_tok[k] = saved[k]
        t = squares(memR, mt, (0, T), range(KD), ve)
        stats(t, (0, T), 0)
        for k in range(KD):
            ve("tt", [rtok[0]], memR[:, k, :], memR[:, k, :], rst[:, 0:T], ALU.mult)
        join()
        start.close()

        def gcol2(i):
            return lambda k: gain2[:, 8 * i + k:8 * i + k + 1]

        def ffn2(pre, l, then):
            wg = IN[pre + "_w_gate_2"][l].rearrange("(k p) n -> p k n", p=P)
            wu = IN[pre + "_w_up_2"][l].rearrange("(k p) n -> p k n", p=P)
            at = lambda w: (lambda i, j: w[:, :, bass.ds(i * (2 * P) + j * P, P)])
            ffn(at(wg), at(wu), lambda f: rows_of(IN[pre + "_w_down_2"][l], f), cols2, None, then)

        def headnorm_steps(items, zb, scaled=True):
            sb2 = [sqb[:, 0, 0:T], sqb[:, 1, 0:T]]
            pend = None
            out_free = [None, None]
            for i, (make, gaincol, dst) in enumerate(list(items) + [(None, None, None)]):
                new = None
                if make is not None:
                    z = i % 2
                    b, t = make()
                    if scaled:
                        t2 = taken[b] = ve("tt", [t, rtok[0], out_free[z]], zb[z], bank[b][:, 0:T], rst[:, N_META:T1], ALU.mult)
                    else:
                        t2 = taken[b] = ve("copy", [t, out_free[z]], zb[z], bank[b][:, 0:T])
                    t1 = ac([t2], sb2[z], zb[z], ACT.Square)
                    new = (z, t1, t2, gaincol, dst)
                if pend is not None:
                    z, t1, t2, gc, dst = pend
                    PE.wait(t1, taken[7])
                    t = PE.tick(mm(bank[7][:, 0:T], C("mean64"), sb2[z], True, True))
                    t = taken[7] = rsqrt(sb2[z], bank[7][:, 0:T], [t])
                    out_free[z] = t = ve("stt", [t, t2], dst, zb[z], gc, sb2[z], ALU.mult, ALU.mult)
                pend = new
                yield

        def memory_kv(l, mem, kmem, vmem, zb):
            for k in range(KD):
                to_pair(([mem[0][:, k, :]], [mem[1][:, k, :]]), 0, memR[:, k, :], [], gain2[:, 48 + 8 * l + k:49 + 8 * l + k])
            PE.wait(AC.now(), VE.now())
            xm = lambda k, part: mem[part][:, k, :]
            mk = lambda c: (lambda: project(take(columns(IN["w_mem_kv_2"][l], c * P)), xm, T))
            yield from headnorm_steps([(mk(c), gain2[:, 74 + l:75 + l], kmem[:, c, :]) for c in range(2)], zb, scaled=False)
            val = lambda s: (lambda: project(take(columns(IN["w_mem_kv_2"][l], MEM_W + s * P)), xm, T), None,
                             [vmem[:, i, s * P:s * P + P] for i in range(2)], lambda t: None)
            yield from turned_steps([val(s) for s in range(2)], zb, TOK_TILES2, 7)

        def memory_units(qmem, kmem, vmem, hm, tk_out):
            units = []

            def opener(pair, first):
                def go():
                    if first:
                        PE.wait(taken[6])
                return go

            def closer(pair, last):
                def go(t):
                    if last:
                        taken[6] = to_pair(([hm[0][:, pair, :]], [hm[1][:, pair, :]]), 0, bank[6][:, 0:T], [t])[1]
                return go

            for pair in range(2):
                for i, (t0, n) in enumerate(TOK_TILES2):
                    for hh in range(2):
                        h = 2 * pair + hh
                        rows = slice(64 * hh, 64 * hh + 64)
                        units.append(dict(
                            n=n, W=T, need=[], qk=[(qmem[rows, pair, t0:t0 + n], kmem[rows, pair, :], T, 0)], mask=None,
                            turn=[(0, P, 0), (P, P, 1)], open=opener(pair, i == 0 and hh == 0),
                            close=closer(pair, i == 1 and hh == 1),
                            pv=[(bank[6][rows, t0:t0 + n], [(st, P, vmem[:, st, h * HD:h * HD + HD]) for st in range(2)])]))
            return units

        def free_bank_add(d, b, t):
            h_tok[d] = taken[b] = ve("tt", [t], hT[:, d, N_META:T1], bank[b][:, 0:T], hT[:, d, N_META:T1], ALU.add)

        def mixer2a():
            lay = Scope()
            qk = lay.take(16, T)
            v = lay.take(2, ML_W)
            og = lay.take(8, T)
            cellp = lay.pair(8, T)
            hm = lay.pair(2, T)
            kmem, qmem = lay.take(2, T), lay.take(2, T)
            vmem = lay.take(2, 256)
            xb = [lay.take(T + 4), lay.take(T + 4)]
            rowg = lay.take(4, T)
            memp = lay.pair(KD, T)
            WT = [[lay.take(T), lay.take(T)] for _ in range(2)]
            tmp = lay.take(3, T)
            sg = lay.take(2, T)
            w_in = IN["a_w_in_2"][0]
            R = slice(0, MH)
            x = xin(cols2)
            tz = [po("memset", [], xb[z][0:MH, 0:3], 0.0) for z in range(2)]
            par_load(small[0:4, 0:2], IN["a_gate_bias_2"][0].rearrange("(a p) -> p a", p=4), slow=True)
            tk = {}
            H4 = slice(0, ML_HEADS)

            def main():
                U = take(columns(w_in, 4 * ML_W))
                tq = squares(hT, h_tok, cols2, range(KD), ve)
                b0, t0_ = project(U, x, T, last=False, toks=xt)
                b1, t1_ = project(U, x, T, M=P - 4, c=4)
                stats(tq, cols2, 7)
                taken[7] = VE.now()
                VE.wait(par_all(), rtok[0])
                for g, b, t in ((0, b0, t0_), (1, b1, t1_)):
                    t = taken[b] = ve("tt", [t], rowg[H4, g, :], bank[b][H4, 0:T], rst[H4, N_META:T1], ALU.mult)
                    tk["g", g] = ve("ts", [t], rowg[H4, g, :], rowg[H4, g, :], small[H4, g:g + 1], None, ALU.add)
                ci, cf, mu, em = (rowg[H4, x, :] for x in range(4))
                t = log_sigmoid(cf, cf, mu, [tk["g", 1]])
                t = ve("scan", [t], cf, C("ones")[H4, 0:T], cf, 0.0, ALU.mult, ALU.add)
                t = ve("tt", [t, tk["g", 0]], ci, ci, cf, ALU.subtract)
                t = ve("scan", [t], mu, C("ones")[H4, 0:T], ci, 0.0, ALU.mult, ALU.max)
                t = ve("tt", [t], em, cf, mu, ALU.add)
                tk["em"] = ac([t], em, em, ACT.Exp, scale=-1.0)
                tk["mu"] = ve("ts", [t], mu, mu, -1.0, None, ALU.mult)
                yield
                prev = [None, None]
                for i in range(16):
                    z = i % 2
                    b, t = project(take(columns(w_in, i * MH, MH)), x, T, M=MH)
                    t = taken[b] = ve("tt", [t, tz[z], prev[z]], xb[z][R, 3:3 + T], bank[b][R, 0:T], rst[R, N_META:T1], ALU.mult)
                    tap = lambda j: gain3[:, 8 + 16 * j + i:9 + 16 * j + i]
                    y = qk[R, i, :]
                    t = ac([t], y, xb[z][R, 0:T], ACT.Copy, scale=tap(0))
                    for j in range(1, 4):
                        t = ve("stt", [t], y, xb[z][R, j:j + T], tap(j), y, ALU.mult, ALU.add)
                    prev[z] = t
                    tk["qk", i] = ac([t], y, y, ACT.Silu)
                    yield
                def value(s):
                    def done(t):
                        if s == 5:
                            tk["v"] = t
                    return (lambda: project(take(columns(w_in, 2 * ML_W + s * P)), x, T), rst[:, N_META:T1],
                            [v[:, i, s * P:s * P + P] for i in range(2)], done)
                yield from turned_steps([value(s) for s in range(6)], (xb[0][:, 0:T], xb[1][:, 0:T]), TOK_TILES2, 7)
                for i in range(8):
                    b, t = project(take(columns(w_in, 3 * ML_W + i * MH, MH)), x, T, M=MH)
                    t = taken[b] = ve("tt", [t], og[R, i, :], bank[b][R, 0:T], rst[R, N_META:T1], ALU.mult)
                    t = ac([t], og[R, i, :], og[R, i, :], ACT.Exp, scale=-1.0)
                    t = ve("ts", [t], og[R, i, :], og[R, i, :], 1.0, None, ALU.add)
                    tk["o", i] = ve("recip", [t], og[R, i, :], og[R, i, :])
                    yield
                z2 = (xb[0][:, 0:T], xb[1][:, 0:T])
                mk = lambda c: (lambda: project(take(columns(w_in, 4 * ML_W + 2 * ML_HEADS + c * P)), x, T))
                yield from headnorm_steps([(mk(c), gain2[:, 72:73], qmem[:, c, :]) for c in range(2)], z2)
                yield from memory_kv(0, memp, kmem, vmem, z2)

            def cells():
                for _ in range(17):
                    yield
                PE.wait(tk["mu"], taken[6])
                for i, (c0, n) in enumerate(TOK_TILES2):
                    m = nc.tensor.transpose(bank[6][:, 4 * i:4 * i + 4], rowg[H4, 0, c0:c0 + n], ident[0:4, 0:4])
                t = PE.tick(m)
                tcs = taken[6] = ve("copy", [t], small[:, 16:24], bank[6][:, 0:8])
                wt_free = [None, None]
                for h in range(ML_HEADS):
                    z = h % 2
                    sel = C("sel")[H4, h * P:h * P + P]
                    PE.wait(tk["em"], tk["mu"], taken[2])
                    t = PE.tick(mm(bank[2][:, 0:T], sel, rowg[H4, 2, :], True, True))
                    PE.wait(taken[3], tk["qk", 2 * h + 1], tk["qk", 8 + 2 * h + 1])
                    kq = [bank[3][:, 0:T], bank[3][:, T:T + P]]
                    for s, (s0, n) in enumerate(TOK_TILES2):
                        for c in range(2):
                            m = mm(kq[s], qk[R, 8 + 2 * h + c, s0:s0 + n], qk[R, 2 * h + c, s0:T], c == 0, c == 1)
                    tp = PE.tick(m)
                    w0, w1 = (WT[z][s][:, s0:T] for s, (s0, n) in enumerate(TOK_TILES2))
                    te = []
                    for s, (s0, n) in enumerate(TOK_TILES2):
                        w = (w0, w1)[s]
                        t1 = taken[2] = ve("stt", [t, tcs, wt_free[z]], w, bank[2][:, s0:T], small[:, 16 + 4 * s + h:17 + 4 * s + h],
                                           C("causalT")[:, 0:T - s0], ALU.add, ALU.min)
                        te.append(ac([t1], w, w, ACT.Exp))
                    for s in range(2):
                        w = (w0, w1)[s]
                        tw = ve("stt", [te[s], tp], w, w, ML_DK ** -0.5, kq[s], ALU.mult, ALU.mult)
                    taken[3] = tw
                    yield
                    while "v" not in tk:
                        yield
                    PE.wait(tw)
                    PE.wait(tk["v"], taken[4], taken[5], taken[7])
                    def sums(o, lhs):
                        mm(o[R, 0:T], lhs(0), WT[z][0][:, 0:T], True, False)
                        return mm(o[R, P:T], lhs(1), WT[z][1][:, P:T], False, True)
                    sums(bank[4], lambda s: v[:, s, h * ML_DK:h * ML_DK + MH])
                    sums(bank[5], lambda s: v[:, s, h * ML_DK + MH:h * ML_DK + ML_DK])
                    m = sums(bank[7], lambda s: C("ones")[:, 0:MH])
                    tn = PE.tick(m)
                    wt_free[z] = tn
                    PE.wait(taken[6])
                    t = PE.tick(mm(bank[6][R, 0:T], sel[:, 0:MH], rowg[H4, 3, :], True, True))
                    den = tmp[R, 2, :]
                    t = taken[6] = ac([t, VE.now()], den, bank[6][R, 0:T], ACT.Copy)
                    t = taken[7] = ac([tn], tmp[R, 0, :], bank[7][R, 0:T], ACT.Abs)
                    t = ve("tt", [t], den, den, tmp[R, 0, :], ALU.max)
                    t = ve("recip", [t], den, den)
                    cell = [sg[R, 0, 0:T], sg[R, 1, 0:T]]
                    taken[4] = ve("tt", [t, c_free[0]], cell[0], bank[4][R, 0:T], den, ALU.mult)
                    taken[5] = tc = ve("tt", [t], cell[1], bank[5][R, 0:T], den, ALU.mult)
                    yield
                    sq = [WT[z][0][R, 0:T], WT[z][1][R, 0:T]]
                    for c in range(2):
                        t = ac([tc, tn], sq[c], cell[c], ACT.Square)
                        PE.wait(t, taken[6])
                        m = mm(bank[6][R, 0:T], C("mean192")[R, 0:MH], sq[c], c == 0, c == 1)
                    wt_free[z] = t = PE.tick(m)
                    t = taken[6] = rsqrt(den, bank[6][R, 0:T], [t])
                    for c in range(2):
                        i = 2 * h + c
                        while ("o", i) not in tk:
                            yield
                        t1 = ve("stt", [t, tc], cell[c], cell[c], gain3[:, i:i + 1], den, ALU.mult, ALU.mult)
                        t1 = ve("tt", [t1, tk["o", i]], og[R, i, :], og[R, i, :], cell[c], ALU.mult)
                        to_pair(([cellp[0][R, i, :]], [cellp[1][R, i, :]]), 0, og[R, i, :], [t1])
                        c_free[0] = VE.now()
                    yield

            c_free = [None]
            drive(main(), [cells()])
            hmt = {}
            bufs = ([WT[0][0], WT[0][1]], [WT[1][0], WT[1][1]], [xb[0][:, 0:T], xb[1][:, 0:T]], small[:, 8:16])
            join()
            for _ in attention(memory_units(qmem, kmem, vmem, hm, hmt), bufs, (2, 3), (4, 5)):
                pass
            w_out = IN["a_w_out_2"][0]
            PE.wait(AC.now(), VE.now())
            for s in range(4):
                UM = take(w_out[ML_W:D, s * 256:s * 256 + 256].rearrange("(k p) n -> p k n", p=P))
                bs = [next_bank(), next_bank()]
                for c in range(2):
                    m = products(bank[bs[c]][:, 0:T], UM, lambda k, part: UM["w"][part][:, k, c * P:c * P + P],
                                 lambda k, part: hm[part][:, k, :], n_k=2, stop=False)
                ring.release(m)
                for c in range(2):
                    d = 2 * s + c
                    U = take(w_out[0:ML_W, d * P:d * P + P].rearrange("(k p) n -> p k n", p=MH), rows=MH)
                    m = products(bank[bs[c]][:, 0:T], U, lambda k, part: U["w"][part][:, k, :],
                                 lambda k, part: cellp[part][R, k, :], start=False)
                    free_bank_add(d, bs[c], ring.release(m))
            lay.close()

        def shared_kv():
            w_kv = IN["w_kv_2"]
            x = xin(cols2)
            lay = Scope()
            zb = (lay.take(T), lay.take(T))
            make = first_of(lambda c: take(columns(w_kv, c * P)), x)
            for i, _ in enumerate(headnorm_steps([(make(c), gain2[:, 77:78], k_sh[:, c, :]) for c in range(6)], zb)):
                pass
            val = lambda s: (lambda: project(take(columns(w_kv, DIL_W + s * P)), x, T), rst[:, N_META:T1],
                             [v_sh[:, i, s * P:s * P + P] for i in range(2)], lambda t: None)
            for _ in turned_steps([val(s) for s in range(6)], zb, TOK_TILES2, 7):
                pass
            lay.close()

        def first_of(unit, x):
            def make(c):
                def go():
                    if c == 0:
                        U = unit(0)
                        tq = squares(hT, h_tok, cols2, range(KD), ve)
                        r = project(U, x, T, toks=xt)
                        stats(tq, cols2, 7)
                        taken[7] = VE.now()
                        return r
                    return project(unit(c), x, T)
                return go
            return make

        bias_rows = IN["scratch"]

        def mixer2b():
            lay = Scope()
            q = lay.take(8, T)
            bias = lay.take(12, T)
            hd = lay.pair(6, T)
            hm = lay.pair(2, T)
            kmem = lay.take(2, T)
            vmem = lay.take(2, 256)
            memp = lay.pair(KD, T)
            SS = [lay.take(3 * T), lay.take(3 * T)]
            PP = [lay.take(3 * T), lay.take(3 * T)]
            PT = [lay.take(3 * T), lay.take(3 * T)]
            ohb = lay.take(1536)
            ohv = ohb[0:BUCKETS + 1, :]
            x = xin(cols2)
            tab = small[0:BUCKETS + 1, 32:44]
            t = po("memset", [], small[:, 32:44], NEG)
            par_load(small[0:BUCKETS, 32:44], IN["rel_bias_2"], [t])
            par_load(ohv, IN["onehot"])
            PE.wait(par_all())
            tabb = [rst2[0:BUCKETS + 1, 0:P], rst2[0:BUCKETS + 1, P:2 * P]]
            VE.wait(par_all())
            row = lambda h, toks: ve("ts", toks, tabb[h % 2], C("ones")[0:BUCKETS + 1, 0:P], small[0:BUCKETS + 1, 32 + h:33 + h],
                                     None, ALU.mult)
            tt = row(0, [])
            for h in range(12):
                g = h // 4
                b = next_bank()
                last, tt = tt, row(h + 1, [PE.now()]) if h < 11 else None
                PE.wait(last)
                t = PE.tick(mm(bank[b][:, :], tabb[h % 2], ohv[:, 512 * g:512 * g + 512], True, True))
                st = bias[:, 2 * (h % 6):2 * (h % 6) + 2, :].rearrange("p a b -> p (a b)")
                if h >= 6:
                    AC.wait((s_bias, 0, 16 * 6))
                taken[b] = ac([t], st, bank[b][:, :], ACT.Copy)
                nc.scalar.wait_ge(AC.sem, AC.n)
                nc.scalar.dma_start(bias_rows[h], st).then_inc(s_bias, 16)
            PO.wait((s_bias, 0, 16 * 12))
            for h in range(12):
                src = bias_rows[h].rearrange("p u -> (p u)")[0:P * 511].rearrange("(p u) -> p u", u=511)[:, 127:127 + T]
                par_load(bias[:, h, :], src)
            tk_bias = par_all()

            order = [0, 2, 4, 1, 3, 5, 6, 7]
            make = first_of(lambda c: take(columns(IN["b_w_q_2"][0], order[c] * P)), x)
            zb = (ohb[:, 0:T], ohb[:, T:2 * T])
            VE.wait(PE.now())
            q_done = {}

            def main():
                items = [(make(i), gain2[:, 76:77] if c < 6 else gain2[:, 73:74], q[:, c, :]) for i, c in enumerate(order)]
                for n, _ in enumerate(headnorm_steps(items, zb)):
                    if n in (3, 6):
                        q_done[n // 3 - 1] = VE.now()
                    yield
                yield from memory_kv(1, memp, kmem, vmem, zb)

            def dilated():
                units = [(h, i) for h in range(DIL_HEADS) for i in range(2)]
                p_free, pt_free, ready = [None, None], [None, None], {}
                outs = ((6, 0), (6, T), (5, 0))
                for x in range(len(units) + 2):
                    if x < len(units):
                        h, i = units[x]
                        pair, rows = h // 2, slice(64 * (h % 2), 64 * (h % 2) + 64)
                        while pair not in q_done:
                            yield
                        z = x % 2
                        t0, n = TOK_TILES2[i]
                        W = t0 + n
                        sc = [bank[2][:, 0:W], bank[2][:, T:T + W], bank[3][:, 0:W]]
                        PE.wait(q_done[pair], taken[2], taken[3])
                        for g in range(3):
                            m = mm(sc[g], q[rows, 2 * g + pair, t0:t0 + n], k_sh[rows, 2 * g + pair, 0:W], True, True)
                        t = PE.tick(m)
                        VE.wait(tk_bias, p_free[z])
                        for g in range(3):
                            tt = ve("tt", [t], SS[z][:, g * W:g * W + W], sc[g], bias[:, 4 * g + h, T - W:T], ALU.add)
                        taken[2] = taken[3] = tt
                        mx, nm, den, rd = (small[:, 8 + 4 * z + y:9 + 4 * z + y] for y in range(4))
                        t = ve("rmax", [tt], mx, SS[z][:, 0:3 * W], AX_X)
                        t = ve("ts", [t], nm, mx, -1.0, None, ALU.mult)
                        t = ac([t, p_free[z]], PP[z][:, 0:3 * W], SS[z][:, 0:3 * W], ACT.Exp, bias=nm, accum_out=den)
                        t = ve("recip", [t], rd, den)
                        ready[x] = ve("ts", [t], PP[z][:, 0:3 * W], PP[z][:, 0:3 * W], rd, None, ALU.mult)
                    if 0 <= x - 1 < len(units):
                        z = (x - 1) % 2
                        nt = 3 * (units[x - 1][1] + 1)
                        PE.wait(ready[x - 1], taken[4], taken[3])
                        for c in range(nt):
                            o = bank[4][:, c * P:c * P + P] if c < 4 else bank[3][:, T + (c - 4) * P:T + (c - 3) * P]
                            m = nc.tensor.transpose(o, PP[z][:, c * P:c * P + P], ident)
                        t = p_free[z] = PE.tick(m)
                        first = min(nt, 4) * P
                        taken[4] = tc = ac([t, pt_free[z]], PT[z][:, 0:first], bank[4][:, 0:first], ACT.Copy)
                        if nt > 4:
                            taken[3] = tc = ac([], PT[z][:, 4 * P:nt * P], bank[3][:, T:T + (nt - 4) * P], ACT.Copy)
                        ready[x - 1] = tc
                    if 0 <= x - 2 < len(units):
                        h, i = units[x - 2]
                        pair, rows = h // 2, slice(64 * (h % 2), 64 * (h % 2) + 64)
                        z, ns, t0 = (x - 2) % 2, i + 1, TOK_TILES2[i][0]
                        PE.wait(ready[x - 2], taken[5], taken[6])
                        for g, (b, c) in enumerate(outs):
                            for k in range(ns):
                                m = mm(bank[b][rows, c + t0:c + t0 + P], v_sh[:, k, (4 * g + h) * HD:(4 * g + h) * HD + HD],
                                       PT[z][:, (g * ns + k) * P:(g * ns + k) * P + P], k == 0, k == ns - 1)
                        t = pt_free[z] = PE.tick(m)
                        if h % 2 == 1 and i == 1:
                            for g, (b, c) in enumerate(outs):
                                taken[b] = to_pair(([hd[0][:, 2 * g + pair, :]], [hd[1][:, 2 * g + pair, :]]), 0,
                                                   bank[b][:, c:c + T], [t, taken[b]])[1]
                    yield

            drive(main(), [dilated()])
            join()
            for b in range(8):
                taken[b] = None
            hmt = {}
            bufs = ([SS[0], SS[1]], [PP[0][:, 0:T], PP[0][:, T:2 * T]], PT, small[:, 8:16])
            for _ in attention(memory_units(q[:, 6:8, :], kmem, vmem, hm, hmt), bufs, (2, 3), (4, 5)):
                pass
            PE.wait(AC.now(), VE.now())
            for d in range(KD):
                b, t = project(take(columns(IN["b_w_out_2"][0], d * P)),
                               lambda k, part: hd[part][:, k, :] if k < 6 else hm[part][:, k - 6, :], T)
                free_bank_add(d, b, t)
            lay.close()

        def then(i):
            return lambda: norm_in(gcol2(i), cols2)

        then(0)()
        ffn2("ffn1", 0, then(4))
        join(but=PE)
        mixer2a()
        then(2)()
        join(but=PE)
        ffn2("ffn2", 0, then(8))
        join(but=PE)
        shared_kv()
        then(1)()
        join(but=PE)
        ffn2("ffn1", 1, then(5))
        join(but=PE)
        mixer2b()
        then(3)()
        join(but=PE)
        ffn2("ffn2", 1, lambda: None)

        join()
        lay = Scope()
        obuf = lay.take(2, D)
        for i in range(2):
            ov = obuf[:, i, :]
            for k in range(KD):
                b = k % 4
                PE.wait(h_tok[k], taken[b] if i or k >= 4 else None)
                t = PE.tick(nc.tensor.transpose(bank[b][:, 0:P], hT[:, k, N_META + i * P:N_META + i * P + P], ident))
                taken[b] = ve("copy", [t], ov[:, k * P:k * P + P], bank[b][:, 0:P])
            nc.sync.wait_ge(VE.sem, VE.n)
            nc.sync.dma_start(out[0, i * P:i * P + P, :], ov).then_inc(s_out, 16)
        nc.sync.wait_ge(s_out, 32)
        assert ring.loads == ring.splits == UNITS
        lay.close()
        keep.close()


_SHAPE = (1, SEQ, D)


def kernel(**inputs):
    import numpy as _np
    import concourse.bacc as _bacc
    from concourse import mybir as _mybir
    from concourse.bass_utils import run_bass_kernel_spmd as _run

    nc = _bacc.Bacc("TRN2", target_bir_lowering=False, num_devices=1)
    arrays, args = {}, {}
    given = dict(inputs)
    given["consts"] = constants()
    given["onehot"] = bucket_rows()
    for name, value in given.items():
        a = _np.ascontiguousarray(value)
        arrays[f"in_{name}"] = a
        args[name] = nc.dram_tensor(f"in_{name}", a.shape, _mybir.dt.from_np(a.dtype), kind="ExternalInput").ap()
    args["scratch"] = nc.dram_tensor("bias_scratch", (12, P, 512), F32).ap()
    out = nc.dram_tensor("out_0", _SHAPE, F32, kind="ExternalOutput").ap()
    program(nc, args, out)
    r = _run(nc, [arrays], core_ids=[0])
    return r.results[0]["out_0"]
```
